# Optimizing a Trainium2 kernel written in Bass

```python
import jax, jax.numpy as jnp
from jax import lax
import numpy as np

D_MODEL = 1024
BATCH = 1
SEQ = 256
DEPTH = 2

N_MIXERS = 2
N_RWKV_LAYERS = (DEPTH + 1) // 2
N_SB_LAYERS = DEPTH // 2
HEAD_DIM = 64
N_HEADS = D_MODEL // HEAD_DIM
D_DECAY_LORA = 64
D_AAA_LORA = 64
D_GATE_LORA = 128
N_TOKEN_SHIFT_MIX = 6
LNX_EPS = 64e-5
Q_BLOCK = 128
N_EXPERTS = 64
TOP_K = 8
D_EXPERT = D_MODEL // 4
D_SHARED = D_MODEL // 4
ROUTED_SCALE = 2.5
EXPERT_BLOCK = 128
RMS_EPS = 1e-6
N_ADA = 6

kernel_name = 'hybrid_rwkv7_stickbreak_moe_block'

def rmsnorm(x, g):
    xf = x.astype(jnp.float32)
    y = xf * lax.rsqrt(jnp.mean(xf * xf, axis=-1, keepdims=True) + RMS_EPS)
    return (y * g.astype(jnp.float32)).astype(x.dtype)

def _wkv7_scan(r, decay, k, v, a_vec, b_vec):
    B, S, H, N = r.shape

    def step(state, inp):
        r_t, w_t, k_t, v_t, a_t, b_t = inp
        sa = jnp.einsum('bhij,bhj->bhi', state, a_t)
        state = (state * w_t[:, :, None, :]
                 + sa[..., None] * b_t[:, :, None, :]
                 + v_t[..., None] * k_t[:, :, None, :])
        return state, jnp.einsum('bhij,bhj->bhi', state, r_t)

    xs = tuple(jnp.moveaxis(t, 1, 0) for t in (r, decay, k, v, a_vec, b_vec))
    s0 = jnp.zeros((B, H, N, N), jnp.float32)
    _, out = lax.scan(step, s0, xs)
    return jnp.moveaxis(out, 0, 1)

def rwkv7_time_mix(h, mu, w_rkv, w_w1, w_w2, w0, w_a1, w_a2, a0, w_g1, w_g2,
                   k_k, k_a, r_k, lnx_g, lnx_b, w_o):
    B, S, D = h.shape
    xx = jnp.pad(h, ((0, 0), (1, 0), (0, 0)))[:, :-1] - h
    xs = h[None] + xx[None] * mu[:, None, None, :]
    rkv = jnp.einsum('nbsd,nde->nbse', xs[:3], w_rkv)
    r, k, v = rkv[0], rkv[1], rkv[2]
    xw, xa, xg = xs[3], xs[4], xs[5]
    w_log = -jax.nn.softplus(-(w0 + jnp.tanh(xw @ w_w1) @ w_w2)) - 0.5
    decay = jnp.exp(-jnp.exp(w_log.astype(jnp.float32)))
    a = jax.nn.sigmoid((a0 + (xa @ w_a1) @ w_a2).astype(jnp.float32))
    g = jax.nn.sigmoid(xg @ w_g1) @ w_g2

    hs = lambda t: t.astype(jnp.float32).reshape(B, S, N_HEADS, HEAD_DIM)
    kk = hs(k * k_k)
    kk = kk / jnp.maximum(jnp.sqrt(jnp.sum(kk * kk, axis=-1, keepdims=True)), 1e-12)
    k_f = k.astype(jnp.float32) * (1.0 + (a - 1.0) * k_a.astype(jnp.float32))
    a_h = hs(a)
    r_h, k_h, v_h, w_h = hs(r), hs(k_f), hs(v), hs(decay)

    o = _wkv7_scan(r_h, w_h, k_h, v_h, -kk, kk * a_h)
    mean = jnp.mean(o, axis=-1, keepdims=True)
    var = jnp.mean(jnp.square(o - mean), axis=-1, keepdims=True)
    o = ((o - mean) * lax.rsqrt(var + LNX_EPS)).reshape(B, S, D)
    o = o * lnx_g.astype(jnp.float32) + lnx_b.astype(jnp.float32)
    bonus = jnp.sum(r_h * k_h * r_k.astype(jnp.float32), axis=-1, keepdims=True) * v_h
    o = o + bonus.reshape(B, S, D)
    return (o.astype(h.dtype) * g) @ w_o

def stick_breaking_attention(h, w_qkv, w_o):
    B, S, D = h.shape
    qkv = (h @ w_qkv).reshape(B, S, 3, N_HEADS, HEAD_DIM)
    q = jnp.transpose(qkv[:, :, 0], (0, 2, 1, 3))
    k = jnp.transpose(qkv[:, :, 1], (0, 2, 1, 3))
    v = jnp.transpose(qkv[:, :, 2], (0, 2, 1, 3))
    n_blk = S // Q_BLOCK
    q_blocks = jnp.moveaxis(q.reshape(B, N_HEADS, n_blk, Q_BLOCK, HEAD_DIM), 2, 0)
    key_pos = jnp.arange(S)
    scale = 1.0 / float(np.sqrt(HEAD_DIM))

    def query_block(args):
        q_i, blk = args
        z = jnp.einsum('bhqd,bhkd->bhqk', q_i, k).astype(jnp.float32) * scale
        q_pos = blk * Q_BLOCK + jnp.arange(Q_BLOCK)
        causal = key_pos[None, :] < q_pos[:, None]
        log_beta = jax.nn.log_sigmoid(z)
        log_1m_beta = jnp.where(causal, jax.nn.log_sigmoid(-z), 0.0)
        tail = lax.cumsum(log_1m_beta, axis=3, reverse=True) - log_1m_beta
        weights = jnp.where(causal, jnp.exp(log_beta + tail), 0.0)
        return jnp.einsum('bhqk,bhkd->bhqd', weights.astype(v.dtype), v)

    o = lax.map(query_block, (q_blocks, jnp.arange(n_blk)))
    o = jnp.transpose(o, (1, 0, 3, 2, 4)).reshape(B, S, D)
    return o @ w_o

def moe_ffn(h, w_router, router_bias, w_gate, w_up, w_down, ws_gate, ws_up, ws_down):
    B, S, D = h.shape
    T = B * S
    xf = h.reshape(T, D)
    scores = jax.nn.sigmoid((xf @ w_router).astype(jnp.float32))
    _, idx = lax.top_k(scores + router_bias.astype(jnp.float32), TOP_K)
    sel = jnp.take_along_axis(scores, idx, axis=1)
    gates = ROUTED_SCALE * sel / jnp.sum(sel, axis=1, keepdims=True)

    A = T * TOP_K
    e_flat = idx.reshape(A).astype(jnp.int32)
    tok_flat = jnp.arange(A, dtype=jnp.int32) // TOP_K
    w_flat = gates.reshape(A)
    order = jnp.argsort(e_flat)
    e_s, tok_s, w_s = e_flat[order], tok_flat[order], w_flat[order]
    counts = jnp.bincount(e_flat, length=N_EXPERTS).astype(jnp.int32)
    padded = ((counts + EXPERT_BLOCK - 1) // EXPERT_BLOCK) * EXPERT_BLOCK
    start = jnp.cumsum(counts) - counts
    pend = jnp.cumsum(padded)
    pstart = pend - padded
    dest = pstart[e_s] + jnp.arange(A, dtype=jnp.int32) - start[e_s]
    n_blocks = (A + N_EXPERTS * (EXPERT_BLOCK - 1) + EXPERT_BLOCK - 1) // EXPERT_BLOCK
    P = n_blocks * EXPERT_BLOCK
    buf_tok = jnp.zeros((P,), jnp.int32).at[dest].set(tok_s)
    buf_w = jnp.zeros((P,), jnp.float32).at[dest].set(w_s)
    blk_start = jnp.arange(n_blocks, dtype=jnp.int32) * EXPERT_BLOCK
    blk_expert = jnp.minimum(jnp.searchsorted(pend, blk_start, side='right'), N_EXPERTS - 1)

    def expert_block(args):
        toks, wts, e = args
        xb = xf[toks]
        hb = jax.nn.silu(xb @ w_gate[e]) * (xb @ w_up[e])
        return (hb @ w_down[e]) * wts[:, None].astype(xb.dtype)

    yb = lax.map(expert_block, (buf_tok.reshape(n_blocks, EXPERT_BLOCK),
                                buf_w.reshape(n_blocks, EXPERT_BLOCK), blk_expert))
    routed = jnp.zeros_like(xf).at[buf_tok].add(yb.reshape(P, D))
    shared = (jax.nn.silu(xf @ ws_gate) * (xf @ ws_up)) @ ws_down
    return (routed + shared).reshape(B, S, D)

def setup_inputs(seed: int = 0) -> dict:
    key = jax.random.key(seed)
    ks = iter(jax.random.split(key, 48))
    nrm = lambda shape, s: jax.random.normal(next(ks), shape, jnp.float32) * s
    D, NR, NS, L = D_MODEL, N_RWKV_LAYERS, N_SB_LAYERS, DEPTH
    E, F, FS = N_EXPERTS, D_EXPERT, D_SHARED
    inv = lambda n: float(n) ** -0.5
    return {
        'x': nrm((BATCH, SEQ, D), 1.0),
        'c': nrm((BATCH, D), 1.0),
        'ada_w': nrm((L, D, N_ADA * D), 0.5 * inv(D)),
        'ada_b': nrm((L, N_ADA * D), 0.02),
        'norm_pre_mix': 1.0 + nrm((L, D), 0.05),
        'norm_post_mix': 1.0 + nrm((L, D), 0.05),
        'norm_pre_ffn': 1.0 + nrm((L, D), 0.05),
        'norm_post_ffn': 1.0 + nrm((L, D), 0.05),
        'rwkv_mu': jax.random.uniform(next(ks), (NR, N_TOKEN_SHIFT_MIX, D), jnp.float32),
        'rwkv_w_rkv': nrm((NR, 3, D, D), inv(D)),
        'rwkv_w_w1': nrm((NR, D, D_DECAY_LORA), inv(D)),
        'rwkv_w_w2': nrm((NR, D_DECAY_LORA, D), 0.5 * inv(D_DECAY_LORA)),
        'rwkv_w0': jax.random.uniform(next(ks), (NR, D), jnp.float32, -6.0, -1.0),
        'rwkv_w_a1': nrm((NR, D, D_AAA_LORA), inv(D)),
        'rwkv_w_a2': nrm((NR, D_AAA_LORA, D), 0.5 * inv(D_AAA_LORA)),
        'rwkv_a0': nrm((NR, D), 0.1),
        'rwkv_w_g1': nrm((NR, D, D_GATE_LORA), inv(D)),
        'rwkv_w_g2': nrm((NR, D_GATE_LORA, D), inv(D_GATE_LORA)),
        'rwkv_k_k': 0.85 + nrm((NR, D), 0.05),
        'rwkv_k_a': 1.0 + nrm((NR, D), 0.05),
        'rwkv_r_k': nrm((NR, N_HEADS, HEAD_DIM), 0.1),
        'rwkv_lnx_g': 1.0 + nrm((NR, D), 0.05),
        'rwkv_lnx_b': nrm((NR, D), 0.01),
        'rwkv_w_o': nrm((NR, D, D), inv(D)),
        'sb_w_qkv': nrm((NS, D, 3 * D), inv(D)),
        'sb_w_o': nrm((NS, D, D), inv(D)),
        'moe_w_router': nrm((L, D, E), inv(D)),
        'moe_router_bias': nrm((L, E), 0.01),
        'moe_w_gate': nrm((L, E, D, F), inv(D)),
        'moe_w_up': nrm((L, E, D, F), inv(D)),
        'moe_w_down': nrm((L, E, F, D), inv(F)),
        'moe_ws_gate': nrm((L, D, FS), inv(D)),
        'moe_ws_up': nrm((L, D, FS), inv(D)),
        'moe_ws_down': nrm((L, FS, D), inv(FS)),
    }

def reference(x, c, ada_w, ada_b, norm_pre_mix, norm_post_mix, norm_pre_ffn, norm_post_ffn,
              rwkv_mu, rwkv_w_rkv, rwkv_w_w1, rwkv_w_w2, rwkv_w0, rwkv_w_a1, rwkv_w_a2, rwkv_a0,
              rwkv_w_g1, rwkv_w_g2, rwkv_k_k, rwkv_k_a, rwkv_r_k, rwkv_lnx_g, rwkv_lnx_b, rwkv_w_o,
              sb_w_qkv, sb_w_o,
              moe_w_router, moe_router_bias, moe_w_gate, moe_w_up, moe_w_down,
              moe_ws_gate, moe_ws_up, moe_ws_down):
    mod_all = jnp.einsum('bd,lde->lbe', jax.nn.silu(c), ada_w) + ada_b[:, None, :]
    for layer in range(DEPTH):
        shift_m, scale_m, gate_m, shift_f, scale_f, gate_f = jnp.split(
            mod_all[layer][:, None, :], N_ADA, axis=-1)
        h = rmsnorm(x, norm_pre_mix[layer]) * (1.0 + scale_m) + shift_m
        i = layer // N_MIXERS
        if layer % N_MIXERS == 0:
            y = rwkv7_time_mix(h, rwkv_mu[i], rwkv_w_rkv[i], rwkv_w_w1[i], rwkv_w_w2[i], rwkv_w0[i],
                               rwkv_w_a1[i], rwkv_w_a2[i], rwkv_a0[i], rwkv_w_g1[i], rwkv_w_g2[i],
                               rwkv_k_k[i], rwkv_k_a[i], rwkv_r_k[i], rwkv_lnx_g[i], rwkv_lnx_b[i],
                               rwkv_w_o[i])
        else:
            y = stick_breaking_attention(h, sb_w_qkv[i], sb_w_o[i])
        x = x + gate_m * rmsnorm(y, norm_post_mix[layer])
        h = rmsnorm(x, norm_pre_ffn[layer]) * (1.0 + scale_f) + shift_f
        y = moe_ffn(h, moe_w_router[layer], moe_router_bias[layer], moe_w_gate[layer],
                    moe_w_up[layer], moe_w_down[layer], moe_ws_gate[layer], moe_ws_up[layer],
                    moe_ws_down[layer])
        x = x + gate_f * rmsnorm(y, norm_post_ffn[layer])
    return x


_drawn_inputs = setup_inputs


def setup_inputs(seed=0):
    import zlib

    import numpy as np

    out = dict(_drawn_inputs(seed))
    spreads = {}
    factors = {'rwkv_lnx_b': 2.943}
    for name, (base, spread) in spreads.items():
        noise = np.random.default_rng([zlib.crc32(name.encode()), seed]).standard_normal(out[name].shape)
        drawn = base * np.exp(spread * noise) if base else spread * noise
        out[name] = __import__('jax').numpy.asarray(drawn.astype(out[name].dtype))
    for name, factor in factors.items():
        out[name] = (out[name] * factor).astype(out[name].dtype)
    return out
```

```python
from contextlib import ExitStack
import math

import concourse.bass as bass
from concourse import mybir

F32 = mybir.dt.float32
ALU = mybir.AluOpType
ACT = mybir.ActivationFunctionType
AX = mybir.AxisListType

P = 128
STOP = 4


def hybrid_trunk(nc, a, out):
    _, S, D = a["x"].shape
    TT = S // P
    KC = D // P
    HD = a["rwkv_r_k"].shape[2]
    H = D // HD
    FC = D // P
    E = a["moe_w_gate"].shape[1]
    F = a["moe_w_gate"].shape[3]
    FK = F // P
    LW, LA, LG = a["rwkv_w_w1"].shape[2], a["rwkv_w_a1"].shape[2], a["rwkv_w_g1"].shape[2]
    NB = 512
    HB = D // NB
    TOPK = 8
    ROUTED_SCALE = 2.5
    RMS_EPS, LNX_EPS = 1e-6, 64e-5
    DECAY = math.exp(-0.5)
    NADA = a["ada_w"].shape[2] // NB
    assert TT == 2 and KC == 8 and HD == 64 and F == 256 and NADA == 12

    with ExitStack() as ctx:
        def sb(name, shape):
            return ctx.enter_context(nc.sbuf_tensor(name, shape, F32))

        def sem(name):
            return ctx.enter_context(nc.semaphore(name))

        PS = ctx.enter_context(nc.psum_tensor("PS", [P, 8, NB], F32))

        x = sb("x", [P, TT, D])
        mt = sb("mt", [P, 5, D])
        h = sb("h", [P, TT, D])
        hT = sb("hT", [P, KC, S + 1])
        ident = sb("ident", [P, P])
        upto = sb("upto", [P, 2, P])
        cumx = sb("cumx", [P, 2, P])
        fromj = sb("fromj", [P, P])
        ones = sb("ones", [P, P])
        halves = sb("halves", [P, 2])
        sel = sb("sel", [P, 1])
        ccol = sb("ccol", [P, KC])
        crep = sb("crep", [P, KC, 32])
        adab, apart, arow = mt[0:2 * NADA, 4, 0:NB], mt[:, 4, NB:2 * NB], mt[0:1, 3, :].rearrange("p (b c) -> p b c", b=2)
        mu = sb("mu", [P, 6, KC])
        ss = sb("ss", [P, 8, TT])
        ms = sb("ms", [P, 8, TT])
        rstd = sb("rstd", [P, 8, TT])
        hs = sb("hs", [P, 4, TT * H])
        bonus = sb("bonus", [P, TT * H])
        edec = sb("edec", [P, FC])
        rb = sb("rb", [P, 2, E])
        top8 = sb("top8", [P, TT, TOPK])
        rsum = sb("rsum", [P, 2, TT])
        AK = 156
        arena = sb("arena", [P, AK * 256])

        def at(kib, *dims):
            n = 1
            for d in dims:
                n *= d
            v = arena[:, int(kib * 256):int(kib * 256) + n]
            names = "abcd"[:len(dims)]
            if len(dims) == 1:
                return v
            return v.rearrange(f"p ({' '.join(names)}) -> p {' '.join(names)}", **dict(zip(names, dims)))

        def slot(s, *dims):
            return at(24 * s, *dims)

        xs = [at(16, KC, S), at(40, KC, S)]
        xx = at(64, KC, S)
        w1w, w1a, w1g = at(72, KC, LW), at(74, KC, LA), at(76, KC, LG)
        w2w, w2a, w2g = at(80, D), at(84, D), at(88, D)
        t1 = at(92, 3, S)
        r_, k_, v_, g_, a_, sig = (at(96 + 8 * i, TT, D) for i in range(6))
        kkrow, karow, rkrow = at(144, D), at(148, D), at(152, D)
        ART = at(48, FC, TT, 2, P)
        bT, kT = at(64, FC, S), at(72, FC, S)
        tmpX, tmpY = at(80, TT, D), at(88, TT, D)
        ARB = at(80, TT * H, P)
        AAB = at(136, TT * H, P)
        AAB_end = 152
        TB = at(18, TT * H, 32)
        U = at(42, 2, NB)
        S0T = at(46, FC, HD)
        acc = at(152, 2, NB)
        DT = h[:, 0, :].rearrange("p (s t) -> p s t", s=32)
        TTi = h[:, 1, :].rearrange("p (s t) -> p s t", s=32)
        SK = [mt[:, 2 - i, :].rearrange("p (f q c) -> p f q c", f=2, q=2) for i in range(2)]
        o_ = r_
        lnsq = at(48, TT, D)
        qkv = at(96, TT, 3 * D)
        qkT = at(120, 2 * FC, S)
        zsb = [at(136, 4, 384), at(142, 4, 384)]
        spb = [at(148, 4, 384), mt[:, 0:2, :].rearrange("p a b -> p (a b)")[:, 0:1536].rearrange("p (a b) -> p a b", a=4)]
        gsil = at(96, TT, F)
        actp = at(98, TT, FK, P)
        actT = at(100, TT, FK, P)
        rt = at(102, 6, TT, E)
        rw = at(105, KC, E)
        zmask = sb("zmask", [P, 384])

        mod_dram = nc.dram_tensor("mod_rows", [2 * NADA, NB], F32, kind="Internal").ap()
        diag_dram = nc.dram_tensor("diag_blocks", [4, 32, TT * H, 32], F32, kind="Internal").ap()
        inv_dram = nc.dram_tensor("inverse_blocks", [4, TT * H, 32, 32], F32, kind="Internal").ap()

        ring_in = [sem(f"ring_in{i}") for i in range(4)]
        x_in = sem("x_in"); router_in = sem("router_in"); small_in = sem("small_in"); lora_in = sem("lora_in"); rows_in = sem("rows_in")
        mpre_in = sem("mpre_in"); mpost_in = sem("mpost_in"); lnx_in = sem("lnx_in")
        const_ok = sem("const_ok"); pool_step = sem("pool_step"); crep_ok = sem("crep_ok"); triA_ok = sem("triA_ok")
        ada_mm = sem("ada_mm"); ada_part = sem("ada_part"); ada_row_mm = sem("ada_row_mm"); ada_row = sem("ada_row")
        mod_stored = [sem("mod_stored0"), sem("mod_stored1")]
        ss_ready = sem("ss_ready"); ms_ready = sem("ms_ready"); rstd_ready = sem("rstd_ready")
        h_ready = sem("h_ready"); x_ready = sem("x_ready")
        tr_mm = sem("tr_mm"); tr_act = sem("tr_act"); tr_dve = sem("tr_dve")
        xs_ready = sem("xs_ready"); lora1_mm = sem("lora1_mm"); lora1_ok = sem("lora1_ok")
        lora2_mm = sem("lora2_mm"); lora2_ok = sem("lora2_ok")
        proj_mm = sem("proj_mm"); proj_ok = sem("proj_ok")
        cum_mm = sem("cum_mm"); decay_ok = sem("decay_ok"); kss_ready = sem("kss_ready"); knorm_ok = sem("knorm_ok")
        xy_free = sem("xy_free"); tok_ready = sem("tok_ready")
        sb_mm = sem("sb_mm"); sb_ok = sem("sb_ok"); sk_mm = sem("sk_mm"); sk_ok = sem("sk_ok"); xo_mm = sem("xo_mm")
        diag_out = sem("diag_out"); diag_in = sem("diag_in"); ti_init = sem("ti_init"); inv_ok = sem("inv_ok"); inv_out = sem("inv_out"); inv_in = sem("inv_in")
        xacc_mm = sem("xacc_mm"); acc_act = sem("acc_act"); acc_dve = sem("acc_dve"); ub_mm = sem("ub_mm"); u_act = sem("u_act"); u_dve = sem("u_dve")
        o_mm = sem("o_mm"); o_ok = sem("o_ok"); st_mm = sem("st_mm"); s0_ok = sem("s0_ok")
        lvar_ready = sem("lvar_ready"); lstd_ok = sem("lstd_ok")
        ccol_ok = sem("ccol_ok"); o_taken = sem("o_taken"); z_mm = sem("z_mm"); z_ok = sem("z_ok"); l_ok = sem("l_ok"); sp_ok = sem("sp_ok"); rc_mm = sem("rc_mm"); ez_ok = sem("ez_ok"); w_ok = sem("w_ok"); pv_mm = sem("pv_mm")
        log_mm = sem("log_mm"); sc_ok = sem("sc_ok"); gates_ok = sem("gates_ok")
        gu_mm = sem("gu_mm"); silu_ok = sem("silu_ok"); hid_ok = sem("hid_ok"); hidT_mm = sem("hidT_mm"); hidT_ok = sem("hidT_ok"); down_mm = sem("down_mm")
        dve_step = sem("dve_step"); act_step = sem("act_step"); x_out = sem("x_out")

        x_d = a["x"].rearrange("b (t p) d -> p (b t) d", p=P)
        out_d = out.rearrange("b (t p) d -> p (b t) d", p=P)

        def tile_of(w, block):
            return w.rearrange("(p k) n -> p k n", k=KC)[:, :, block * NB:(block + 1) * NB]

        def row_on_all(v, n):
            return v.rearrange("(o n) -> o n", o=1).broadcast_to([P, n])

        ring, arrivals = [], [0] * 4

        def ring_item(s, copies, free):
            arrivals[s] += 16 * len(copies)
            ring.append((s, copies, free))
            return s, arrivals[s]

        def ada_copy(s, i):
            return [(slot(s, KC, NB), tile_of(a["ada_w"][i // NADA], i % NADA))]

        def expert_copies(s, gate, up, down):
            half = KC * F
            base = slot(s, 2 * half + FK * D)
            return [(base[:, 0:half], gate.rearrange("(p k) f -> p (k f)", k=KC)),
                    (base[:, half:2 * half], up.rearrange("(p k) f -> p (k f)", k=KC)),
                    (base[:, 2 * half:], down.rearrange("(p c) d -> p (c d)", c=FK))]

        ada_at, proj_at = {}, {}
        for i, s in zip(range(4), (0, 1, 2, 0)):
            ada_at[i] = ring_item(s, ada_copy(s, i), [(ada_mm, 1)] if i == 3 else [])
        for j, s in enumerate((1, 2, 0, 1, 2, 0)):
            free = (ada_mm, (2, 3, 4)[j]) if j < 3 else (proj_mm, j - 2)
            proj_at[j] = ring_item(s, [(slot(s, KC, NB), tile_of(a["rwkv_w_rkv"][0, j // HB], j % HB))], [free])
        for i in range(4, 2 * NADA):
            s = 1 - i % 2
            free = (proj_mm, i) if i == 4 else (proj_mm, 6) if i == 5 else (ada_mm, i - 1)
            ada_at[i] = ring_item(s, ada_copy(s, i), [free])
        for j in range(HB):
            s = 1 - j
            proj_at[6 + j] = ring_item(s, [(slot(s, KC, NB), tile_of(a["rwkv_w_o"][0], j))], [(ada_mm, 23 + j)])

        UNITS = TT * (E + 1)
        base_in = {0: list(arrivals)}
        arrivals[2] += 48
        for e in range(E):
            arrivals[(3 + e) % 4] += 48
        ring2_start = len(ring)
        qslots = (3, 0, 1, 2, 3, 0)
        for j, s in enumerate(qslots):
            free = [(down_mm, UNITS - 2 * (3 - j))] if j < 4 else [(proj_mm, 8 + j - 4 + 1)]
            proj_at[8 + j] = ring_item(s, [(slot(s, KC, NB), tile_of(a["sb_w_qkv"][0], j))], free)
        for j, s in enumerate((1, 2)):
            proj_at[14 + j] = ring_item(s, [(slot(s, KC, NB), tile_of(a["sb_w_o"][0], j))], [(proj_mm, 8 + 2 + j + 1)])
        base_in[1] = list(arrivals)

        block = ctx.enter_context(nc.Block())

        @block.sync
        def _(sp):
            def run(items):
                for s, copies, free in items:
                    for sm, v in free:
                        sp.wait_ge(sm, v)
                    for dst, src in copies:
                        sp.dma_start(dst, src).then_inc(ring_in[s], 16)

            def moe(layer):
                first = 2 if layer == 0 else 3
                if layer == 0:
                    sp.wait_ge(h_ready, 2)
                else:
                    sp.wait_ge(proj_mm, 13)
                for dst, src in expert_copies(first, a["moe_ws_gate"][layer], a["moe_ws_up"][layer], a["moe_ws_down"][layer]):
                    sp.dma_start(dst, src).then_inc(ring_in[first], 16)

                def expert(e, s):
                    for dst, src in expert_copies(s, a["moe_w_gate"][layer, e], a["moe_w_up"][layer, e], a["moe_w_down"][layer, e]):
                        sp.dma_start(dst, src).then_inc(ring_in[s], 16)

                if layer == 0:
                    waits = [(proj_mm, 6), (proj_mm, 8), (proj_mm, 7)]
                else:
                    waits = [(proj_mm, 14), (proj_mm, 15), (proj_mm, 16)]
                for e in range(3):
                    sp.wait_ge(*waits[e])
                    expert(e, (first + 1 + e) % 4)
                sp.wait_ge(down_mm, UNITS * layer + 2)
                expert(3, first)
                with sp.Fori(0, E // 4 - 1) as j:
                    for q in range(4):
                        sp.wait_ge(down_mm, j * 8 + (UNITS * layer + 2 * (q + 2)))
                        e = sp.snap(j * 4 + (4 + q))
                        s = (first + 1 + q) % 4
                        expert_dyn(e, s, layer)

            def expert_dyn(e, s, layer):
                half = KC * F
                base = slot(s, 2 * half + FK * D)
                for n, (lo, hi, w) in enumerate(((0, half, "moe_w_gate"), (half, 2 * half, "moe_w_up"), (2 * half, 2 * half + FK * D, "moe_w_down"))):
                    src = a[w][layer].rearrange("e (p k) f -> p e (k f)", p=P)[:, bass.ds(e, 1), :]
                    sp.dma_start(base[:, lo:hi].rearrange("p (o f) -> p o f", o=1), src).then_inc(ring_in[s], 16)

            sp.dma_start(x[:], x_d).then_inc(x_in, 16)
            run(ring[:ring2_start])
            if STOP >= 2:
                moe(0)
            if STOP >= 3:
                run(ring[ring2_start:])
            if STOP >= 4:
                moe(1)
            sp.wait_ge(x_ready, STOP)
            sp.dma_start(out_d, x[:]).then_inc(x_out, 16)
            sp.wait_ge(x_out, 16)

        @block.gpsimd
        def _(pool):
            steps = [0]

            def link(ins):
                steps[0] += 1
                ins.then_inc(pool_step, 1)
                pool.wait_ge(pool_step, steps[0])

            pool.dma_start(ccol[:], a["c"].rearrange("b (p k) -> p (b k)", k=KC)).then_inc(small_in, 16)
            pool.dma_start(adab, a["ada_b"].rearrange("l (n c) -> (l n) c", c=NB)).then_inc(small_in, 16)
            pool.dma_start(mu[:], a["rwkv_mu"][0].rearrange("n (p k) -> p n k", k=KC)).then_inc(small_in, 16)
            for l in range(2):
                pool.dma_start(rb[:, l, :], row_on_all(a["moe_router_bias"][l], E)).then_inc(small_in, 16)
            for dst, src in ((w1w, a["rwkv_w_w1"]), (w1a, a["rwkv_w_a1"]), (w1g, a["rwkv_w_g1"])):
                pool.dma_start(dst, src[0].rearrange("(p k) n -> p k n", k=KC)).then_inc(lora_in, 16)
            pool.dma_start(w2w[0:LW], a["rwkv_w_w2"][0]).then_inc(lora_in, 16)
            pool.dma_start(w2w[LW:LW + 1], a["rwkv_w0"]).then_inc(lora_in, 16)
            pool.dma_start(w2a[0:LA], a["rwkv_w_a2"][0]).then_inc(lora_in, 16)
            pool.dma_start(w2a[LA:LA + 1], a["rwkv_a0"]).then_inc(lora_in, 16)
            pool.dma_start(w2g, a["rwkv_w_g2"][0]).then_inc(lora_in, 16)
            for dst, n in ((kkrow, "rwkv_k_k"), (karow, "rwkv_k_a")):
                pool.dma_start(dst, row_on_all(a[n][0], D)).then_inc(rows_in, 16)
            pool.dma_start(rkrow, row_on_all(a["rwkv_r_k"][0].rearrange("h d -> (h d)"), D)).then_inc(rows_in, 16)

            g = nc.gpsimd
            link(g.memset(sel[:], 0.0))
            link(g.memset(ident[:], 0.0))
            link(g.memset(ones[:], 1.0))
            link(g.memset(zmask[:], 0.0))
            link(g.memset(halves[:], 0.0))
            link(g.memset(hT[:, :, 0:1], 0.0))
            link(g.memset(t1[64:65, 0:2, :], 1.0))
            link(g.memset(upto[:], 1.0))
            for q in range(4):
                link(g.memset(sel[32 * q:32 * q + 1, :], 1.0))
            link(g.memset(halves[64:128, 0:1], 1.0))
            link(g.memset(halves[0:64, 1:2], 1.0))
            link(g.affine_select(out=ident[:], in_=ident[:], compare_op=ALU.not_equal, fill=1.0, base=0, pattern=[[-1, P]], channel_multiplier=1))
            link(g.affine_select(out=upto[:, 0, :], in_=upto[:, 0, :], compare_op=ALU.is_ge, fill=0.0, base=-1, pattern=[[1, P]], channel_multiplier=-1))
            link(g.affine_select(out=upto[:, 1, :], in_=upto[:, 1, :], compare_op=ALU.is_ge, fill=0.0, base=0, pattern=[[1, P]], channel_multiplier=-1))
            link(g.affine_select(out=fromj[:], in_=ones[:], compare_op=ALU.is_ge, fill=0.0, base=0, pattern=[[-1, P]], channel_multiplier=1))
            for c in (0, 2):
                last = g.affine_select(out=zmask[:, c * P:(c + 1) * P], in_=zmask[:, c * P:(c + 1) * P], compare_op=ALU.is_ge, fill=-1e30, base=-1, pattern=[[1, P]], channel_multiplier=-1)
                if c == 0:
                    link(last)
            last.then_inc(const_ok, 1)

            def load_pre(s):
                l, off = s // 2, NADA // 2 * (s % 2) + NADA * (s // 2)
                gain = "norm_pre_mix" if s % 2 == 0 else "norm_pre_ffn"
                pool.wait_ge(mod_stored[1], 16 * ((off + 3) // 2 + 1))
                pool.wait_ge(mod_stored[0], 16 * ((off + 2) // 2 + 1))
                flat = mod_dram.rearrange("a b -> (a b)")
                pool.dma_start(mt[:, 0, :], row_on_all(flat[off * NB:(off + 2) * NB], D)).then_inc(mpre_in, 16)
                pool.dma_start(mt[:, 1, :], row_on_all(flat[(off + 2) * NB:(off + 4) * NB], D)).then_inc(mpre_in, 16)
                pool.dma_start(mt[:, 2, :], row_on_all(a[gain][l], D)).then_inc(mpre_in, 16)

            def load_post(s):
                l, off = s // 2, NADA // 2 * (s % 2) + NADA * (s // 2)
                gain = "norm_post_mix" if s % 2 == 0 else "norm_post_ffn"
                pool.wait_ge(mod_stored[1], 16 * ((off + 5) // 2 + 1))
                pool.wait_ge(mod_stored[0], 16 * ((off + 4) // 2 + 1))
                flat = mod_dram.rearrange("a b -> (a b)")
                pool.dma_start(mt[:, 3, :], row_on_all(flat[(off + 4) * NB:(off + 6) * NB], D)).then_inc(mpost_in, 16)
                pool.dma_start(mt[:, 4, :], row_on_all(a[gain][l], D)).then_inc(mpost_in, 16)

            load_pre(0)
            pool.wait_ge(h_ready, 1)
            pool.dma_start(mt[:, 0, :], row_on_all(a["rwkv_lnx_g"][0], D)).then_inc(lnx_in, 16)
            pool.wait_ge(sb_ok, FC)
            for i in range(4):
                pool.dma_start(diag_dram[i], AAB[32 * i:32 * i + 32, :, 32 * i:32 * i + 32]).then_inc(diag_out, 16)
            pool.wait_ge(diag_out, 64)
            pool.wait_ge(tr_mm, 20)
            for i in range(4):
                pool.dma_start(DT[32 * i:32 * i + 32], diag_dram[i].rearrange("s u t -> u s t")).then_inc(diag_in, 16)
            link(g.memset(TTi, 0.0))
            g.affine_select(out=TTi, in_=TTi, compare_op=ALU.not_equal, fill=1.0, base=0, pattern=[[1, 32], [-1, 32]], channel_multiplier=0).then_inc(ti_init, 1)
            pool.wait_ge(inv_ok, 1)
            pool.dma_start(inv_dram.rearrange("i u s t -> (i u) (s t)"), h[:, 1, :]).then_inc(inv_out, 16)
            pool.wait_ge(inv_out, 16)
            for i in range(4):
                pool.dma_start(TB[32 * i:32 * i + 32], inv_dram[i].rearrange("u s t -> s u t")).then_inc(inv_in, 16)
            pool.wait_ge(xo_mm, FC)
            pool.dma_start(mt[:, 1, :], row_on_all(a["rwkv_lnx_b"][0], D)).then_inc(lnx_in, 16)
            pool.wait_ge(mod_stored[1], 16 * NADA)
            pool.wait_ge(mod_stored[0], 16 * NADA)
            load_post(0)
            for s in range(1, STOP):
                pool.wait_ge(h_ready, (0, 2, 3, 5)[s])
                load_pre(s)
                pool.wait_ge(x_ready, s)
                if s % 2:
                    pool.dma_start(rw, a["moe_w_router"][s // 2].rearrange("(p k) e -> p k e", k=KC)).then_inc(router_in, 16)
                load_post(s)

        @block.tensor
        def _(pe):
            mm = nc.tensor.matmul

            def ada_mm_step(i):
                s, v = ada_at[i]
                pe.wait_ge(ring_in[s], v)
                if i >= 1:
                    pe.wait_ge(ada_part, i)
                w = slot(s, KC, NB)
                for j in range(2):
                    for q in range(4):
                        last = mm(PS[32 * q:32 * q + 32, 7, :], crep[:, 2 * q + j, :], w[:, 2 * q + j, :], start=(j == 0), stop=(j == 1))
                last.then_inc(ada_mm, 1)

            def ada_row_step(i):
                pe.wait_ge(ada_part, i + 1)
                if i >= 1:
                    pe.wait_ge(ada_row, i)
                mm(PS[0:1, 6, :], sel[:, 0:1], apart, start=True, stop=False)
                mm(PS[0:1, 6, :], ident[0:2 * NADA, i:i + 1], adab, start=False, stop=True).then_inc(ada_row_mm, 1)

            def ada(i):
                if i in ada_at:
                    ada_mm_step(i)
                if i - 1 in ada_at and i != 4:
                    ada_row_step(i - 1)

            def turn(n, src):
                for f in range(4):
                    fill = 4 * n + f
                    if fill >= 2:
                        pe.wait_ge(tr_act if fill % 2 == 0 else tr_dve, fill // 2)
                    for q in range(4):
                        last = nc.tensor.transpose(PS[:, 4 + f % 2, q * P:(q + 1) * P], src(f // 2, 4 * (f % 2) + q), ident[:])
                    last.then_inc(tr_mm, 1)

            def turned(n):
                pe.wait_ge(tr_act, 2 * (n + 1))
                pe.wait_ge(tr_dve, 2 * (n + 1))

            def hsrc(t, k):
                return h[:, t, k * P:(k + 1) * P]

            def proj(n, src, banks, free):
                s, v = proj_at[n]
                pe.wait_ge(ring_in[s], v)
                for sm, val in free:
                    pe.wait_ge(sm, val)
                w = slot(s, KC, NB)
                for t in range(TT):
                    for k in range(KC):
                        last = mm(PS[:, banks[t], :], src(k, t), w[:, k, :], start=(k == 0), stop=(k == KC - 1))
                last.then_inc(proj_mm, 1)

            def hTsrc(k, t):
                return hT[:, k, 1 + t * P:1 + (t + 1) * P]

            def head(fc, p):
                return 2 * fc + p

            pe.wait_ge(const_ok, 1)
            pe.wait_ge(crep_ok, 1)
            for i in range(4):
                ada_mm_step(i)
                ada_row_step(i)

            pe.wait_ge(h_ready, 1)
            turn(0, hsrc)
            pe.wait_ge(lora_in, 16 * 8)
            for m, (w1, w2, n1, n2) in enumerate(((w1w, w2w, LW, LW + 1), (w1a, w2a, LA, LA + 1), (w1g, w2g, LG, LG))):
                pe.wait_ge(xs_ready, m + 1)
                if m:
                    pe.wait_ge(lora1_ok, m)
                else:
                    turned(0)
                for k in range(KC):
                    last = mm(PS[0:n1, 5, 0:S], w1[:, k, :], xs[m % 2][:, k, :], start=(k == 0), stop=(k == KC - 1))
                last.then_inc(lora1_mm, 1)
                pe.wait_ge(lora1_ok, m + 1)
                if m:
                    pe.wait_ge(lora2_ok, m)
                for t in range(TT):
                    for b in range(HB):
                        last = mm(PS[:, 2 * t + b, :], t1[0:n2, m, t * P:(t + 1) * P], w2[0:n2, b * NB:(b + 1) * NB], start=True, stop=True)
                last.then_inc(lora2_mm, 1)
            for m in range(3):
                pe.wait_ge(xs_ready, 4 + m)
                for b in range(HB):
                    n = HB * m + b
                    src = (lambda m: lambda k, t: xs[(3 + m) % 2][:, k, t * P:(t + 1) * P])(m)
                    proj(n, src, (2 * b, 2 * b + 1), [(lora2_ok, 3)] if n < 2 else [(proj_ok, n - 1)])

            for fc in range(FC):
                for t in range(TT):
                    last = mm(PS[:, 5, fc:fc + 1], sig[:, t, fc * P:(fc + 1) * P], halves[:, t:t + 1], start=(fc == 0 and t == 0), stop=(t == TT - 1), skip_group_check=True)
            last.then_inc(cum_mm, 1)
            pe.wait_ge(triA_ok, 1)
            for n in (1, 0):
                if n == 1:
                    pe.wait_ge(proj_ok, 6)
                else:
                    pe.wait_ge(decay_ok, 3)
                for t in range(TT):
                    for b in range(HB):
                        last = mm(PS[:, 2 * t + b, :], cumx[:, n, :], sig[:, t, b * NB:(b + 1) * NB], start=True, stop=True)
                last.then_inc(cum_mm, 1)
            ada(4)
            ada(5)
            for n, buf in ((1, a_), (2, k_), (3, r_), (4, h)):
                pe.wait_ge(tok_ready, n)
                if n == 1:
                    pe.wait_ge(decay_ok, 1)
                turn(n, (lambda b: lambda t, k: b[:, t, k * P:(k + 1) * P])(buf))
                ada(5 + n)
            turned(4)

            for fc in range(FC):
                if fc >= 2:
                    pe.wait_ge(sb_ok, fc - 1)
                else:
                    pe.wait_ge(decay_ok, 4)
                for t in range(TT):
                    for p in range(2):
                        last = mm(PS[:, 2 * (fc % 2) + p, t * 256:(t + 1) * 256], bT[64 * p:64 * p + 64, fc, t * P:(t + 1) * P],
                                  ART[64 * p:64 * p + 64, fc, t, :, :], start=(t == 0), stop=(t == 1), skip_group_check=True)
                last.then_inc(sb_mm, 1)
                if fc % 2:
                    ada(10 + fc // 2)

            FP = FC // 2

            def score_k(t, j):
                n = FP * t + j
                if j:
                    pe.wait_ge(sk_ok, n)
                for f in range(2):
                    fc = 2 * j + f
                    for p in range(2):
                        last = mm(PS[:, 2 + p, f * 256:(f + 1) * 256], kT[64 * p:64 * p + 64, fc, t * P:(t + 1) * P],
                                  ART[64 * p:64 * p + 64, fc, t, :, :], start=(f == 0), stop=True, skip_group_check=True)
                last.then_inc(sk_mm, 1)

            def score_v(t, j):
                n = FP * t + j
                pe.wait_ge(sk_ok, n + 1)
                for f in range(2):
                    fc = 2 * j + f
                    for p in range(2):
                        rhs = v_[:, t, head(fc, p) * HD:(head(fc, p) + 1) * HD]
                        mm(PS[:, p, fc * HD:(fc + 1) * HD], SK[j % 2][:, f, p, 0:P], rhs, start=(fc == 0), stop=False, skip_group_check=True)
                        last = mm(PS[:, 4 + p, fc * HD:(fc + 1) * HD], SK[j % 2][:, f, p, P:2 * P], rhs, start=(fc == 0), stop=False, skip_group_check=True)
                last.then_inc(xo_mm, 1)

            for t in range(TT):
                if t == 0:
                    pe.wait_ge(sb_ok, FC)
                else:
                    pe.wait_ge(o_ok, 1)
                    pe.wait_ge(s0_ok, 1)
                score_k(t, 0)
                for j in range(FP):
                    if j + 1 < FP:
                        score_k(t, j + 1)
                    score_v(t, j)
                for fc in range(FC) if t else ():
                    for p in range(2):
                        mm(PS[:, 4 + p, fc * HD:(fc + 1) * HD], ART[64 * p:64 * p + 64, fc, t, 1, :], S0T[64 * p:64 * p + 64, fc, :], start=False, stop=False, skip_group_check=True)
                        last = mm(PS[:, p, fc * HD:(fc + 1) * HD], ART[64 * p:64 * p + 64, fc, t, 0, :], S0T[64 * p:64 * p + 64, fc, :], start=False, stop=False, skip_group_check=True)
                if t == 0:
                    for i in range(14, 20):
                        ada(i)
                    pe.wait_ge(inv_in, 64)
                for i in range(4):
                    n = 4 * t + i
                    rows = slice(32 * i, 32 * i + 32)
                    if i:
                        pe.wait_ge(u_act, n)
                        pe.wait_ge(u_dve, n)
                        for fc in range(FC):
                            for p in range(2):
                                last = mm(PS[rows, p, fc * HD:(fc + 1) * HD], AAB[0:32 * i, t * H + head(fc, p), rows], U[0:32 * i, p, fc * HD:(fc + 1) * HD],
                                          start=False, stop=False, skip_group_check=True)
                        last.then_inc(xacc_mm, 1)
                    if i == 0 and t:
                        last.then_inc(xacc_mm, 1)
                    pe.wait_ge(acc_act, n + 1)
                    pe.wait_ge(acc_dve, n + 1)
                    for fc in range(FC):
                        for p in range(2):
                            last = mm(PS[rows, 2 + p, fc * HD:(fc + 1) * HD], TB[rows, t * H + head(fc, p), :], acc[rows, p, fc * HD:(fc + 1) * HD],
                                      start=(fc == 0), stop=True, skip_group_check=True)
                    last.then_inc(ub_mm, 1)
                    if t == 0:
                        ada(20 + i)
                pe.wait_ge(u_act, 4 * t + 4)
                pe.wait_ge(u_dve, 4 * t + 4)
                for fc in range(FC):
                    for p in range(2):
                        last = mm(PS[:, 4 + p, fc * HD:(fc + 1) * HD], ARB[:, t * H + head(fc, p), :], U[:, p, fc * HD:(fc + 1) * HD], start=False, stop=True, skip_group_check=True)
                last.then_inc(o_mm, 1)
                if t == 0:
                    for fc in range(FC):
                        for p in range(2):
                            cols = slice(head(fc, p) * HD, (head(fc, p) + 1) * HD)
                            mm(PS[64 * p:64 * p + 64, 2, fc * HD:(fc + 1) * HD], a_[:, 0, cols], U[:, p, fc * HD:(fc + 1) * HD], start=(fc == 0), stop=False, skip_group_check=True)
                            last = mm(PS[64 * p:64 * p + 64, 2, fc * HD:(fc + 1) * HD], k_[:, 0, cols], v_[:, 0, cols], start=False, stop=True, skip_group_check=True)
                    last.then_inc(st_mm, 1)
                    ada(24)

            def out_proj(n, t_set):
                turned(t_set)
                for j in range(HB):
                    proj(n + j, hTsrc, (j, 2 + j), [])

            pe.wait_ge(o_ok, 2)
            pe.wait_ge(h_ready, 2)
            turn(5, hsrc)
            out_proj(6, 5)

            def moe(layer, t_set):
                pe.wait_ge(h_ready, (3, 6)[layer])
                turn(t_set, hsrc)
                pe.wait_ge(router_in, 16 * (layer + 1))
                turned(t_set)
                for t in range(TT):
                    for k in range(KC):
                        last = mm(PS[:, 4, t * E:(t + 1) * E], hTsrc(k, t), rw[:, k, :], start=(t == 0 and k == 0), stop=(k == KC - 1), skip_group_check=True)
                last.then_inc(log_mm, 1)
                pe.wait_ge(sc_ok, 2 * (layer + 1))
                base = UNITS * layer
                first = (2, 3)[layer]
                half = KC * F

                def gate_up(off, n, s, arrive):
                    t = n % 2
                    if t == 0:
                        pe.wait_ge(ring_in[s], arrive)
                    if not (isinstance(off, int) and n < 2 and layer == 0):
                        pe.wait_ge(hid_ok, off + (base + n - 1))
                    w = slot(s, 2, KC, F)
                    for k in range(KC):
                        last = mm(PS[:, 4 + t, :], hTsrc(k, t), w[:, :, k, :], start=(k == 0), stop=(k == KC - 1))
                    last.then_inc(gu_mm, 1)

                def turn_hidden(off, n):
                    t = n % 2
                    pe.wait_ge(hid_ok, off + (base + n + 1))
                    if not (isinstance(off, int) and n < 2 and layer == 0):
                        pe.wait_ge(hidT_ok, off + (base + n - 1))
                    for c in range(FK):
                        last = nc.tensor.transpose(PS[:, 6 + t, c * P:(c + 1) * P], actp[:, t, c, :], ident[:])
                    last.then_inc(hidT_mm, 1)

                def down(off, n, s, fresh, final):
                    t = n % 2
                    pe.wait_ge(hidT_ok, off + (base + n + 1))
                    w = slot(s, 2 * half + FK * D)[:, 2 * half:].rearrange("p (c d) -> p c d", c=FK)
                    for c in range(FK):
                        for b in range(HB):
                            last = mm(PS[:, 2 * t + b, :], actT[:, t, c, :], w[:, c, b * NB:(b + 1) * NB],
                                      start=(fresh and c == 0), stop=(final and c == FK - 1), skip_group_check=True)
                    last.then_inc(down_mm, 1)

                slots = [(first + i) % 4 for i in range(4)]
                got = list(base_in[layer])
                got[first] += 48
                gate_up(0, 0, first, got[first])
                gate_up(0, 1, first, 0)
                turn_hidden(0, 0)

                def body(j, first_time):
                    for q in range(8):
                        n = 2 + q
                        s = slots[(1 + q // 2) % 4]
                        sprev = slots[(1 + (q - 2) // 2) % 4] if q >= 2 else slots[0]
                        gate_up(j * 8, n, s, j * 48 + (got[s] + 48))
                        turn_hidden(j * 8, n - 1)
                        down(j * 8, n - 2, sprev, first_time and q < 2, False)

                body(0, True)
                with pe.Fori(1, E // 4) as j:
                    body(j, False)
                n = UNITS - 1
                turn_hidden(0, n)
                down(0, n - 1, slots[0], False, True)
                down(0, n, slots[0], False, True)

            if STOP >= 2:
                moe(0, 6)

            if STOP >= 3:
                pe.wait_ge(h_ready, 4)
                turn(7, hsrc)
                turned(7)
                for n in range(6):
                    proj(8 + n, hTsrc, (2 * (n % 2), 2 * (n % 2) + 1), [(proj_ok, 6 + n - 1)] if n >= 2 else [(x_ready, 2)])
                for n, part in ((8, 0), (9, 1)):
                    pe.wait_ge(proj_ok, 6 + 2 * (part + 1))
                    turn(n, (lambda q: lambda t, k: qkv[:, t, q * D + k * P:q * D + (k + 1) * P])(part))
                turned(9)
                pe.wait_ge(proj_ok, 12)

                def z_scores(g):
                    if g:
                        pe.wait_ge(z_ok, g)
                    if g >= 2:
                        pe.wait_ge(o_taken, g - 1)
                    for j in range(4):
                        fc, p = 2 * g + j // 2, j % 2
                        q, k = qkT[64 * p:64 * p + 64, fc, :], qkT[64 * p:64 * p + 64, FC + fc, :]
                        mm(PS[:, j, 0:S], k[:, 0:P], q, start=True, stop=True, skip_group_check=True)
                        last = mm(PS[:, j, S:S + P], k[:, P:S], q[:, P:S], start=False, stop=True, skip_group_check=True)
                    last.then_inc(z_mm, 1)

                def tail_sums(g):
                    pe.wait_ge(sp_ok, g + 1)
                    if g:
                        pe.wait_ge(ez_ok, g)
                    for j in range(4):
                        mm(PS[:, 4 + j, 0:384], fromj[:], spb[g % 2][:, j, :], start=True, stop=False, skip_group_check=True)
                        last = mm(PS[:, 4 + j, P:S], ones[:], spb[g % 2][:, j, S:384], start=False, stop=True, skip_group_check=True)
                    last.then_inc(rc_mm, 1)

                def weigh_v(g):
                    pe.wait_ge(w_ok, g + 1)
                    if g + 1 < 4:
                        pe.wait_ge(z_ok, g + 2)
                    for j in range(4):
                        hd = 4 * g + j
                        w = spb[g % 2][:, j, :]
                        v0, v1 = (qkv[:, t, 2 * D + hd * HD:2 * D + (hd + 1) * HD] for t in range(TT))
                        mm(PS[:, j, 384:384 + HD], w[:, 0:P], v0, start=True, stop=True, skip_group_check=True)
                        mm(PS[:, j, 384 + HD:NB], w[:, P:2 * P], v0, start=False, stop=False, skip_group_check=True)
                        last = mm(PS[:, j, 384 + HD:NB], w[:, 2 * P:384], v1, start=False, stop=True, skip_group_check=True)
                    last.then_inc(pv_mm, 1)

                z_scores(0)
                for g in range(4):
                    if g + 1 < 4:
                        z_scores(g + 1)
                    tail_sums(g)
                    weigh_v(g)
                pe.wait_ge(h_ready, 5)
                turn(10, hsrc)
                out_proj(14, 10)
            if STOP >= 4:
                moe(1, 11)

        @block.scalar
        def _(act):
            fn = nc.scalar.activation
            steps = [0]

            def link(ins):
                steps[0] += 1
                ins.then_inc(act_step, 1)
                act.wait_ge(act_step, steps[0])

            def copy(out_, in_):
                return fn(out_, in_, ACT.Copy)

            def ada_part_step(i):
                act.wait_ge(ada_mm, i + 1)
                if i >= 1:
                    act.wait_ge(ada_row_mm, i)
                copy(apart, PS[:, 7, :]).then_inc(ada_part, 1)

            def ada_row_step(i):
                act.wait_ge(ada_row_mm, i + 1)
                if i >= 2:
                    act.wait_ge(mod_stored[i % 2], 16 * (i // 2))
                copy(arow[:, i % 2, :], PS[0:1, 6, :]).then_inc(ada_row, 1)
                act.wait_ge(ada_row, i + 1)
                act.dma_start(mod_dram[i:i + 1, :], arow[:, i % 2, :]).then_inc(mod_stored[i % 2], 16)

            def ada(i):
                if i in ada_at:
                    ada_part_step(i)
                if i - 1 in ada_at and i != 4:
                    ada_row_step(i - 1)

            def rms(n, src):
                for t in range(TT):
                    fn(h[:, t, :], src(t), ACT.Square, accum_out=ss[:, n, t:t + 1]).then_inc(ss_ready, 1)
                act.wait_ge(ms_ready, n + 1)
                fn(rstd[:, n, :], ms[:, n, :], ACT.Sqrt).then_inc(rstd_ready, 1)

            def turn(n, dst):
                for t in range(TT):
                    act.wait_ge(tr_mm, 4 * n + 2 * t + 1)
                    copy(dst(t, 0), PS[:, 4, :].rearrange("p (k s) -> p k s", k=4)).then_inc(tr_act, 1)

            def hdst(t, b):
                return hT[:, 4 * b:4 * b + 4, 1 + t * P:1 + (t + 1) * P]

            def pre(s, t_set):
                if s:
                    act.wait_ge(x_ready, s)
                else:
                    act.wait_ge(x_in, 16)
                rms(2 * s, lambda t: x[:, t, :])
                turn(t_set, hdst)

            def post(s, y_done):
                act.wait_ge(*y_done)
                rms(2 * s + 1, lambda t: PS[:, 2 * t:2 * t + 2, :])

            act.wait_ge(small_in, 5 * 16)
            fn(ccol[:], ccol[:], ACT.Silu).then_inc(ccol_ok, 1)
            act.wait_ge(ccol_ok, 1)
            fn(crep[:], ccol[:].rearrange("p (k o) -> p k o", o=1).broadcast_to([P, KC, 32]), ACT.Copy).then_inc(crep_ok, 1)
            for i in range(4):
                ada_part_step(i)
                ada_row_step(i)

            pre(0, 0)
            for m, (dst, f1, f2, n1) in enumerate(((sig, ACT.Tanh, ACT.Sigmoid, LW), (a_, ACT.Copy, ACT.Sigmoid, LA), (g_, ACT.Sigmoid, ACT.Copy, LG))):
                act.wait_ge(lora1_mm, m + 1)
                fn(t1[0:n1, m, :], PS[0:n1, 5, 0:S], f1).then_inc(lora1_ok, 1)
                act.wait_ge(lora2_mm, m + 1)
                fn(dst.rearrange("p t (b c) -> p (t b) c", b=HB), PS[:, 0:4, :], f2).then_inc(lora2_ok, 1)
            for n in range(6):
                dst = (r_, k_, v_)[n // 2]
                b = n % 2
                act.wait_ge(proj_mm, n + 1)
                copy(dst[:, :, b * NB:(b + 1) * NB], PS[:, 2 * b:2 * b + 2, :]).then_inc(proj_ok, 1)
            act.wait_ge(cum_mm, 1)
            fn(edec[:], PS[:, 5, 0:FC], ACT.Exp, scale=-DECAY).then_inc(decay_ok, 1)
            act.wait_ge(kss_ready, 1)
            fn(hs[:, 1, :], hs[:, 0, :], ACT.Sqrt).then_inc(knorm_ok, 1)
            act.wait_ge(cum_mm, 2)
            act.wait_ge(xy_free, 1)
            sums = PS[:, 0:4, :]
            fn(tmpX.rearrange("p t (b c) -> p (t b) c", b=HB), sums, ACT.Exp, scale=DECAY).then_inc(decay_ok, 1)
            fn(tmpY.rearrange("p t (b c) -> p (t b) c", b=HB), sums, ACT.Exp, scale=-DECAY).then_inc(decay_ok, 1)
            act.wait_ge(cum_mm, 3)
            fn(sig.rearrange("p t (b c) -> p (t b) c", b=HB), sums, ACT.Exp, scale=-DECAY).then_inc(decay_ok, 1)
            ada(4)
            ada(5)
            for n, dst in ((1, lambda t, b: bT[:, 4 * b:4 * b + 4, t * P:(t + 1) * P]),
                           (2, lambda t, b: kT[:, 4 * b:4 * b + 4, t * P:(t + 1) * P]),
                           (3, lambda t, b: ART[:, 4 * b:4 * b + 4, t, 1, :]),
                           (4, lambda t, b: ART[:, 4 * b:4 * b + 4, t, 0, :])):
                turn(n, dst)
                ada(5 + n)
            for i in range(10, 20):
                ada(i)
            for t in range(TT):
                for i in range(4):
                    n = 4 * t + i
                    rows = slice(32 * i, 32 * i + 32)
                    if i == 0:
                        act.wait_ge(xo_mm, FC // 2 * (t + 1))
                    if n >= 1:
                        act.wait_ge(xacc_mm, n)
                    copy(acc[rows, 0, :], PS[rows, 0, :]).then_inc(acc_act, 1)
                    if t == 0 and i:
                        ada(20 + i - 1)
                    act.wait_ge(ub_mm, n + 1)
                    copy(U[rows, 0, :], PS[rows, 2, :]).then_inc(u_act, 1)
                act.wait_ge(o_mm, t + 1)
                copy(o_[:, t, :].rearrange("p (f q d) -> p q f d", f=FC, q=2), PS[:, 4:6, :].rearrange("p q (f d) -> p q f d", f=FC)).then_inc(o_ok, 1)
                if t == 0:
                    ada(23)
                    ada(24)
            act.wait_ge(lvar_ready, 1)
            fn(hs[:, 3, :], hs[:, 2, :], ACT.Sqrt).then_inc(lstd_ok, 1)
            turn(5, hdst)
            post(0, (proj_mm, 8))

            def moe(layer, s, t_set):
                pre(s, t_set)
                act.wait_ge(log_mm, layer + 1)
                fn(rt[:, 0], PS[:, 4, 0:TT * E].rearrange("p (t e) -> p t e", t=TT), ACT.Sigmoid).then_inc(sc_ok, 1)
                base = UNITS * layer

                def silu(off, n):
                    t = n % 2
                    act.wait_ge(gu_mm, off + (base + n + 1))
                    if not (isinstance(off, int) and n < 2 and layer == 0):
                        act.wait_ge(hid_ok, off + (base + n - 1))
                    fn(gsil[:, t, :], PS[:, 4 + t, 0:F], ACT.Silu).then_inc(silu_ok, 1)

                def hidden_turned(off, n):
                    t = n % 2
                    act.wait_ge(hidT_mm, off + (base + n + 1))
                    if not (isinstance(off, int) and n < 2 and layer == 0):
                        act.wait_ge(down_mm, off + (base + n - 1))
                    copy(actT[:, t], PS[:, 6 + t, 0:F].rearrange("p (c s) -> p c s", c=FK)).then_inc(hidT_ok, 1)

                silu(0, 0)
                silu(0, 1)
                hidden_turned(0, 0)
                for q in range(8):
                    silu(0, 2 + q)
                    hidden_turned(0, 1 + q)
                with act.Fori(1, E // 4) as j:
                    for q in range(8):
                        silu(j * 8, 2 + q)
                        hidden_turned(j * 8, 1 + q)
                hidden_turned(0, UNITS - 1)
                post(s, (down_mm, UNITS * (layer + 1)))

            if STOP >= 2:
                moe(0, 1, 6)

            if STOP >= 3:
                pre(2, 7)
                for n in range(6):
                    act.wait_ge(proj_mm, 8 + n + 1)
                    fn(qkv[:, :, n * NB:(n + 1) * NB], PS[:, 2 * (n % 2):2 * (n % 2) + 2, :], ACT.Copy,
                       scale=HD ** -0.5 if n < 2 else 1.0).then_inc(proj_ok, 1)
                for n in (8, 9):
                    turn(n, (lambda o: lambda t, b: qkT[:, o + 4 * b:o + 4 * b + 4, t * P:(t + 1) * P])((n - 8) * FC))

                def log_part(g):
                    b = spb[g % 2]
                    act.wait_ge(z_ok, g + 1)
                    if g >= 2:
                        act.wait_ge(pv_mm, g - 1)
                    link(fn(b, zsb[g % 2], ACT.Abs))
                    link(fn(b, b, ACT.Exp, scale=-1.0))
                    fn(b, b, ACT.Ln, bias=1.0).then_inc(l_ok, 1)

                def weights(g):
                    act.wait_ge(ez_ok, g + 1)
                    fn(spb[g % 2], zsb[g % 2], ACT.Exp).then_inc(w_ok, 1)

                log_part(0)
                for g in range(4):
                    if g + 1 < 4:
                        log_part(g + 1)
                    weights(g)
                turn(10, hdst)
                post(2, (proj_mm, 16))
            if STOP >= 4:
                moe(1, 3, 11)

        @block.vector
        def _(dve):
            V = nc.vector
            steps = [0]

            def link(ins):
                steps[0] += 1
                ins.then_inc(dve_step, 1)
                dve.wait_ge(dve_step, steps[0])

            def rms(n):
                dve.wait_ge(ss_ready, 2 * (n + 1))
                link(V.tensor_scalar(ms[:, n, :], ss[:, n, :], 1.0 / D, RMS_EPS, ALU.mult, ALU.add))
                V.reciprocal(ms[:, n, :], ms[:, n, :]).then_inc(ms_ready, 1)
                dve.wait_ge(rstd_ready, n + 1)

            def turn(n, dst):
                for t in range(TT):
                    dve.wait_ge(tr_mm, 4 * n + 2 * t + 2)
                    V.tensor_copy(dst(t, 1), PS[:, 5, :].rearrange("p (k s) -> p k s", k=4)).then_inc(tr_dve, 1)

            def hdst(t, b):
                return hT[:, 4 * b:4 * b + 4, 1 + t * P:1 + (t + 1) * P]

            def hperm(t):
                return h[:, t, :].rearrange("p (k q) -> p q k", k=KC)

            def pre(s, t_set):
                rms(2 * s)
                dve.wait_ge(mpre_in, 48 * (s + 1))
                link(V.scalar_tensor_tensor(out=mt[:, 1, :], in0=mt[:, 1, :], scalar=1.0, in1=mt[:, 2, :], op0=ALU.add, op1=ALU.mult))
                for t in range(TT):
                    link(V.scalar_tensor_tensor(out=mt[:, 2, :], in0=x[:, t, :], scalar=rstd[:, 2 * s, t:t + 1], in1=mt[:, 1, :], op0=ALU.mult, op1=ALU.mult))
                    last = V.tensor_tensor(hperm(t), mt[:, 2, :].rearrange("p (q k) -> p q k", k=KC), mt[:, 0, :].rearrange("p (q k) -> p q k", k=KC), ALU.add)
                    if t == 0:
                        link(last)
                last.then_inc(h_ready, 1)
                turn(t_set, hdst)

            def post(s):
                dve.wait_ge(mpost_in, 32 * (s + 1))
                link(V.tensor_tensor(mt[:, 3, :], mt[:, 3, :], mt[:, 4, :], ALU.mult))
                rms(2 * s + 1)
                for t in range(TT):
                    link(V.scalar_tensor_tensor(out=mt[:, 4, :].rearrange("p (b c) -> p b c", b=HB), in0=PS[:, 2 * t:2 * t + 2, :], scalar=rstd[:, 2 * s + 1, t:t + 1],
                                                in1=mt[:, 3, :].rearrange("p (b c) -> p b c", b=HB), op0=ALU.mult, op1=ALU.mult))
                    last = V.tensor_tensor(x[:, t, :], x[:, t, :], mt[:, 4, :], ALU.add)
                    if t == 0:
                        link(last)
                last.then_inc(x_ready, 1)

            dve.wait_ge(const_ok, 1)
            V.tensor_scalar(cumx[0:64], upto[0:64], -1.0, None, ALU.add)
            V.tensor_copy(cumx[64:128], upto[64:128]).then_inc(triA_ok, 1)

            pre(0, 0)
            dve.wait_ge(tr_act, 2)
            dve.wait_ge(tr_dve, 2)
            link(V.tensor_tensor(xx, hT[:, :, 0:S], hT[:, :, 1:S + 1], ALU.subtract))
            dve.wait_ge(small_in, 5 * 16)
            for m, n in enumerate((3, 4, 5, 0, 1, 2)):
                if m >= 2:
                    if m <= 4:
                        dve.wait_ge(lora1_mm, m - 1)
                    else:
                        dve.wait_ge(proj_mm, 2)
                for k in range(KC):
                    last = V.scalar_tensor_tensor(out=xs[m % 2][:, k, :], in0=xx[:, k, :], scalar=mu[:, n, k:k + 1], in1=hT[:, k, 1:S + 1], op0=ALU.mult, op1=ALU.add)
                last.then_inc(xs_ready, 1)

            def heads(v):
                return v.rearrange("p t (h d) -> p (t h) d", d=HD)

            def both(row):
                return row.rearrange("p (o d) -> p o d", o=1).broadcast_to([P, TT, D])

            def per_head(col):
                return col.rearrange("p (n o) -> p n o", o=1).broadcast_to([P, TT * H, HD])

            dve.wait_ge(proj_ok, 4)
            dve.wait_ge(rows_in, 48)
            dve.wait_ge(lora2_ok, 3)
            dve.wait_ge(tr_mm, 4)
            link(V.tensor_tensor(h[:], k_, both(kkrow), ALU.mult))
            link(V.tensor_tensor(tmpX, h[:], h[:], ALU.mult))
            V.tensor_reduce(hs[:, 0, :], heads(tmpX), AX.X, ALU.add).then_inc(kss_ready, 1)
            link(V.scalar_tensor_tensor(out=tmpY, in0=a_, scalar=-1.0, in1=both(karow), op0=ALU.add, op1=ALU.mult))
            link(V.scalar_tensor_tensor(out=k_, in0=tmpY, scalar=1.0, in1=k_, op0=ALU.add, op1=ALU.mult))
            link(V.tensor_tensor(tmpX, r_, k_, ALU.mult))
            link(V.tensor_tensor(tmpX, tmpX, both(rkrow), ALU.mult))
            V.tensor_reduce(bonus[:], heads(tmpX), AX.X, ALU.add).then_inc(xy_free, 1)
            dve.wait_ge(knorm_ok, 1)
            link(V.tensor_scalar(hs[:, 1, :], hs[:, 1, :], 1e-12, None, ALU.max))
            link(V.reciprocal(hs[:, 1, :], hs[:, 1, :]))
            link(V.tensor_tensor(heads(h[:]), heads(h[:]), per_head(hs[:, 1, :]), ALU.mult))
            link(V.tensor_tensor(a_, a_, h[:], ALU.mult))
            dve.wait_ge(decay_ok, 2)
            V.tensor_tensor(a_, a_, tmpX, ALU.mult).then_inc(tok_ready, 1)
            V.tensor_tensor(k_, k_, tmpX, ALU.mult).then_inc(tok_ready, 1)
            dve.wait_ge(decay_ok, 3)
            V.tensor_tensor(r_, r_, tmpY, ALU.mult).then_inc(tok_ready, 1)
            dve.wait_ge(decay_ok, 4)
            V.scalar_tensor_tensor(out=h[:], in0=h[:], scalar=-1.0, in1=sig, op0=ALU.mult, op1=ALU.mult).then_inc(tok_ready, 1)
            turn(1, lambda t, b: bT[:, 4 * b:4 * b + 4, t * P:(t + 1) * P])
            turn(2, lambda t, b: kT[:, 4 * b:4 * b + 4, t * P:(t + 1) * P])
            turn(3, lambda t, b: ART[:, 4 * b:4 * b + 4, t, 1, :])
            turn(4, lambda t, b: ART[:, 4 * b:4 * b + 4, t, 0, :])
            for fc in range(FC):
                dve.wait_ge(sb_mm, fc + 1)
                b = 2 * (fc % 2)
                if fc == 0:
                    dve.wait_ge(tok_ready, 4)
                for q, dst in ((0, AAB), (1, ARB)):
                    for t in range(TT):
                        u = t * H + 2 * fc
                        last = V.tensor_tensor(dst[:, u:u + 2, :], PS[:, b:b + 2, t * 256 + q * P:t * 256 + (q + 1) * P],
                                               upto[:, q:q + 1, :].broadcast_to([P, 2, P]), ALU.mult)
                last.then_inc(sb_ok, 1)

            def mask_k(t, j):
                n = FC // 2 * t + j
                dve.wait_ge(sk_mm, n + 1)
                if n >= 2:
                    dve.wait_ge(xo_mm, n - 1)
                for f in range(2):
                    last = V.tensor_tensor(SK[j % 2][:, f], PS[:, 2:4, f * 256:(f + 1) * 256],
                                           upto[:].rearrange("p (o a) b -> p o (a b)", o=1).broadcast_to([P, 2, 2 * P]), ALU.mult)
                last.then_inc(sk_ok, 1)

            for t in range(TT):
                for j in range(FC // 2):
                    mask_k(t, j)
                if t == 0:
                    dve.wait_ge(diag_in, 64)
                    dve.wait_ge(ti_init, 1)
                    for s in range(31):
                        w = 31 - s
                        prod = at(22, 1 + s, w)
                        link(V.tensor_tensor(prod, TTi[:, 0:s + 1, s:s + 1].broadcast_to([P, s + 1, w]), DT[:, s:s + 1, s + 1:32].broadcast_to([P, s + 1, w]), ALU.mult))
                        last = V.tensor_tensor(TTi[:, 0:s + 1, s + 1:32], TTi[:, 0:s + 1, s + 1:32], prod, ALU.add)
                        if s < 30:
                            link(last)
                    last.then_inc(inv_ok, 1)
                for i in range(4):
                    n = 4 * t + i
                    rows = slice(32 * i, 32 * i + 32)
                    if i == 0:
                        dve.wait_ge(xo_mm, FC // 2 * (t + 1))
                    if n >= 1:
                        dve.wait_ge(xacc_mm, n)
                    V.tensor_copy(acc[rows, 1, :], PS[rows, 1, :]).then_inc(acc_dve, 1)
                    dve.wait_ge(ub_mm, n + 1)
                    V.tensor_copy(U[rows, 1, :], PS[rows, 3, :]).then_inc(u_dve, 1)
                if t == 0:
                    dve.wait_ge(st_mm, 1)
                    V.tensor_tensor(S0T, PS[:, 2, :].rearrange("p (f d) -> p f d", f=FC), edec[:].rearrange("p (f o) -> p f o", o=1).broadcast_to([P, FC, HD]), ALU.mult).then_inc(s0_ok, 1)

            dve.wait_ge(o_ok, 2)
            dve.wait_ge(lnx_in, 32)
            link(V.tensor_reduce(hs[:, 0, :], heads(o_), AX.X, ALU.add))
            link(V.tensor_scalar(hs[:, 0, :], hs[:, 0, :], -1.0 / HD, None, ALU.mult))
            link(V.tensor_tensor(heads(o_), heads(o_), per_head(hs[:, 0, :]), ALU.add))
            link(V.tensor_tensor(lnsq, o_, o_, ALU.mult))
            link(V.tensor_reduce(hs[:, 2, :], heads(lnsq), AX.X, ALU.add))
            link(V.tensor_scalar(hs[:, 2, :], hs[:, 2, :], 1.0 / HD, LNX_EPS, ALU.mult, ALU.add))
            V.reciprocal(hs[:, 2, :], hs[:, 2, :]).then_inc(lvar_ready, 1)
            link(V.tensor_tensor(heads(lnsq), heads(v_), per_head(bonus[:]), ALU.mult))
            dve.wait_ge(lstd_ok, 1)
            link(V.tensor_tensor(heads(o_), heads(o_), per_head(hs[:, 3, :]), ALU.mult))
            link(V.tensor_tensor(o_, o_, both(mt[:, 0, :]), ALU.mult))
            link(V.tensor_tensor(o_, o_, both(mt[:, 1, :]), ALU.add))
            link(V.tensor_tensor(o_, o_, lnsq, ALU.add))
            for t in range(TT):
                last = V.tensor_tensor(hperm(t), o_[:, t, :].rearrange("p (q k) -> p q k", k=KC), g_[:, t, :].rearrange("p (q k) -> p q k", k=KC), ALU.mult)
            last.then_inc(h_ready, 1)
            turn(5, hdst)
            post(0)

            def moe(layer, s, t_set):
                pre(s, t_set)
                sc, biased, rest, mask, chosen, gates = (rt[:, i] for i in range(6))
                dve.wait_ge(sc_ok, 2 * layer + 1)
                link(V.tensor_tensor(biased, sc, rb[:, layer:layer + 1, :].broadcast_to([P, TT, E]), ALU.add))
                for t in range(TT):
                    link(V.max(top8[:, t, :], biased[:, t, :]))
                    link(V.match_replace(rest[:, t, :], top8[:, t, :], biased[:, t, :], -1e30))
                link(V.tensor_tensor(mask, biased, rest, ALU.not_equal))
                link(V.tensor_tensor(chosen, sc, mask, ALU.mult))
                link(V.tensor_reduce(rsum[:, 0, :], chosen, AX.X, ALU.add))
                link(V.reciprocal(rsum[:, 1, :], rsum[:, 0, :]))
                for t in range(TT):
                    last = V.tensor_scalar(gates[:, t, :], chosen[:, t, :], rsum[:, 1, t:t + 1], ROUTED_SCALE, ALU.mult, ALU.mult)
                last.then_inc(sc_ok, 1)
                base = UNITS * layer
                dve.wait_ge(sc_ok, 2 * layer + 2)

                def hidden(off, n, gate):
                    t = n % 2
                    dve.wait_ge(silu_ok, off + (base + n + 1))
                    if not (isinstance(off, int) and n < 2 and layer == 0):
                        dve.wait_ge(hidT_mm, off + (base + n - 1))
                    V.scalar_tensor_tensor(out=actp[:, t].rearrange("p c q -> p q c"), in0=PS[:, 4 + t, F:2 * F].rearrange("p (q c) -> p q c", c=FK), scalar=gate,
                                           in1=gsil[:, t, :].rearrange("p (q c) -> p q c", c=FK), op0=ALU.mult, op1=ALU.mult).then_inc(hid_ok, 1)

                hidden(0, 0, 1.0)
                hidden(0, 1, 1.0)
                with dve.Fori(0, E // 4) as j:
                    for q in range(8):
                        hidden(j * 8, 2 + q, gates[:, q % 2, bass.ds(j * 4 + q // 2, 1)])
                post(s)

            if STOP >= 2:
                moe(0, 1, 6)

            if STOP >= 3:
                pre(2, 7)
                for n in (8, 9):
                    turn(n, (lambda o: lambda t, b: qkT[:, o + 4 * b:o + 4 * b + 4, t * P:(t + 1) * P])((n - 8) * FC))

                def take_z(g):
                    dve.wait_ge(z_mm, g + 1)
                    if g >= 2:
                        dve.wait_ge(w_ok, g - 1)
                    V.tensor_tensor(zsb[g % 2], PS[:, 0:4, 0:384], zmask[:].rearrange("p (o c) -> p o c", o=1).broadcast_to([P, 4, 384]), ALU.add).then_inc(z_ok, 1)

                def softplus(g):
                    dve.wait_ge(l_ok, g + 1)
                    V.scalar_tensor_tensor(out=spb[g % 2], in0=zsb[g % 2], scalar=0.0, in1=spb[g % 2], op0=ALU.max, op1=ALU.add).then_inc(sp_ok, 1)

                def log_weights(g):
                    dve.wait_ge(rc_mm, g + 1)
                    V.tensor_tensor(zsb[g % 2], zsb[g % 2], PS[:, 4:8, 0:384], ALU.subtract).then_inc(ez_ok, 1)

                def take_o(g):
                    dve.wait_ge(pv_mm, g + 1)
                    for t in range(TT):
                        dst = h[:, t, :].rearrange("p (k j q) -> p j q k", k=KC, j=H)[:, 4 * g:4 * g + 4]
                        last = V.tensor_copy(dst, PS[:, 0:4, 384 + t * HD:384 + (t + 1) * HD].rearrange("p j (q k) -> p j q k", k=KC))
                    last.then_inc(o_taken if g < 3 else h_ready, 1)

                take_z(0)
                softplus(0)
                for g in range(4):
                    if g + 1 < 4:
                        take_z(g + 1)
                    log_weights(g)
                    if g + 1 < 4:
                        softplus(g + 1)
                    take_o(g)
                turn(10, hdst)
                post(2)
            if STOP >= 4:
                moe(1, 3, 11)


_IN = ['x', 'c', 'ada_w', 'ada_b', 'norm_pre_mix', 'norm_post_mix', 'norm_pre_ffn', 'norm_post_ffn', 'rwkv_mu', 'rwkv_w_rkv',
       'rwkv_w_w1', 'rwkv_w_w2', 'rwkv_w0', 'rwkv_w_a1', 'rwkv_w_a2', 'rwkv_a0', 'rwkv_w_g1', 'rwkv_w_g2', 'rwkv_k_k',
       'rwkv_k_a', 'rwkv_r_k', 'rwkv_lnx_g', 'rwkv_lnx_b', 'rwkv_w_o', 'sb_w_qkv', 'sb_w_o', 'moe_w_router',
       'moe_router_bias', 'moe_w_gate', 'moe_w_up', 'moe_w_down', 'moe_ws_gate', 'moe_ws_up', 'moe_ws_down']


def kernel(**inputs):
    import numpy as np
    import concourse.bacc as bacc
    from concourse.bass_utils import run_bass_kernel_spmd

    nc = bacc.Bacc("TRN2", target_bir_lowering=False, num_devices=1)
    arrays, aps = {}, {}
    for name in _IN:
        v = np.ascontiguousarray(inputs[name])
        arrays[f"in_{name}"] = v
        aps[name] = nc.dram_tensor(f"in_{name}", v.shape, mybir.dt.from_np(v.dtype), kind="ExternalInput").ap()
    out = nc.dram_tensor("out", inputs["x"].shape, F32, kind="ExternalOutput").ap()
    hybrid_trunk(nc, aps, out)
    r = run_bass_kernel_spmd(nc, [arrays], core_ids=[0])
    return r.results[0]["out"]
```

```python
from contextlib import ExitStack
import math

import concourse.bass as bass
from concourse import mybir

F32 = mybir.dt.float32
BF16 = mybir.dt.bfloat16
I32 = mybir.dt.int32
ALU = mybir.AluOpType
ACT = mybir.ActivationFunctionType
AX = mybir.AxisListType

P = 128
STOP = 4


def hybrid_trunk(nc, a, out):
    _, S, D = a["x"].shape
    TT = S // P
    KC = D // P
    HD = a["rwkv_r_k"].shape[2]
    H = D // HD
    FC = D // P
    E = a["moe_w_gate"].shape[1]
    F = a["moe_w_gate"].shape[3]
    FK = F // P
    LW, LA, LG = a["rwkv_w_w1"].shape[2], a["rwkv_w_a1"].shape[2], a["rwkv_w_g1"].shape[2]
    NB = 512
    HB = D // NB
    TOPK = 8
    ROUTED_SCALE = 2.5
    RMS_EPS, LNX_EPS = 1e-6, 64e-5
    DECAY = math.exp(-0.5)
    W = 64
    NW = S // W - 1
    MAXWIN = S // W + 1
    LIST = 48
    R0 = E // 4
    NADA = a["ada_w"].shape[2] // NB
    assert TT == 2 and KC == 8 and HD == 64 and F == 256 and NADA == 12

    with ExitStack() as ctx:
        def sb(name, shape):
            return ctx.enter_context(nc.sbuf_tensor(name, shape, F32))

        def sem(name):
            return ctx.enter_context(nc.semaphore(name))

        PS = ctx.enter_context(nc.psum_tensor("PS", [P, 8, NB], F32))

        x = sb("x", [P, TT, D])
        mt = sb("mt", [P, 5, D])
        h = sb("h", [P, TT, D])
        hT = sb("hT", [P, KC, S + 1])
        ident = sb("ident", [P, P])
        upto = sb("upto", [P, 2, P])
        cumx = sb("cumx", [P, 2, P])
        fromj = sb("fromj", [P, P])
        ones = sb("ones", [P, P])
        halves = sb("halves", [P, 2])
        sel = sb("sel", [P, 1])
        ccol = sb("ccol", [P, KC])
        crep = sb("crep", [P, KC, 32])
        adab, apart, arow = mt[0:2 * NADA, 4, 0:NB], mt[:, 4, NB:2 * NB], mt[0:1, 3, :].rearrange("p (b c) -> p b c", b=2)
        mu = sb("mu", [P, 6, KC])
        ss = sb("ss", [P, 8, TT])
        ms = sb("ms", [P, 8, TT])
        rstd = sb("rstd", [P, 8, TT])
        hs = sb("hs", [P, 4, TT * H])
        bonus = sb("bonus", [P, TT * H])
        edec = sb("edec", [P, FC])
        top8 = sb("top8", [P, TT, TOPK])
        rsum = sb("rsum", [P, 2, TT])
        place = sb("place", [P, MAXWIN * W])
        efl = sb("efl", [E, 3, NW])
        ecol = sb("ecol", [E, 1])
        wcol = sb("wcol", [E, NW])
        lrow = sb("lrow", [1, 16])
        lists = ctx.enter_context(nc.sbuf_tensor("lists", [1, 2, LIST], I32))
        rounds = ctx.enter_context(nc.sbuf_tensor("rounds", [1, 1], I32))
        AK = 156
        arena = sb("arena", [P, AK * 256])

        def at(kib, *dims):
            n = 1
            for d in dims:
                n *= d
            v = arena[:, int(kib * 256):int(kib * 256) + n]
            names = "abcd"[:len(dims)]
            if len(dims) == 1:
                return v
            return v.rearrange(f"p ({' '.join(names)}) -> p {' '.join(names)}", **dict(zip(names, dims)))

        def slot(s, *dims):
            return at(24 * s, *dims)

        xs = [at(16, KC, S), at(40, KC, S)]
        xx = at(64, KC, S)
        w1w, w1a, w1g = at(72, KC, LW), at(74, KC, LA), at(76, KC, LG)
        w2w, w2a, w2g = at(80, D), at(84, D), at(88, D)
        t1 = at(92, 3, S)
        r_, k_, v_, g_, a_, sig = (at(96 + 8 * i, TT, D) for i in range(6))
        kkrow, karow, rkrow = at(144, D), at(148, D), at(152, D)
        ART = at(48, FC, TT, 2, P)
        bT, kT = at(64, FC, S), at(72, FC, S)
        tmpX, tmpY = at(80, TT, D), at(88, TT, D)
        ARB = at(80, TT * H, P)
        AAB = at(136, TT * H, P)
        AAB_end = 152
        TB = at(18, TT * H, 32)
        U = at(42, 2, NB)
        S0T = at(46, FC, HD)
        acc = at(152, 2, NB)
        DT = h[:, 0, :].rearrange("p (s t) -> p s t", s=32)
        TTi = h[:, 1, :].rearrange("p (s t) -> p s t", s=32)
        SK = [mt[:, 2 - i, :].rearrange("p (f q c) -> p f q c", f=2, q=2) for i in range(2)]
        o_ = r_
        lnsq = at(48, TT, D)
        qkv = at(96, TT, 3 * D)
        qkT = at(120, 2 * FC, S)
        zsb = [at(136, 4, 384), at(142, 4, 384)]
        spb = [at(148, 4, 384), mt[:, 0:2, :].rearrange("p a b -> p (a b)")[:, 0:1536].rearrange("p (a b) -> p a b", a=4)]
        posm = at(107, TT, E)
        def half_at(kib, *dims):
            n = 1
            for d in dims:
                n *= d
            v = arena[:, int(kib * 256):int(kib * 256) + n // 2].bitcast(BF16)
            names = "abcd"[:len(dims)]
            return v.rearrange(f"p ({' '.join(names)}) -> p {' '.join(names)}", **dict(zip(names, dims)))
        hpart = [half_at(108 + 4 * i, TT, D) for i in range(3)]
        hrest = at(120, TT, D)
        xg = [at(128 + 4 * i, KC, 2 * W) for i in range(2)]
        pick = [half_at(136 + i / 2, TT, 2 * W) for i in range(2)]
        wpick = [at(137 + i, TT, 2 * W) for i in range(2)]
        wpickT = at(139, TT, P)
        ye = at(140, D)
        hidp = at(144, FK, P)
        hidT = at(145, FK, P)
        sg = at(146, F)
        gsil = at(96, TT, F)
        actp = at(98, TT, FK, P)
        actT = at(100, TT, FK, P)
        rt = at(102, 6, TT, E)
        rw = at(105, KC, E)
        rb = at(148, 1, E)
        hit = at(147, NW, LIST)[0:E]
        zmask = mt[:, 1, NB:NB + 384]

        mod_dram = nc.dram_tensor("mod_rows", [2 * NADA, NB], F32, kind="Internal").ap()
        diag_dram = nc.dram_tensor("diag_blocks", [4, 32, TT * H, 32], F32, kind="Internal").ap()
        inv_dram = nc.dram_tensor("inverse_blocks", [4, TT * H, 32, 32], F32, kind="Internal").ap()

        ring_in = [sem(f"ring_in{i}") for i in range(4)]
        ring2_in = [sem(f"ring2_in{i}") for i in range(4)]
        moe_sems = [{n: sem(f"{n}{l}") for n in ("pick_ok", "gather_mm", "xg_act", "xg_dve", "gateup_mm", "sg_ok", "hidp_ok", "wpickT_mm", "wpickT_ok",
                                                 "hidpT_mm", "hidT2_ok", "y_mm", "ye_act", "ye_dve")} for l in range(2)]
        hb_ok = sem("hb_ok"); hb_half = sem("hb_half"); hr_ok = sem("hr_ok"); mask_ok = sem("mask_ok"); pos_mm = sem("pos_mm"); flag_ok = sem("flag_ok"); idx_mm = sem("idx_mm"); hit_ok = sem("hit_ok")
        list_mm = sem("list_mm"); list_ok = sem("list_ok"); moe_done = sem("moe_done")
        x_in = sem("x_in"); router_in = sem("router_in"); small_in = sem("small_in"); lora_in = sem("lora_in"); rows_in = sem("rows_in")
        mpre_in = sem("mpre_in"); mpost_in = sem("mpost_in"); lnx_in = sem("lnx_in")
        const_ok = sem("const_ok"); pool_step = sem("pool_step"); crep_ok = sem("crep_ok"); triA_ok = sem("triA_ok")
        ada_mm = sem("ada_mm"); ada_part = sem("ada_part"); ada_row_mm = sem("ada_row_mm"); ada_row = sem("ada_row")
        mod_stored = [sem("mod_stored0"), sem("mod_stored1")]
        ss_ready = sem("ss_ready"); ms_ready = sem("ms_ready"); rstd_ready = sem("rstd_ready")
        h_ready = sem("h_ready"); x_ready = sem("x_ready")
        tr_mm = sem("tr_mm"); tr_act = sem("tr_act"); tr_dve = sem("tr_dve")
        xs_ready = sem("xs_ready"); lora1_mm = sem("lora1_mm"); lora1_ok = sem("lora1_ok")
        lora2_mm = sem("lora2_mm"); lora2_ok = sem("lora2_ok")
        proj_mm = sem("proj_mm"); proj_ok = sem("proj_ok")
        cum_mm = sem("cum_mm"); decay_ok = sem("decay_ok"); kss_ready = sem("kss_ready"); knorm_ok = sem("knorm_ok")
        xy_free = sem("xy_free"); tok_ready = sem("tok_ready")
        sb_mm = sem("sb_mm"); sb_ok = sem("sb_ok"); sk_mm = sem("sk_mm"); sk_ok = sem("sk_ok"); xo_mm = sem("xo_mm")
        diag_out = sem("diag_out"); diag_in = sem("diag_in"); ti_init = sem("ti_init"); inv_ok = sem("inv_ok"); inv_out = sem("inv_out"); inv_in = sem("inv_in")
        xacc_mm = sem("xacc_mm"); acc_act = sem("acc_act"); acc_dve = sem("acc_dve"); ub_mm = sem("ub_mm"); u_act = sem("u_act"); u_dve = sem("u_dve")
        o_mm = sem("o_mm"); o_ok = sem("o_ok"); st_mm = sem("st_mm"); s0_ok = sem("s0_ok")
        lvar_ready = sem("lvar_ready"); lstd_ok = sem("lstd_ok")
        ccol_ok = sem("ccol_ok"); o_taken = sem("o_taken"); z_mm = sem("z_mm"); z_ok = sem("z_ok"); l_ok = sem("l_ok"); sp_ok = sem("sp_ok"); rc_mm = sem("rc_mm"); ez_ok = sem("ez_ok"); w_ok = sem("w_ok"); pv_mm = sem("pv_mm")
        log_mm = sem("log_mm"); sc_ok = sem("sc_ok"); gates_ok = sem("gates_ok")
        gu_mm = sem("gu_mm"); silu_ok = sem("silu_ok"); hid_ok = sem("hid_ok"); hidT_mm = sem("hidT_mm"); hidT_ok = sem("hidT_ok"); down_mm = sem("down_mm")
        dve_step = sem("dve_step"); act_step = sem("act_step"); x_out = sem("x_out")

        x_d = a["x"].rearrange("b (t p) d -> p (b t) d", p=P)
        out_d = out.rearrange("b (t p) d -> p (b t) d", p=P)

        def tile_of(w, block):
            return w.rearrange("(p k) n -> p k n", k=KC)[:, :, block * NB:(block + 1) * NB]

        def row_on_all(v, n):
            return v.rearrange("(o n) -> o n", o=1).broadcast_to([P, n])

        ring, arrivals = [], [0] * 4

        def ring_item(s, copies, free):
            arrivals[s] += 16 * len(copies)
            ring.append((s, copies, free))
            return s, arrivals[s]

        def ada_copy(s, i):
            return [(slot(s, KC, NB), tile_of(a["ada_w"][i // NADA], i % NADA))]

        def expert_copies(s, gate, up, down):
            half = KC * F
            base = slot(s, 2 * half + FK * D)
            return [(base[:, 0:half], gate.rearrange("(p k) f -> p (k f)", k=KC)),
                    (base[:, half:2 * half], up.rearrange("(p k) f -> p (k f)", k=KC)),
                    (base[:, 2 * half:], down.rearrange("(p c) d -> p (c d)", c=FK))]

        ada_at, proj_at = {}, {}
        for i, s in zip(range(4), (0, 1, 2, 0)):
            ada_at[i] = ring_item(s, ada_copy(s, i), [(ada_mm, 1)] if i == 3 else [])
        for j, s in enumerate((1, 2, 0, 1, 2, 0)):
            free = (ada_mm, (2, 3, 4)[j]) if j < 3 else (proj_mm, j - 2)
            proj_at[j] = ring_item(s, [(slot(s, KC, NB), tile_of(a["rwkv_w_rkv"][0, j // HB], j % HB))], [free])
        for i in range(4, 2 * NADA):
            s = 1 - i % 2
            free = (proj_mm, i) if i == 4 else (proj_mm, 6) if i == 5 else (ada_mm, i - 1)
            ada_at[i] = ring_item(s, ada_copy(s, i), [free])
        for j in range(HB):
            s = 1 - j
            proj_at[6 + j] = ring_item(s, [(slot(s, KC, NB), tile_of(a["rwkv_w_o"][0], j))], [(ada_mm, 23 + j)])

        UNITS = TT
        base_in = {0: list(arrivals)}
        arrivals = [0] * 4
        ring2_start = len(ring)
        qslots = (3, 0, 1, 2, 3, 0)
        for j, s in enumerate(qslots):
            free = [(moe_done, 1)] if j < 4 else [(proj_mm, 8 + j - 4 + 1)]
            proj_at[8 + j] = ring_item(s, [(slot(s, KC, NB), tile_of(a["sb_w_qkv"][0], j))], free)
        for j, s in enumerate((1, 2)):
            proj_at[14 + j] = ring_item(s, [(slot(s, KC, NB), tile_of(a["sb_w_o"][0], j))], [(proj_mm, 8 + 2 + j + 1)])
        base_in[1] = list(arrivals)

        block = ctx.enter_context(nc.Block())

        @block.sync
        def _(sp):
            def run(items, arrive):
                for s, copies, free in items:
                    for sm, v in free:
                        sp.wait_ge(sm, v)
                    for dst, src in copies:
                        sp.dma_start(dst, src).then_inc(arrive[s], 16)

            def moe(layer):
                arrive = (ring_in, ring2_in)[layer]
                y_mm = moe_sems[layer]["y_mm"]
                first = 2 if layer == 0 else 3
                if layer == 0:
                    sp.wait_ge(h_ready, 2)
                else:
                    sp.wait_ge(proj_mm, 13)
                for dst, src in expert_copies(first, a["moe_ws_gate"][layer], a["moe_ws_up"][layer], a["moe_ws_down"][layer]):
                    sp.dma_start(dst, src).then_inc(arrive[first], 16)

                def expert(e, s):
                    for dst, src in expert_copies(s, a["moe_w_gate"][layer, e], a["moe_w_up"][layer, e], a["moe_w_down"][layer, e]):
                        sp.dma_start(dst, src).then_inc(arrive[s], 16)

                def expert_at_register(e, s):
                    half = KC * F
                    base = slot(s, 2 * half + FK * D)
                    for lo, hi, w in ((0, half, "moe_w_gate"), (half, 2 * half, "moe_w_up"), (2 * half, 2 * half + FK * D, "moe_w_down")):
                        src = a[w][layer].rearrange("e (p k) f -> p e (k f)", p=P)[:, bass.ds(e, 1), :]
                        sp.dma_start(base[:, lo:hi].rearrange("p (o f) -> p o f", o=1), src).then_inc(arrive[s], 16)

                if layer == 0:
                    waits = [(proj_mm, 6), (proj_mm, 8), (proj_mm, 7)]
                else:
                    waits = [(proj_mm, 14), (proj_mm, 15), (proj_mm, 16)]
                for e in range(3):
                    sp.wait_ge(*waits[e])
                    expert(e, (first + 1 + e) % 4)
                sp.wait_ge(down_mm, UNITS * (layer + 1))
                expert(3, first)
                with sp.Fori(1, R0) as j:
                    for q in range(4):
                        sp.wait_ge(y_mm, j * 4 + (2 * (q // 2) - 2))
                        expert_at_register(sp.snap(j * 4 + q), (first + 1 + q) % 4)
                sp.wait_ge(list_ok, layer + 1)
                end = sp.value_load(rounds[0:1, 0:1], min_val=R0 + 1, max_val=R0 + LIST // 4 - 3)
                with sp.Fori(R0, end) as j:
                    for q in range(4):
                        e = sp.value_load(lists[0:1, 0, bass.ds(j * 4 + (q - E), 1)], min_val=0, max_val=E - 1)
                        sp.wait_ge(y_mm, j * 4 + (2 * (q // 2) - 2))
                        expert_at_register(e, (first + 1 + q) % 4)

            sp.dma_start(x[:], x_d).then_inc(x_in, 16)
            run(ring[:ring2_start], ring_in)
            if STOP >= 2:
                moe(0)
            if STOP >= 3:
                run(ring[ring2_start:], ring2_in)
            if STOP >= 4:
                moe(1)
            sp.wait_ge(x_ready, STOP)
            sp.dma_start(out_d, x[:]).then_inc(x_out, 16)
            sp.wait_ge(x_out, 16)

        @block.gpsimd
        def _(pool):
            steps = [0]

            def link(ins):
                steps[0] += 1
                ins.then_inc(pool_step, 1)
                pool.wait_ge(pool_step, steps[0])

            pool.dma_start(ccol[:], a["c"].rearrange("b (p k) -> p (b k)", k=KC)).then_inc(small_in, 16)
            pool.dma_start(adab, a["ada_b"].rearrange("l (n c) -> (l n) c", c=NB)).then_inc(small_in, 16)
            pool.dma_start(mu[:], a["rwkv_mu"][0].rearrange("n (p k) -> p n k", k=KC)).then_inc(small_in, 16)
            for dst, src in ((w1w, a["rwkv_w_w1"]), (w1a, a["rwkv_w_a1"]), (w1g, a["rwkv_w_g1"])):
                pool.dma_start(dst, src[0].rearrange("(p k) n -> p k n", k=KC)).then_inc(lora_in, 16)
            pool.dma_start(w2w[0:LW], a["rwkv_w_w2"][0]).then_inc(lora_in, 16)
            pool.dma_start(w2w[LW:LW + 1], a["rwkv_w0"]).then_inc(lora_in, 16)
            pool.dma_start(w2a[0:LA], a["rwkv_w_a2"][0]).then_inc(lora_in, 16)
            pool.dma_start(w2a[LA:LA + 1], a["rwkv_a0"]).then_inc(lora_in, 16)
            pool.dma_start(w2g, a["rwkv_w_g2"][0]).then_inc(lora_in, 16)
            for dst, n in ((kkrow, "rwkv_k_k"), (karow, "rwkv_k_a")):
                pool.dma_start(dst, row_on_all(a[n][0], D)).then_inc(rows_in, 16)
            pool.dma_start(rkrow, row_on_all(a["rwkv_r_k"][0].rearrange("h d -> (h d)"), D)).then_inc(rows_in, 16)

            g = nc.gpsimd
            link(g.memset(sel[:], 0.0))
            link(g.memset(ident[:], 0.0))
            link(g.memset(ones[:], 1.0))
            link(g.iota(place[:], pattern=[[1, MAXWIN * W]], base=1, channel_multiplier=0, allow_small_or_imprecise_dtypes=True))
            link(g.iota(ecol[:], pattern=[[0, 1]], base=0, channel_multiplier=1, allow_small_or_imprecise_dtypes=True))
            for w in range(NW):
                link(g.memset(wcol[:, w:w + 1], float(W * (w + 1) - W * (MAXWIN - 1))))
            link(g.memset(halves[:], 0.0))
            link(g.memset(hT[:, :, 0:1], 0.0))
            link(g.memset(t1[64:65, 0:2, :], 1.0))
            link(g.memset(upto[:], 1.0))
            for q in range(4):
                link(g.memset(sel[32 * q:32 * q + 1, :], 1.0))
            link(g.memset(halves[64:128, 0:1], 1.0))
            link(g.memset(halves[0:64, 1:2], 1.0))
            link(g.affine_select(out=ident[:], in_=ident[:], compare_op=ALU.not_equal, fill=1.0, base=0, pattern=[[-1, P]], channel_multiplier=1))
            link(g.affine_select(out=upto[:, 0, :], in_=upto[:, 0, :], compare_op=ALU.is_ge, fill=0.0, base=-1, pattern=[[1, P]], channel_multiplier=-1))
            link(g.affine_select(out=upto[:, 1, :], in_=upto[:, 1, :], compare_op=ALU.is_ge, fill=0.0, base=0, pattern=[[1, P]], channel_multiplier=-1))
            g.affine_select(out=fromj[:], in_=ones[:], compare_op=ALU.is_ge, fill=0.0, base=0, pattern=[[-1, P]], channel_multiplier=1).then_inc(const_ok, 1)

            def load_pre(s):
                l, off = s // 2, NADA // 2 * (s % 2) + NADA * (s // 2)
                gain = "norm_pre_mix" if s % 2 == 0 else "norm_pre_ffn"
                pool.wait_ge(mod_stored[1], 16 * ((off + 3) // 2 + 1))
                pool.wait_ge(mod_stored[0], 16 * ((off + 2) // 2 + 1))
                flat = mod_dram.rearrange("a b -> (a b)")
                pool.dma_start(mt[:, 0, :], row_on_all(flat[off * NB:(off + 2) * NB], D)).then_inc(mpre_in, 16)
                pool.dma_start(mt[:, 1, :], row_on_all(flat[(off + 2) * NB:(off + 4) * NB], D)).then_inc(mpre_in, 16)
                pool.dma_start(mt[:, 2, :], row_on_all(a[gain][l], D)).then_inc(mpre_in, 16)

            def load_post(s):
                l, off = s // 2, NADA // 2 * (s % 2) + NADA * (s // 2)
                gain = "norm_post_mix" if s % 2 == 0 else "norm_post_ffn"
                pool.wait_ge(mod_stored[1], 16 * ((off + 5) // 2 + 1))
                pool.wait_ge(mod_stored[0], 16 * ((off + 4) // 2 + 1))
                flat = mod_dram.rearrange("a b -> (a b)")
                pool.dma_start(mt[:, 3, :], row_on_all(flat[(off + 4) * NB:(off + 6) * NB], D)).then_inc(mpost_in, 16)
                pool.dma_start(mt[:, 4, :], row_on_all(a[gain][l], D)).then_inc(mpost_in, 16)

            load_pre(0)
            pool.wait_ge(h_ready, 1)
            pool.dma_start(mt[:, 0, :], row_on_all(a["rwkv_lnx_g"][0], D)).then_inc(lnx_in, 16)
            pool.wait_ge(sb_ok, FC)
            for i in range(4):
                pool.dma_start(diag_dram[i], AAB[32 * i:32 * i + 32, :, 32 * i:32 * i + 32]).then_inc(diag_out, 16)
            pool.wait_ge(diag_out, 64)
            pool.wait_ge(tr_mm, 20)
            for i in range(4):
                pool.dma_start(DT[32 * i:32 * i + 32], diag_dram[i].rearrange("s u t -> u s t")).then_inc(diag_in, 16)
            link(g.memset(TTi, 0.0))
            g.affine_select(out=TTi, in_=TTi, compare_op=ALU.not_equal, fill=1.0, base=0, pattern=[[1, 32], [-1, 32]], channel_multiplier=0).then_inc(ti_init, 1)
            pool.wait_ge(inv_ok, 1)
            pool.dma_start(inv_dram.rearrange("i u s t -> (i u) (s t)"), h[:, 1, :]).then_inc(inv_out, 16)
            pool.wait_ge(inv_out, 16)
            for i in range(4):
                pool.dma_start(TB[32 * i:32 * i + 32], inv_dram[i].rearrange("u s t -> s u t")).then_inc(inv_in, 16)
            pool.wait_ge(xo_mm, FC)
            pool.dma_start(mt[:, 1, :], row_on_all(a["rwkv_lnx_b"][0], D)).then_inc(lnx_in, 16)
            pool.wait_ge(mod_stored[1], 16 * NADA)
            pool.wait_ge(mod_stored[0], 16 * NADA)
            load_post(0)
            for s in range(1, STOP):
                pool.wait_ge(h_ready, (0, 2, 3, 5)[s])
                load_pre(s)
                pool.wait_ge(x_ready, s)
                if s % 2:
                    pool.dma_start(rw, a["moe_w_router"][s // 2].rearrange("(p k) e -> p k e", k=KC)).then_inc(router_in, 16)
                    pool.dma_start(rb[:, 0, :], row_on_all(a["moe_router_bias"][s // 2], E)).then_inc(router_in, 16)
                load_post(s)

        @block.tensor
        def _(pe):
            mm = nc.tensor.matmul

            def ada_mm_step(i):
                s, v = ada_at[i]
                pe.wait_ge(ring_in[s], v)
                if i >= 1:
                    pe.wait_ge(ada_part, i)
                w = slot(s, KC, NB)
                for j in range(2):
                    for q in range(4):
                        last = mm(PS[32 * q:32 * q + 32, 7, :], crep[:, 2 * q + j, :], w[:, 2 * q + j, :], start=(j == 0), stop=(j == 1))
                last.then_inc(ada_mm, 1)

            def ada_row_step(i):
                pe.wait_ge(ada_part, i + 1)
                if i >= 1:
                    pe.wait_ge(ada_row, i)
                mm(PS[0:1, 6, :], sel[:, 0:1], apart, start=True, stop=False)
                mm(PS[0:1, 6, :], ident[0:2 * NADA, i:i + 1], adab, start=False, stop=True).then_inc(ada_row_mm, 1)

            def ada(i):
                if i in ada_at:
                    ada_mm_step(i)
                if i - 1 in ada_at and i != 4:
                    ada_row_step(i - 1)

            def turn(n, src):
                for f in range(4):
                    fill = 4 * n + f
                    if fill >= 2:
                        pe.wait_ge(tr_act if fill % 2 == 0 else tr_dve, fill // 2)
                    for q in range(4):
                        last = nc.tensor.transpose(PS[:, 4 + f % 2, q * P:(q + 1) * P], src(f // 2, 4 * (f % 2) + q), ident[:])
                    last.then_inc(tr_mm, 1)

            def turned(n):
                pe.wait_ge(tr_act, 2 * (n + 1))
                pe.wait_ge(tr_dve, 2 * (n + 1))

            def hsrc(t, k):
                return h[:, t, k * P:(k + 1) * P]

            def proj(n, src, banks, free):
                s, v = proj_at[n]
                pe.wait_ge((ring_in if n < 8 else ring2_in)[s], v)
                for sm, val in free:
                    pe.wait_ge(sm, val)
                w = slot(s, KC, NB)
                for t in range(TT):
                    for k in range(KC):
                        last = mm(PS[:, banks[t], :], src(k, t), w[:, k, :], start=(k == 0), stop=(k == KC - 1))
                last.then_inc(proj_mm, 1)

            def hTsrc(k, t):
                return hT[:, k, 1 + t * P:1 + (t + 1) * P]

            def head(fc, p):
                return 2 * fc + p

            pe.wait_ge(const_ok, 1)
            pe.wait_ge(crep_ok, 1)
            for i in range(4):
                ada_mm_step(i)
                ada_row_step(i)

            pe.wait_ge(h_ready, 1)
            turn(0, hsrc)
            pe.wait_ge(lora_in, 16 * 8)
            for m, (w1, w2, n1, n2) in enumerate(((w1w, w2w, LW, LW + 1), (w1a, w2a, LA, LA + 1), (w1g, w2g, LG, LG))):
                pe.wait_ge(xs_ready, m + 1)
                if m:
                    pe.wait_ge(lora1_ok, m)
                else:
                    turned(0)
                for k in range(KC):
                    last = mm(PS[0:n1, 5, 0:S], w1[:, k, :], xs[m % 2][:, k, :], start=(k == 0), stop=(k == KC - 1))
                last.then_inc(lora1_mm, 1)
                pe.wait_ge(lora1_ok, m + 1)
                if m:
                    pe.wait_ge(lora2_ok, m)
                for t in range(TT):
                    for b in range(HB):
                        last = mm(PS[:, 2 * t + b, :], t1[0:n2, m, t * P:(t + 1) * P], w2[0:n2, b * NB:(b + 1) * NB], start=True, stop=True)
                last.then_inc(lora2_mm, 1)
            for m in range(3):
                pe.wait_ge(xs_ready, 4 + m)
                for b in range(HB):
                    n = HB * m + b
                    src = (lambda m: lambda k, t: xs[(3 + m) % 2][:, k, t * P:(t + 1) * P])(m)
                    proj(n, src, (2 * b, 2 * b + 1), [(lora2_ok, 3)] if n < 2 else [(proj_ok, n - 1)])

            for fc in range(FC):
                for t in range(TT):
                    last = mm(PS[:, 5, fc:fc + 1], sig[:, t, fc * P:(fc + 1) * P], halves[:, t:t + 1], start=(fc == 0 and t == 0), stop=(t == TT - 1), skip_group_check=True)
            last.then_inc(cum_mm, 1)
            pe.wait_ge(triA_ok, 1)
            for n in (1, 0):
                if n == 1:
                    pe.wait_ge(proj_ok, 6)
                else:
                    pe.wait_ge(decay_ok, 3)
                for t in range(TT):
                    for b in range(HB):
                        last = mm(PS[:, 2 * t + b, :], cumx[:, n, :], sig[:, t, b * NB:(b + 1) * NB], start=True, stop=True)
                last.then_inc(cum_mm, 1)
            ada(4)
            ada(5)
            for n, buf in ((1, a_), (2, k_), (3, r_), (4, h)):
                pe.wait_ge(tok_ready, n)
                if n == 1:
                    pe.wait_ge(decay_ok, 1)
                turn(n, (lambda b: lambda t, k: b[:, t, k * P:(k + 1) * P])(buf))
                ada(5 + n)
            turned(4)

            for fc in range(FC):
                if fc >= 2:
                    pe.wait_ge(sb_ok, fc - 1)
                else:
                    pe.wait_ge(decay_ok, 4)
                for t in range(TT):
                    for p in range(2):
                        last = mm(PS[:, 2 * (fc % 2) + p, t * 256:(t + 1) * 256], bT[64 * p:64 * p + 64, fc, t * P:(t + 1) * P],
                                  ART[64 * p:64 * p + 64, fc, t, :, :], start=(t == 0), stop=(t == 1), skip_group_check=True)
                last.then_inc(sb_mm, 1)
                if fc % 2:
                    ada(10 + fc // 2)

            FP = FC // 2

            def score_k(t, j):
                n = FP * t + j
                if j:
                    pe.wait_ge(sk_ok, n)
                for f in range(2):
                    fc = 2 * j + f
                    for p in range(2):
                        last = mm(PS[:, 2 + p, f * 256:(f + 1) * 256], kT[64 * p:64 * p + 64, fc, t * P:(t + 1) * P],
                                  ART[64 * p:64 * p + 64, fc, t, :, :], start=(f == 0), stop=True, skip_group_check=True)
                last.then_inc(sk_mm, 1)

            def score_v(t, j):
                n = FP * t + j
                pe.wait_ge(sk_ok, n + 1)
                for f in range(2):
                    fc = 2 * j + f
                    for p in range(2):
                        rhs = v_[:, t, head(fc, p) * HD:(head(fc, p) + 1) * HD]
                        mm(PS[:, p, fc * HD:(fc + 1) * HD], SK[j % 2][:, f, p, 0:P], rhs, start=(fc == 0), stop=False, skip_group_check=True)
                        last = mm(PS[:, 4 + p, fc * HD:(fc + 1) * HD], SK[j % 2][:, f, p, P:2 * P], rhs, start=(fc == 0), stop=False, skip_group_check=True)
                last.then_inc(xo_mm, 1)

            for t in range(TT):
                if t == 0:
                    pe.wait_ge(sb_ok, FC)
                else:
                    pe.wait_ge(o_ok, 1)
                    pe.wait_ge(s0_ok, 1)
                score_k(t, 0)
                for j in range(FP):
                    if j + 1 < FP:
                        score_k(t, j + 1)
                    score_v(t, j)
                for fc in range(FC) if t else ():
                    for p in range(2):
                        mm(PS[:, 4 + p, fc * HD:(fc + 1) * HD], ART[64 * p:64 * p + 64, fc, t, 1, :], S0T[64 * p:64 * p + 64, fc, :], start=False, stop=False, skip_group_check=True)
                        last = mm(PS[:, p, fc * HD:(fc + 1) * HD], ART[64 * p:64 * p + 64, fc, t, 0, :], S0T[64 * p:64 * p + 64, fc, :], start=False, stop=False, skip_group_check=True)
                if t == 0:
                    for i in range(14, 20):
                        ada(i)
                    pe.wait_ge(inv_in, 64)
                for i in range(4):
                    n = 4 * t + i
                    rows = slice(32 * i, 32 * i + 32)
                    if i:
                        pe.wait_ge(u_act, n)
                        pe.wait_ge(u_dve, n)
                        for fc in range(FC):
                            for p in range(2):
                                last = mm(PS[rows, p, fc * HD:(fc + 1) * HD], AAB[0:32 * i, t * H + head(fc, p), rows], U[0:32 * i, p, fc * HD:(fc + 1) * HD],
                                          start=False, stop=False, skip_group_check=True)
                        last.then_inc(xacc_mm, 1)
                    if i == 0 and t:
                        last.then_inc(xacc_mm, 1)
                    pe.wait_ge(acc_act, n + 1)
                    pe.wait_ge(acc_dve, n + 1)
                    for fc in range(FC):
                        for p in range(2):
                            last = mm(PS[rows, 2 + p, fc * HD:(fc + 1) * HD], TB[rows, t * H + head(fc, p), :], acc[rows, p, fc * HD:(fc + 1) * HD],
                                      start=(fc == 0), stop=True, skip_group_check=True)
                    last.then_inc(ub_mm, 1)
                    if t == 0:
                        ada(20 + i)
                pe.wait_ge(u_act, 4 * t + 4)
                pe.wait_ge(u_dve, 4 * t + 4)
                for fc in range(FC):
                    for p in range(2):
                        last = mm(PS[:, 4 + p, fc * HD:(fc + 1) * HD], ARB[:, t * H + head(fc, p), :], U[:, p, fc * HD:(fc + 1) * HD], start=False, stop=True, skip_group_check=True)
                last.then_inc(o_mm, 1)
                if t == 0:
                    for fc in range(FC):
                        for p in range(2):
                            cols = slice(head(fc, p) * HD, (head(fc, p) + 1) * HD)
                            mm(PS[64 * p:64 * p + 64, 2, fc * HD:(fc + 1) * HD], a_[:, 0, cols], U[:, p, fc * HD:(fc + 1) * HD], start=(fc == 0), stop=False, skip_group_check=True)
                            last = mm(PS[64 * p:64 * p + 64, 2, fc * HD:(fc + 1) * HD], k_[:, 0, cols], v_[:, 0, cols], start=False, stop=True, skip_group_check=True)
                    last.then_inc(st_mm, 1)
                    ada(24)

            def out_proj(n, t_set):
                turned(t_set)
                for j in range(HB):
                    proj(n + j, hTsrc, (j, 2 + j), [])

            pe.wait_ge(o_ok, 2)
            pe.wait_ge(h_ready, 2)
            turn(5, hsrc)
            out_proj(6, 5)

            def moe(layer, t_set):
                Q = moe_sems[layer]
                arrive = (ring_in, ring2_in)[layer]
                pe.wait_ge(h_ready, (3, 6)[layer])
                turn(t_set, hsrc)
                pe.wait_ge(router_in, 32 * (layer + 1))
                turned(t_set)
                for t in range(TT):
                    for k in range(KC):
                        last = mm(PS[:, 4, t * E:(t + 1) * E], hTsrc(k, t), rw[:, k, :], start=(t == 0 and k == 0), stop=(k == KC - 1), skip_group_check=True)
                last.then_inc(log_mm, 1)
                pe.wait_ge(sc_ok, layer + 1)
                first = (2, 3)[layer]
                half = KC * F
                got = list(base_in[layer])
                got[first] += 48
                base = UNITS * layer

                pe.wait_ge(arrive[first], got[first])
                w = slot(first, 2, KC, F)
                for t in range(TT):
                    for k in range(KC):
                        last = mm(PS[:, 4 + t, :], hTsrc(k, t), w[:, :, k, :], start=(k == 0), stop=(k == KC - 1))
                    last.then_inc(gu_mm, 1)
                for t in range(TT):
                    pe.wait_ge(hid_ok, base + t + 1)
                    for c in range(FK):
                        last = nc.tensor.transpose(PS[:, 6 + t, c * P:(c + 1) * P], actp[:, t, c, :], ident[:])
                    last.then_inc(hidT_mm, 1)
                w = slot(first, 2 * half + FK * D)[:, 2 * half:].rearrange("p (c d) -> p c d", c=FK)
                for t in range(TT):
                    pe.wait_ge(hidT_ok, base + t + 1)
                    for c in range(FK):
                        for b in range(HB):
                            last = mm(PS[:, 2 * t + b, :], actT[:, t, c, :], w[:, c, b * NB:(b + 1) * NB], start=(c == 0), stop=False, skip_group_check=True)
                    last.then_inc(down_mm, 1)

                pe.wait_ge(mask_ok, layer + 1)
                mask = rt[:, 3]
                mm(PS[:, 4, 0:E], upto[:, 0, :], mask[:, 0, :], start=True, stop=True, skip_group_check=True)
                mm(PS[:, 4, E:2 * E], upto[:, 0, :], mask[:, 1, :], start=False, stop=False, skip_group_check=True)
                mm(PS[:, 4, E:2 * E], ones[:], mask[:, 0, :], start=False, stop=True, skip_group_check=True)
                mm(PS[0:E, 5, 0:1], mask[:, 0, :], ones[:, 0:1], start=True, stop=False)
                mm(PS[0:E, 5, 0:1], mask[:, 1, :], ones[:, 0:1], start=False, stop=True).then_inc(pos_mm, 1)
                pe.wait_ge(flag_ok, layer + 1)
                mm(PS[0:E, 6, 0:NW], upto[0:E, 0, 0:E], efl[:, 0, :], start=True, stop=False)
                mm(PS[0:E, 6, 0:NW], ones[0:E, 0:E], efl[:, 1, :], start=False, stop=True).then_inc(idx_mm, 1)
                pe.wait_ge(hit_ok, layer + 1)
                for n, col in ((0, lambda w: ecol[:]), (1, lambda w: wcol[:, w:w + 1])):
                    for w_ in range(NW):
                        mm(PS[0:1, 7, n * LIST:(n + 1) * LIST], col(w_), hit[:, w_, :], start=(n == 0 and w_ == 0), stop=(w_ == NW - 1), skip_group_check=True)
                mm(PS[0:1, 7, 2 * LIST:2 * LIST + NW], ones[0:E, 0:1], efl[:, 0, :], start=False, stop=True, skip_group_check=True).then_inc(list_mm, 1)

                def gather(i, f, par):
                    pe.wait_ge(Q["pick_ok"], i + 1)
                    if not (isinstance(i, int) and i == 0):
                        pe.wait_ge(Q["xg_dve"] if f else Q["xg_act"], i)
                    for kk in range(4):
                        k = 4 * f + kk
                        for n in range(3):
                            for t in range(TT):
                                last = mm(PS[:, 4 + f, kk * P:(kk + 1) * P], hpart[n][:, t, k * P:(k + 1) * P], pick[par][:, t, :],
                                          start=(n == 0 and t == 0), stop=(n == 2 and t == TT - 1), skip_group_check=True)
                    last.then_inc(Q["gather_mm"], 1)

                pe.wait_ge(hb_ok, layer + 1)
                gather(0, 0, 0)
                gather(0, 1, 0)
                pe.wait_ge(list_ok, layer + 1)
                end = pe.value_load(rounds[0:1, 0:1], min_val=R0 + 1, max_val=R0 + LIST // 4 - 3)

                def pair(j, q, peeled):
                    i = 2 * j + q if peeled else pe.snap(j * 2 + q)
                    slots = [(first + 1 + 2 * q + m) % 4 for m in range(2)]
                    for s in slots:
                        pe.wait_ge(arrive[s], j * 48 + (got[s] + 48))
                    pe.wait_ge(Q["xg_act"], i + 1)
                    pe.wait_ge(Q["xg_dve"], i + 1)
                    if not (peeled and i == 0):
                        pe.wait_ge(Q["ye_dve"], i)
                    ws = [slot(s, 2, KC, F) for s in slots]
                    for k in range(KC):
                        for m in range(2):
                            last = mm(PS[W * m:W * m + W, 6, :], xg[q][:, k, W * m:W * m + W], ws[m][:, :, k, :], start=(k == 0), stop=(k == KC - 1))
                    last.then_inc(Q["gateup_mm"], 1)
                    if not (peeled and i == 0):
                        pe.wait_ge(Q["ye_act"], i)
                    for t in range(TT):
                        last = nc.tensor.transpose(PS[:, 7, t * P:(t + 1) * P], wpick[q][:, t, :], ident[:])
                    last.then_inc(Q["wpickT_mm"], 1)
                    gather(i + 1, 0, 1 - q)
                    pe.wait_ge(Q["hidp_ok"], i + 1)
                    for c in range(FK):
                        last = nc.tensor.transpose(PS[:, 6, c * P:(c + 1) * P], hidp[:, c, :], ident[:])
                    last.then_inc(Q["hidpT_mm"], 1)
                    gather(i + 1, 1, 1 - q)
                    pe.wait_ge(Q["wpickT_ok"], i + 1)
                    pe.wait_ge(Q["hidT2_ok"], i + 1)
                    wd = [slot(s, 2 * half + FK * D)[:, 2 * half:].rearrange("p (c d) -> p c d", c=FK) for s in slots]
                    for b in range(HB):
                        for c in range(FK):
                            for m in range(2):
                                last = mm(PS[W * m:W * m + W, 7 - b, :], hidT[:, c, W * m:W * m + W], wd[m][:, c, b * NB:(b + 1) * NB], start=(c == 0), stop=(c == FK - 1))
                        last.then_inc(Q["y_mm"], 1)
                    for b in range(HB):
                        pe.wait_ge(Q["ye_dve"] if b else Q["ye_act"], i + 1)
                        for t in range(TT):
                            mm(PS[:, 2 * t + b, :], wpickT[:, t, :], ye[:, b * NB:(b + 1) * NB], start=False, stop=False, skip_group_check=True)

                pair(0, 0, True)
                pair(0, 1, True)
                with pe.Fori(1, end) as j:
                    pair(j, 0, False)
                    pair(j, 1, False)
                pe.wait_ge(Q["xg_act"], end * 2 + 1)
                nc.tensor.transpose(PS[:, 4, 0:P], ident[:], ident[:]).then_inc(moe_done, 1)

            if STOP >= 2:
                moe(0, 6)

            if STOP >= 3:
                pe.wait_ge(h_ready, 4)
                turn(7, hsrc)
                turned(7)
                for n in range(6):
                    proj(8 + n, hTsrc, (2 * (n % 2), 2 * (n % 2) + 1), [(proj_ok, 6 + n - 1)] if n >= 2 else [(x_ready, 2)])
                for n, part in ((8, 0), (9, 1)):
                    pe.wait_ge(proj_ok, 6 + 2 * (part + 1))
                    turn(n, (lambda q: lambda t, k: qkv[:, t, q * D + k * P:q * D + (k + 1) * P])(part))
                turned(9)
                pe.wait_ge(proj_ok, 12)

                def z_scores(g):
                    if g:
                        pe.wait_ge(z_ok, g)
                    if g >= 2:
                        pe.wait_ge(o_taken, g - 1)
                    for j in range(4):
                        fc, p = 2 * g + j // 2, j % 2
                        q, k = qkT[64 * p:64 * p + 64, fc, :], qkT[64 * p:64 * p + 64, FC + fc, :]
                        mm(PS[:, j, 0:S], k[:, 0:P], q, start=True, stop=True, skip_group_check=True)
                        last = mm(PS[:, j, S:S + P], k[:, P:S], q[:, P:S], start=False, stop=True, skip_group_check=True)
                    last.then_inc(z_mm, 1)

                def tail_sums(g):
                    pe.wait_ge(sp_ok, g + 1)
                    if g:
                        pe.wait_ge(ez_ok, g)
                    for j in range(4):
                        mm(PS[:, 4 + j, 0:384], fromj[:], spb[g % 2][:, j, :], start=True, stop=False, skip_group_check=True)
                        last = mm(PS[:, 4 + j, P:S], ones[:], spb[g % 2][:, j, S:384], start=False, stop=True, skip_group_check=True)
                    last.then_inc(rc_mm, 1)

                def weigh_v(g):
                    pe.wait_ge(w_ok, g + 1)
                    if g + 1 < 4:
                        pe.wait_ge(z_ok, g + 2)
                    for j in range(4):
                        hd = 4 * g + j
                        w = spb[g % 2][:, j, :]
                        v0, v1 = (qkv[:, t, 2 * D + hd * HD:2 * D + (hd + 1) * HD] for t in range(TT))
                        mm(PS[:, j, 384:384 + HD], w[:, 0:P], v0, start=True, stop=True, skip_group_check=True)
                        mm(PS[:, j, 384 + HD:NB], w[:, P:2 * P], v0, start=False, stop=False, skip_group_check=True)
                        last = mm(PS[:, j, 384 + HD:NB], w[:, 2 * P:384], v1, start=False, stop=True, skip_group_check=True)
                    last.then_inc(pv_mm, 1)

                z_scores(0)
                for g in range(4):
                    if g + 1 < 4:
                        z_scores(g + 1)
                    tail_sums(g)
                    weigh_v(g)
                pe.wait_ge(h_ready, 5)
                turn(10, hsrc)
                out_proj(14, 10)
            if STOP >= 4:
                moe(1, 11)

        @block.scalar
        def _(act):
            fn = nc.scalar.activation
            steps = [0]

            def link(ins):
                steps[0] += 1
                ins.then_inc(act_step, 1)
                act.wait_ge(act_step, steps[0])

            def copy(out_, in_):
                return fn(out_, in_, ACT.Copy)

            def ada_part_step(i):
                act.wait_ge(ada_mm, i + 1)
                if i >= 1:
                    act.wait_ge(ada_row_mm, i)
                copy(apart, PS[:, 7, :]).then_inc(ada_part, 1)

            def ada_row_step(i):
                act.wait_ge(ada_row_mm, i + 1)
                if i >= 2:
                    act.wait_ge(mod_stored[i % 2], 16 * (i // 2))
                copy(arow[:, i % 2, :], PS[0:1, 6, :]).then_inc(ada_row, 1)
                act.wait_ge(ada_row, i + 1)
                act.dma_start(mod_dram[i:i + 1, :], arow[:, i % 2, :]).then_inc(mod_stored[i % 2], 16)

            def ada(i):
                if i in ada_at:
                    ada_part_step(i)
                if i - 1 in ada_at and i != 4:
                    ada_row_step(i - 1)

            def rms(n, src):
                for t in range(TT):
                    fn(h[:, t, :], src(t), ACT.Square, accum_out=ss[:, n, t:t + 1]).then_inc(ss_ready, 1)
                act.wait_ge(ms_ready, n + 1)
                fn(rstd[:, n, :], ms[:, n, :], ACT.Sqrt).then_inc(rstd_ready, 1)

            def turn(n, dst):
                for t in range(TT):
                    act.wait_ge(tr_mm, 4 * n + 2 * t + 1)
                    copy(dst(t, 0), PS[:, 4, :].rearrange("p (k s) -> p k s", k=4)).then_inc(tr_act, 1)

            def hdst(t, b):
                return hT[:, 4 * b:4 * b + 4, 1 + t * P:1 + (t + 1) * P]

            def pre(s, t_set):
                if s:
                    act.wait_ge(x_ready, s)
                else:
                    act.wait_ge(x_in, 16)
                rms(2 * s, lambda t: x[:, t, :])
                turn(t_set, hdst)

            def post(s, y_done):
                act.wait_ge(*y_done)
                rms(2 * s + 1, lambda t: PS[:, 2 * t:2 * t + 2, :])

            act.wait_ge(small_in, 3 * 16)
            fn(ccol[:], ccol[:], ACT.Silu).then_inc(ccol_ok, 1)
            act.wait_ge(ccol_ok, 1)
            fn(crep[:], ccol[:].rearrange("p (k o) -> p k o", o=1).broadcast_to([P, KC, 32]), ACT.Copy).then_inc(crep_ok, 1)
            for i in range(4):
                ada_part_step(i)
                ada_row_step(i)

            pre(0, 0)
            for m, (dst, f1, f2, n1) in enumerate(((sig, ACT.Tanh, ACT.Sigmoid, LW), (a_, ACT.Copy, ACT.Sigmoid, LA), (g_, ACT.Sigmoid, ACT.Copy, LG))):
                act.wait_ge(lora1_mm, m + 1)
                fn(t1[0:n1, m, :], PS[0:n1, 5, 0:S], f1).then_inc(lora1_ok, 1)
                act.wait_ge(lora2_mm, m + 1)
                fn(dst.rearrange("p t (b c) -> p (t b) c", b=HB), PS[:, 0:4, :], f2).then_inc(lora2_ok, 1)
            for n in range(6):
                dst = (r_, k_, v_)[n // 2]
                b = n % 2
                act.wait_ge(proj_mm, n + 1)
                copy(dst[:, :, b * NB:(b + 1) * NB], PS[:, 2 * b:2 * b + 2, :]).then_inc(proj_ok, 1)
            act.wait_ge(cum_mm, 1)
            fn(edec[:], PS[:, 5, 0:FC], ACT.Exp, scale=-DECAY).then_inc(decay_ok, 1)
            act.wait_ge(kss_ready, 1)
            fn(hs[:, 1, :], hs[:, 0, :], ACT.Sqrt).then_inc(knorm_ok, 1)
            act.wait_ge(cum_mm, 2)
            act.wait_ge(xy_free, 1)
            sums = PS[:, 0:4, :]
            fn(tmpX.rearrange("p t (b c) -> p (t b) c", b=HB), sums, ACT.Exp, scale=DECAY).then_inc(decay_ok, 1)
            fn(tmpY.rearrange("p t (b c) -> p (t b) c", b=HB), sums, ACT.Exp, scale=-DECAY).then_inc(decay_ok, 1)
            act.wait_ge(cum_mm, 3)
            fn(sig.rearrange("p t (b c) -> p (t b) c", b=HB), sums, ACT.Exp, scale=-DECAY).then_inc(decay_ok, 1)
            ada(4)
            ada(5)
            for n, dst in ((1, lambda t, b: bT[:, 4 * b:4 * b + 4, t * P:(t + 1) * P]),
                           (2, lambda t, b: kT[:, 4 * b:4 * b + 4, t * P:(t + 1) * P]),
                           (3, lambda t, b: ART[:, 4 * b:4 * b + 4, t, 1, :]),
                           (4, lambda t, b: ART[:, 4 * b:4 * b + 4, t, 0, :])):
                turn(n, dst)
                ada(5 + n)
            for i in range(10, 20):
                ada(i)
            for t in range(TT):
                for i in range(4):
                    n = 4 * t + i
                    rows = slice(32 * i, 32 * i + 32)
                    if i == 0:
                        act.wait_ge(xo_mm, FC // 2 * (t + 1))
                    if n >= 1:
                        act.wait_ge(xacc_mm, n)
                    copy(acc[rows, 0, :], PS[rows, 0, :]).then_inc(acc_act, 1)
                    if t == 0 and i:
                        ada(20 + i - 1)
                    act.wait_ge(ub_mm, n + 1)
                    copy(U[rows, 0, :], PS[rows, 2, :]).then_inc(u_act, 1)
                act.wait_ge(o_mm, t + 1)
                copy(o_[:, t, :].rearrange("p (f q d) -> p q f d", f=FC, q=2), PS[:, 4:6, :].rearrange("p q (f d) -> p q f d", f=FC)).then_inc(o_ok, 1)
                if t == 0:
                    ada(23)
                    ada(24)
            act.wait_ge(lvar_ready, 1)
            fn(hs[:, 3, :], hs[:, 2, :], ACT.Sqrt).then_inc(lstd_ok, 1)
            turn(5, hdst)
            post(0, (proj_mm, 8))

            def moe(layer, s, t_set):
                pre(s, t_set)
                act.wait_ge(log_mm, layer + 1)
                fn(rt[:, 0], PS[:, 4, 0:TT * E].rearrange("p (t e) -> p t e", t=TT), ACT.Sigmoid).then_inc(sc_ok, 1)
                for t in range(TT):
                    act.wait_ge(gu_mm, UNITS * layer + t + 1)
                    fn(gsil[:, t, :], PS[:, 4 + t, 0:F], ACT.Silu).then_inc(silu_ok, 1)
                copy(hpart[0], h[:]).then_inc(hb_half, 1)
                for t in range(TT):
                    act.wait_ge(hidT_mm, UNITS * layer + t + 1)
                    copy(actT[:, t], PS[:, 6 + t, 0:F].rearrange("p (c s) -> p c s", c=FK)).then_inc(hidT_ok, 1)
                act.wait_ge(hr_ok, layer + 1)
                copy(hpart[1], hrest).then_inc(hb_half, 1)
                Q = moe_sems[layer]

                def take_picked(i, par):
                    act.wait_ge(Q["gather_mm"], i * 2 + 1)
                    copy(xg[par][:, 0:4, :], PS[:, 4, :].rearrange("p (k s) -> p k s", k=4)).then_inc(Q["xg_act"], 1)

                def pair(i, par):
                    act.wait_ge(Q["gateup_mm"], i + 1)
                    if not (isinstance(i, int) and i == 0):
                        act.wait_ge(Q["hidp_ok"], i)
                    fn(sg, PS[:, 6, 0:F], ACT.Silu).then_inc(Q["sg_ok"], 1)
                    act.wait_ge(Q["wpickT_mm"], i + 1)
                    copy(wpickT, PS[:, 7, 0:TT * P].rearrange("p (t s) -> p t s", t=TT)).then_inc(Q["wpickT_ok"], 1)
                    take_picked(i + 1, 1 - par)
                    act.wait_ge(Q["hidpT_mm"], i + 1)
                    copy(hidT, PS[:, 6, 0:F].rearrange("p (c s) -> p c s", c=FK)).then_inc(Q["hidT2_ok"], 1)
                    act.wait_ge(Q["y_mm"], i * 2 + 1)
                    copy(ye[:, 0:NB], PS[:, 7, :]).then_inc(Q["ye_act"], 1)

                take_picked(0, 0)
                act.wait_ge(list_ok, layer + 1)
                end = act.value_load(rounds[0:1, 0:1], min_val=R0 + 1, max_val=R0 + LIST // 4 - 3)
                pair(0, 0)
                pair(1, 1)
                with act.Fori(1, end) as j:
                    pair(act.snap(j * 2), 0)
                    pair(act.snap(j * 2 + 1), 1)
                post(s, (moe_done, layer + 1))

            if STOP >= 2:
                moe(0, 1, 6)

            if STOP >= 3:
                pre(2, 7)
                for n in range(6):
                    act.wait_ge(proj_mm, 8 + n + 1)
                    fn(qkv[:, :, n * NB:(n + 1) * NB], PS[:, 2 * (n % 2):2 * (n % 2) + 2, :], ACT.Copy,
                       scale=HD ** -0.5 if n < 2 else 1.0).then_inc(proj_ok, 1)
                for n in (8, 9):
                    turn(n, (lambda o: lambda t, b: qkT[:, o + 4 * b:o + 4 * b + 4, t * P:(t + 1) * P])((n - 8) * FC))

                def log_part(g):
                    b = spb[g % 2]
                    act.wait_ge(z_ok, g + 1)
                    if g >= 2:
                        act.wait_ge(pv_mm, g - 1)
                    link(fn(b, zsb[g % 2], ACT.Abs))
                    link(fn(b, b, ACT.Exp, scale=-1.0))
                    fn(b, b, ACT.Ln, bias=1.0).then_inc(l_ok, 1)

                def weights(g):
                    act.wait_ge(ez_ok, g + 1)
                    fn(spb[g % 2], zsb[g % 2], ACT.Exp).then_inc(w_ok, 1)

                log_part(0)
                for g in range(4):
                    if g + 1 < 4:
                        log_part(g + 1)
                    weights(g)
                turn(10, hdst)
                post(2, (proj_mm, 16))
            if STOP >= 4:
                moe(1, 3, 11)

        @block.vector
        def _(dve):
            V = nc.vector
            steps = [0]

            def link(ins):
                steps[0] += 1
                ins.then_inc(dve_step, 1)
                dve.wait_ge(dve_step, steps[0])

            def rms(n):
                dve.wait_ge(ss_ready, 2 * (n + 1))
                link(V.tensor_scalar(ms[:, n, :], ss[:, n, :], 1.0 / D, RMS_EPS, ALU.mult, ALU.add))
                V.reciprocal(ms[:, n, :], ms[:, n, :]).then_inc(ms_ready, 1)
                dve.wait_ge(rstd_ready, n + 1)

            def turn(n, dst):
                for t in range(TT):
                    dve.wait_ge(tr_mm, 4 * n + 2 * t + 2)
                    V.tensor_copy(dst(t, 1), PS[:, 5, :].rearrange("p (k s) -> p k s", k=4)).then_inc(tr_dve, 1)

            def hdst(t, b):
                return hT[:, 4 * b:4 * b + 4, 1 + t * P:1 + (t + 1) * P]

            def hperm(t):
                return h[:, t, :].rearrange("p (k q) -> p q k", k=KC)

            def pre(s, t_set):
                rms(2 * s)
                dve.wait_ge(mpre_in, 48 * (s + 1))
                link(V.scalar_tensor_tensor(out=mt[:, 1, :], in0=mt[:, 1, :], scalar=1.0, in1=mt[:, 2, :], op0=ALU.add, op1=ALU.mult))
                for t in range(TT):
                    link(V.scalar_tensor_tensor(out=mt[:, 2, :], in0=x[:, t, :], scalar=rstd[:, 2 * s, t:t + 1], in1=mt[:, 1, :], op0=ALU.mult, op1=ALU.mult))
                    last = V.tensor_tensor(hperm(t), mt[:, 2, :].rearrange("p (q k) -> p q k", k=KC), mt[:, 0, :].rearrange("p (q k) -> p q k", k=KC), ALU.add)
                    if t == 0:
                        link(last)
                last.then_inc(h_ready, 1)
                turn(t_set, hdst)

            def post(s):
                dve.wait_ge(mpost_in, 32 * (s + 1))
                link(V.tensor_tensor(mt[:, 3, :], mt[:, 3, :], mt[:, 4, :], ALU.mult))
                rms(2 * s + 1)
                for t in range(TT):
                    link(V.scalar_tensor_tensor(out=mt[:, 4, :].rearrange("p (b c) -> p b c", b=HB), in0=PS[:, 2 * t:2 * t + 2, :], scalar=rstd[:, 2 * s + 1, t:t + 1],
                                                in1=mt[:, 3, :].rearrange("p (b c) -> p b c", b=HB), op0=ALU.mult, op1=ALU.mult))
                    last = V.tensor_tensor(x[:, t, :], x[:, t, :], mt[:, 4, :], ALU.add)
                    if t == 0:
                        link(last)
                last.then_inc(x_ready, 1)

            dve.wait_ge(const_ok, 1)
            V.tensor_scalar(cumx[0:64], upto[0:64], -1.0, None, ALU.add)
            V.tensor_copy(cumx[64:128], upto[64:128]).then_inc(triA_ok, 1)

            pre(0, 0)
            dve.wait_ge(tr_act, 2)
            dve.wait_ge(tr_dve, 2)
            link(V.tensor_tensor(xx, hT[:, :, 0:S], hT[:, :, 1:S + 1], ALU.subtract))
            dve.wait_ge(small_in, 3 * 16)
            for m, n in enumerate((3, 4, 5, 0, 1, 2)):
                if m >= 2:
                    if m <= 4:
                        dve.wait_ge(lora1_mm, m - 1)
                    else:
                        dve.wait_ge(proj_mm, 2)
                for k in range(KC):
                    last = V.scalar_tensor_tensor(out=xs[m % 2][:, k, :], in0=xx[:, k, :], scalar=mu[:, n, k:k + 1], in1=hT[:, k, 1:S + 1], op0=ALU.mult, op1=ALU.add)
                last.then_inc(xs_ready, 1)

            def heads(v):
                return v.rearrange("p t (h d) -> p (t h) d", d=HD)

            def both(row):
                return row.rearrange("p (o d) -> p o d", o=1).broadcast_to([P, TT, D])

            def per_head(col):
                return col.rearrange("p (n o) -> p n o", o=1).broadcast_to([P, TT * H, HD])

            dve.wait_ge(proj_ok, 4)
            dve.wait_ge(rows_in, 48)
            dve.wait_ge(lora2_ok, 3)
            dve.wait_ge(tr_mm, 4)
            link(V.tensor_tensor(h[:], k_, both(kkrow), ALU.mult))
            link(V.tensor_tensor(tmpX, h[:], h[:], ALU.mult))
            V.tensor_reduce(hs[:, 0, :], heads(tmpX), AX.X, ALU.add).then_inc(kss_ready, 1)
            link(V.scalar_tensor_tensor(out=tmpY, in0=a_, scalar=-1.0, in1=both(karow), op0=ALU.add, op1=ALU.mult))
            link(V.scalar_tensor_tensor(out=k_, in0=tmpY, scalar=1.0, in1=k_, op0=ALU.add, op1=ALU.mult))
            link(V.tensor_tensor(tmpX, r_, k_, ALU.mult))
            link(V.tensor_tensor(tmpX, tmpX, both(rkrow), ALU.mult))
            V.tensor_reduce(bonus[:], heads(tmpX), AX.X, ALU.add).then_inc(xy_free, 1)
            dve.wait_ge(knorm_ok, 1)
            link(V.tensor_scalar(hs[:, 1, :], hs[:, 1, :], 1e-12, None, ALU.max))
            link(V.reciprocal(hs[:, 1, :], hs[:, 1, :]))
            link(V.tensor_tensor(heads(h[:]), heads(h[:]), per_head(hs[:, 1, :]), ALU.mult))
            link(V.tensor_tensor(a_, a_, h[:], ALU.mult))
            dve.wait_ge(decay_ok, 2)
            V.tensor_tensor(a_, a_, tmpX, ALU.mult).then_inc(tok_ready, 1)
            V.tensor_tensor(k_, k_, tmpX, ALU.mult).then_inc(tok_ready, 1)
            dve.wait_ge(decay_ok, 3)
            V.tensor_tensor(r_, r_, tmpY, ALU.mult).then_inc(tok_ready, 1)
            dve.wait_ge(decay_ok, 4)
            V.scalar_tensor_tensor(out=h[:], in0=h[:], scalar=-1.0, in1=sig, op0=ALU.mult, op1=ALU.mult).then_inc(tok_ready, 1)
            turn(1, lambda t, b: bT[:, 4 * b:4 * b + 4, t * P:(t + 1) * P])
            turn(2, lambda t, b: kT[:, 4 * b:4 * b + 4, t * P:(t + 1) * P])
            turn(3, lambda t, b: ART[:, 4 * b:4 * b + 4, t, 1, :])
            turn(4, lambda t, b: ART[:, 4 * b:4 * b + 4, t, 0, :])
            for fc in range(FC):
                dve.wait_ge(sb_mm, fc + 1)
                b = 2 * (fc % 2)
                if fc == 0:
                    dve.wait_ge(tok_ready, 4)
                for q, dst in ((0, AAB), (1, ARB)):
                    for t in range(TT):
                        u = t * H + 2 * fc
                        last = V.tensor_tensor(dst[:, u:u + 2, :], PS[:, b:b + 2, t * 256 + q * P:t * 256 + (q + 1) * P],
                                               upto[:, q:q + 1, :].broadcast_to([P, 2, P]), ALU.mult)
                last.then_inc(sb_ok, 1)

            def mask_k(t, j):
                n = FC // 2 * t + j
                dve.wait_ge(sk_mm, n + 1)
                if n >= 2:
                    dve.wait_ge(xo_mm, n - 1)
                for f in range(2):
                    last = V.tensor_tensor(SK[j % 2][:, f], PS[:, 2:4, f * 256:(f + 1) * 256],
                                           upto[:].rearrange("p (o a) b -> p o (a b)", o=1).broadcast_to([P, 2, 2 * P]), ALU.mult)
                last.then_inc(sk_ok, 1)

            for t in range(TT):
                for j in range(FC // 2):
                    mask_k(t, j)
                if t == 0:
                    dve.wait_ge(diag_in, 64)
                    dve.wait_ge(ti_init, 1)
                    for s in range(31):
                        w = 31 - s
                        prod = at(22, 1 + s, w)
                        link(V.tensor_tensor(prod, TTi[:, 0:s + 1, s:s + 1].broadcast_to([P, s + 1, w]), DT[:, s:s + 1, s + 1:32].broadcast_to([P, s + 1, w]), ALU.mult))
                        last = V.tensor_tensor(TTi[:, 0:s + 1, s + 1:32], TTi[:, 0:s + 1, s + 1:32], prod, ALU.add)
                        if s < 30:
                            link(last)
                    last.then_inc(inv_ok, 1)
                for i in range(4):
                    n = 4 * t + i
                    rows = slice(32 * i, 32 * i + 32)
                    if i == 0:
                        dve.wait_ge(xo_mm, FC // 2 * (t + 1))
                    if n >= 1:
                        dve.wait_ge(xacc_mm, n)
                    V.tensor_copy(acc[rows, 1, :], PS[rows, 1, :]).then_inc(acc_dve, 1)
                    dve.wait_ge(ub_mm, n + 1)
                    V.tensor_copy(U[rows, 1, :], PS[rows, 3, :]).then_inc(u_dve, 1)
                if t == 0:
                    dve.wait_ge(st_mm, 1)
                    V.tensor_tensor(S0T, PS[:, 2, :].rearrange("p (f d) -> p f d", f=FC), edec[:].rearrange("p (f o) -> p f o", o=1).broadcast_to([P, FC, HD]), ALU.mult).then_inc(s0_ok, 1)

            dve.wait_ge(o_ok, 2)
            dve.wait_ge(lnx_in, 32)
            link(V.tensor_reduce(hs[:, 0, :], heads(o_), AX.X, ALU.add))
            link(V.tensor_scalar(hs[:, 0, :], hs[:, 0, :], -1.0 / HD, None, ALU.mult))
            link(V.tensor_tensor(heads(o_), heads(o_), per_head(hs[:, 0, :]), ALU.add))
            link(V.tensor_tensor(lnsq, o_, o_, ALU.mult))
            link(V.tensor_reduce(hs[:, 2, :], heads(lnsq), AX.X, ALU.add))
            link(V.tensor_scalar(hs[:, 2, :], hs[:, 2, :], 1.0 / HD, LNX_EPS, ALU.mult, ALU.add))
            V.reciprocal(hs[:, 2, :], hs[:, 2, :]).then_inc(lvar_ready, 1)
            link(V.tensor_tensor(heads(lnsq), heads(v_), per_head(bonus[:]), ALU.mult))
            dve.wait_ge(lstd_ok, 1)
            link(V.tensor_tensor(heads(o_), heads(o_), per_head(hs[:, 3, :]), ALU.mult))
            link(V.tensor_tensor(o_, o_, both(mt[:, 0, :]), ALU.mult))
            link(V.tensor_tensor(o_, o_, both(mt[:, 1, :]), ALU.add))
            link(V.tensor_tensor(o_, o_, lnsq, ALU.add))
            for t in range(TT):
                last = V.tensor_tensor(hperm(t), o_[:, t, :].rearrange("p (q k) -> p q k", k=KC), g_[:, t, :].rearrange("p (q k) -> p q k", k=KC), ALU.mult)
            last.then_inc(h_ready, 1)
            turn(5, hdst)
            post(0)

            def moe(layer, s, t_set):
                pre(s, t_set)
                sc, biased, rest, mask, chosen, gates = (rt[:, i] for i in range(6))
                dve.wait_ge(sc_ok, layer + 1)
                dve.wait_ge(router_in, 32 * (layer + 1))
                link(V.tensor_tensor(biased, sc, rb.broadcast_to([P, TT, E]), ALU.add))
                for t in range(TT):
                    link(V.max(top8[:, t, :], biased[:, t, :]))
                    link(V.match_replace(rest[:, t, :], top8[:, t, :], biased[:, t, :], -1e30))
                V.tensor_tensor(mask, biased, rest, ALU.not_equal).then_inc(mask_ok, 1)
                dve.wait_ge(mask_ok, layer + 1)
                link(V.tensor_tensor(chosen, sc, mask, ALU.mult))
                link(V.tensor_reduce(rsum[:, 0, :], chosen, AX.X, ALU.add))
                link(V.reciprocal(rsum[:, 1, :], rsum[:, 0, :]))
                for t in range(TT):
                    last = V.tensor_scalar(gates[:, t, :], chosen[:, t, :], rsum[:, 1, t:t + 1], ROUTED_SCALE, ALU.mult, ALU.mult)
                link(last)
                Q = moe_sems[layer]
                for t in range(TT):
                    dve.wait_ge(silu_ok, UNITS * layer + t + 1)
                    V.tensor_tensor(actp[:, t].rearrange("p c q -> p q c"), PS[:, 4 + t, F:2 * F].rearrange("p (q c) -> p q c", c=FK),
                                    gsil[:, t, :].rearrange("p (q c) -> p q c", c=FK), ALU.mult).then_inc(hid_ok, 1)
                dve.wait_ge(hb_half, 2 * layer + 1)
                V.tensor_tensor(hrest, h[:], hpart[0], ALU.subtract).then_inc(hr_ok, 1)
                dve.wait_ge(pos_mm, layer + 1)
                link(V.scalar_tensor_tensor(out=posm, in0=PS[:, 4, 0:TT * E].rearrange("p (t e) -> p t e", t=TT), scalar=1.0, in1=mask, op0=ALU.add, op1=ALU.mult))
                for w in range(NW):
                    last = V.tensor_scalar(efl[:, 0, w:w + 1], PS[0:E, 5, 0:1], float(W * (w + 1)), None, ALU.is_gt)
                V.memset(efl[:, 1, 0:1], 0.0)
                link(last)
                link(V.tensor_copy(efl[:, 1, 1:2], efl[:, 0, 0:1]))
                V.tensor_tensor(efl[:, 1, 2:3], efl[:, 0, 0:1], efl[:, 0, 1:2], ALU.add).then_inc(flag_ok, 1)

                def picks(i, par, where):
                    if not (isinstance(i, int) and i < 2):
                        dve.wait_ge(Q["wpickT_mm"], i - 1)
                    for m in range(2):
                        e, c0 = where(m)
                        for t in range(TT):
                            pos, gate = posm[:, t, bass.ds(e, 1)], gates[:, t, bass.ds(e, 1)]
                            V.tensor_scalar(pick[par][:, t, W * m:W * m + W], place[:, bass.ds(c0, W)], pos, None, ALU.is_equal)
                            last = V.tensor_scalar(wpick[par][:, t, W * m:W * m + W], place[:, bass.ds(c0, W)], pos, gate, ALU.is_equal, ALU.mult)
                    last.then_inc(Q["pick_ok"], 1)

                picks(0, 0, lambda m: (m, 0))
                dve.wait_ge(idx_mm, layer + 1)
                link(V.tensor_scalar(efl[:, 2, :], PS[0:E, 6, 0:NW], 1.0, None, ALU.add))
                for w in range(NW):
                    last = V.tensor_scalar(hit[:, w, :], place[0:E, 0:LIST], efl[:, 2, w:w + 1], efl[:, 0, w:w + 1], ALU.is_equal, ALU.mult)
                last.then_inc(hit_ok, 1)
                dve.wait_ge(hb_half, 2 * layer + 2)
                V.tensor_tensor(hpart[2], hrest, hpart[1], ALU.subtract).then_inc(hb_ok, 1)
                picks(1, 1, lambda m: (2 + m, 0))
                dve.wait_ge(list_mm, layer + 1)
                V.tensor_copy(lists[0:1, 0, :], PS[0:1, 7, 0:LIST])
                V.tensor_scalar(lists[0:1, 1, :], PS[0:1, 7, LIST:2 * LIST], float(W * (MAXWIN - 1)), None, ALU.add)
                link(V.tensor_reduce(lrow[:, 0:1], PS[0:1, 7, 2 * LIST:2 * LIST + NW], AX.X, ALU.add))
                link(V.tensor_scalar(lrow[:, 8:16], place[0:1, 0:8], 4.0, lrow[:, 0:1], ALU.mult, ALU.is_lt))
                link(V.tensor_reduce(lrow[:, 1:2], lrow[:, 8:16], AX.X, ALU.add))
                V.tensor_scalar(rounds[:], lrow[:, 1:2], float(R0 + 1), None, ALU.add).then_inc(list_ok, 1)
                dve.wait_ge(list_ok, layer + 1)
                end = dve.value_load(rounds[0:1, 0:1], min_val=R0 + 1, max_val=R0 + LIST // 4 - 3)

                def take_picked(i, par):
                    dve.wait_ge(Q["gather_mm"], i * 2 + 2)
                    V.tensor_copy(xg[par][:, 4:8, :], PS[:, 5, :].rearrange("p (k s) -> p k s", k=4)).then_inc(Q["xg_dve"], 1)

                def pair(i, par, where):
                    dve.wait_ge(Q["sg_ok"], i + 1)
                    if not (isinstance(i, int) and i == 0):
                        dve.wait_ge(Q["hidpT_mm"], i)
                    V.tensor_tensor(hidp.rearrange("p c q -> p q c"), PS[:, 6, F:2 * F].rearrange("p (q c) -> p q c", c=FK),
                                    sg.rearrange("p (q c) -> p q c", c=FK), ALU.mult).then_inc(Q["hidp_ok"], 1)
                    take_picked(i + 1, 1 - par)
                    dve.wait_ge(Q["y_mm"], i * 2 + 2)
                    V.tensor_copy(ye[:, NB:D], PS[:, 6, :]).then_inc(Q["ye_dve"], 1)
                    picks(i + 2, par, where)

                take_picked(0, 0)
                pair(0, 0, lambda m: (4 + m, 0))
                pair(1, 1, lambda m: (6 + m, 0))
                with dve.Fori(1, R0 - 1) as j:
                    for q in range(2):
                        pair(dve.snap(j * 2 + q), q, lambda m: (dve.snap(j * 4 + (4 + 2 * q + m)), 0))
                with dve.Fori(R0 - 1, end) as j:
                    for q in range(2):
                        def listed(m):
                            n = dve.snap(j * 4 + (4 + 2 * q + m - E))
                            return (dve.value_load(lists[0:1, 0, bass.ds(n, 1)], min_val=0, max_val=E - 1),
                                    dve.value_load(lists[0:1, 1, bass.ds(n, 1)], min_val=0, max_val=W * (MAXWIN - 1)))
                        pair(dve.snap(j * 2 + q), q, listed)
                post(s)

            if STOP >= 2:
                moe(0, 1, 6)

            if STOP >= 3:
                pre(2, 7)
                V.memset(zmask[:, P:2 * P], 0.0)
                V.tensor_scalar(zmask[:, 0:P], upto[:, 0, :], -1.0, 1e30, ALU.add, ALU.mult)
                link(V.tensor_scalar(zmask[:, 2 * P:384], upto[:, 0, :], -1.0, 1e30, ALU.add, ALU.mult))
                for n in (8, 9):
                    turn(n, (lambda o: lambda t, b: qkT[:, o + 4 * b:o + 4 * b + 4, t * P:(t + 1) * P])((n - 8) * FC))

                def take_z(g):
                    dve.wait_ge(z_mm, g + 1)
                    if g >= 2:
                        dve.wait_ge(w_ok, g - 1)
                    V.tensor_tensor(zsb[g % 2], PS[:, 0:4, 0:384], zmask.rearrange("p (o c) -> p o c", o=1).broadcast_to([P, 4, 384]), ALU.add).then_inc(z_ok, 1)

                def softplus(g):
                    dve.wait_ge(l_ok, g + 1)
                    V.scalar_tensor_tensor(out=spb[g % 2], in0=zsb[g % 2], scalar=0.0, in1=spb[g % 2], op0=ALU.max, op1=ALU.add).then_inc(sp_ok, 1)

                def log_weights(g):
                    dve.wait_ge(rc_mm, g + 1)
                    V.tensor_tensor(zsb[g % 2], zsb[g % 2], PS[:, 4:8, 0:384], ALU.subtract).then_inc(ez_ok, 1)

                def take_o(g):
                    dve.wait_ge(pv_mm, g + 1)
                    for t in range(TT):
                        dst = h[:, t, :].rearrange("p (k j q) -> p j q k", k=KC, j=H)[:, 4 * g:4 * g + 4]
                        last = V.tensor_copy(dst, PS[:, 0:4, 384 + t * HD:384 + (t + 1) * HD].rearrange("p j (q k) -> p j q k", k=KC))
                    last.then_inc(o_taken if g < 3 else h_ready, 1)

                take_z(0)
                softplus(0)
                for g in range(4):
                    if g + 1 < 4:
                        take_z(g + 1)
                    log_weights(g)
                    if g + 1 < 4:
                        softplus(g + 1)
                    take_o(g)
                turn(10, hdst)
                post(2)
            if STOP >= 4:
                moe(1, 3, 11)


_IN = ['x', 'c', 'ada_w', 'ada_b', 'norm_pre_mix', 'norm_post_mix', 'norm_pre_ffn', 'norm_post_ffn', 'rwkv_mu', 'rwkv_w_rkv',
       'rwkv_w_w1', 'rwkv_w_w2', 'rwkv_w0', 'rwkv_w_a1', 'rwkv_w_a2', 'rwkv_a0', 'rwkv_w_g1', 'rwkv_w_g2', 'rwkv_k_k',
       'rwkv_k_a', 'rwkv_r_k', 'rwkv_lnx_g', 'rwkv_lnx_b', 'rwkv_w_o', 'sb_w_qkv', 'sb_w_o', 'moe_w_router',
       'moe_router_bias', 'moe_w_gate', 'moe_w_up', 'moe_w_down', 'moe_ws_gate', 'moe_ws_up', 'moe_ws_down']


def kernel(**inputs):
    import numpy as np
    import concourse.bacc as bacc
    from concourse.bass_utils import run_bass_kernel_spmd

    nc = bacc.Bacc("TRN2", target_bir_lowering=False, num_devices=1)
    arrays, aps = {}, {}
    for name in _IN:
        v = np.ascontiguousarray(inputs[name])
        arrays[f"in_{name}"] = v
        aps[name] = nc.dram_tensor(f"in_{name}", v.shape, mybir.dt.from_np(v.dtype), kind="ExternalInput").ap()
    out = nc.dram_tensor("out", inputs["x"].shape, F32, kind="ExternalOutput").ap()
    hybrid_trunk(nc, aps, out)
    r = run_bass_kernel_spmd(nc, [arrays], core_ids=[0])
    return r.results[0]["out"]
```

```python
from contextlib import ExitStack
import math

import concourse.bass as bass
from concourse import mybir

F32 = mybir.dt.float32
BF16 = mybir.dt.bfloat16
I32 = mybir.dt.int32
ALU = mybir.AluOpType
ACT = mybir.ActivationFunctionType
AX = mybir.AxisListType

P = 128
SUBLAYERS = 4


def hybrid_trunk(nc, a, out):
    _, S, D = a["x"].shape
    TT = S // P
    KC = D // P
    HD = a["rwkv_r_k"].shape[2]
    H = D // HD
    FC = D // P
    E = a["moe_w_gate"].shape[1]
    F = a["moe_w_gate"].shape[3]
    FK = F // P
    LW, LA, LG = a["rwkv_w_w1"].shape[2], a["rwkv_w_a1"].shape[2], a["rwkv_w_g1"].shape[2]
    NB = 512
    HB = D // NB
    TOPK = 8
    ROUTED_SCALE = 2.5
    RMS_EPS, LNX_EPS = 1e-6, 64e-5
    DECAY = math.exp(-0.5)
    W = 64
    NW = S // W - 1
    MAXWIN = S // W + 1
    LIST = 48
    R0 = E // 4
    NADA = a["ada_w"].shape[2] // NB
    assert TT == 2 and KC == 8 and HD == 64 and F == 256 and NADA == 12

    with ExitStack() as ctx:
        def sb(name, shape):
            return ctx.enter_context(nc.sbuf_tensor(name, shape, F32))

        def sem(name):
            return ctx.enter_context(nc.semaphore(name))

        PS = ctx.enter_context(nc.psum_tensor("PS", [P, 8, NB], F32))

        x = sb("x", [P, TT, D])
        mt = sb("mt", [P, 5, D])
        h = sb("h", [P, TT, D])
        hT = sb("hT", [P, KC, S + 1])
        ident = sb("ident", [P, P])
        upto = sb("upto", [P, 2, P])
        cumx = sb("cumx", [P, 2, P])
        fromj = sb("fromj", [P, P])
        ones = sb("ones", [P, P])
        halves = sb("halves", [P, 2])
        sel = sb("sel", [P, 2 * NADA])
        ccol = sb("ccol", [P, KC])
        crep = sb("crep", [P, KC, 32])
        BIAS0, APN = 97, 97 + 2 * NADA
        apart, arow = mt[:, 4, NB:2 * NB], mt[0:1, 3, :].rearrange("p (b c) -> p b c", b=2)
        mu = sb("mu", [P, 6, KC])
        ss = sb("ss", [P, 8, TT])
        ms = sb("ms", [P, 8, TT])
        rstd = sb("rstd", [P, 8, TT])
        hs = sb("hs", [P, 4, TT * H])
        bonus = sb("bonus", [P, TT * H])
        edec = sb("edec", [P, FC])
        top8 = sb("top8", [P, TT, TOPK])
        rsum = sb("rsum", [P, 2, TT])
        place = sb("place", [P, MAXWIN * W])
        efl = sb("efl", [E, 3, NW])
        ecol = sb("ecol", [E, 1])
        wcol = sb("wcol", [E, NW])
        lrow = sb("lrow", [1, 16])
        lists = ctx.enter_context(nc.sbuf_tensor("lists", [1, 2, 4 + LIST], I32))
        rounds = ctx.enter_context(nc.sbuf_tensor("rounds", [1, 2], I32))
        AK = 156
        arena = sb("arena", [P, AK * 256])

        def at(kib, *dims):
            n = 1
            for d in dims:
                n *= d
            v = arena[:, int(kib * 256):int(kib * 256) + n]
            names = "abcd"[:len(dims)]
            if len(dims) == 1:
                return v
            return v.rearrange(f"p ({' '.join(names)}) -> p {' '.join(names)}", **dict(zip(names, dims)))

        def slot(s, *dims):
            return at(24 * s, *dims)

        selrep = at(40, 4, P)
        xs = [at(16, KC, S), at(40, KC, S)]
        xx = at(64, KC, S)
        w1w, w1a, w1g = at(72, KC, LW), at(74, KC, LA), at(76, KC, LG)
        w2w, w2a, w2g = at(80, D), at(84, D), at(88, D)
        t1 = at(92, 3, S)
        r_, k_, v_, g_, a_, sig = (at(96 + 8 * i, TT, D) for i in range(6))
        kkrow, karow, rkrow = at(144, D), at(148, D), at(152, D)
        ART = at(48, FC, TT, 2, P)
        bT, kT = at(64, FC, S), at(72, FC, S)
        tmpX, tmpY = at(80, TT, D), at(88, TT, D)
        ARB = at(80, TT * H, P)
        AAB = at(136, TT * H, P)
        TB = at(18, TT * H, 32)
        U = at(42, 2, NB)
        S0T = at(46, FC, HD)
        acc = at(152, 2, NB)
        DT = h[:, 0, :].rearrange("p (s t) -> p s t", s=32)
        TTi = h[:, 1, :].rearrange("p (s t) -> p s t", s=32)
        SK = [mt[:, 2 - i, :].rearrange("p (f q c) -> p f q c", f=2, q=2) for i in range(2)]
        o_ = r_
        lnsq = at(48, TT, D)
        qkv = at(96, TT, 3 * D)
        qkT = at(120, 2 * FC, S)
        zsb = [at(136, 4, 384), at(142, 4, 384), at(40, 4, 384)]
        spb = [at(148, 4, 384), mt[:, 0:2, :].rearrange("p a b -> p (a b)")[:, 0:1536].rearrange("p (a b) -> p a b", a=4), at(64, 4, 384)]
        posm = at(107, TT, E)
        def half_at(kib, *dims):
            n = 1
            for d in dims:
                n *= d
            v = arena[:, int(kib * 256):int(kib * 256) + n // 2].bitcast(BF16)
            names = "abcd"[:len(dims)]
            return v.rearrange(f"p ({' '.join(names)}) -> p {' '.join(names)}", **dict(zip(names, dims)))
        hpart = [half_at(108 + 4 * i, TT, D) for i in range(3)]
        hrest = at(120, TT, D)
        xg = [at(128 + 4 * i, KC, 2 * W) for i in range(2)]
        pick = [half_at(136 + i / 2, TT, 2 * W) for i in range(2)]
        wpick = [at(137 + i, TT, 2 * W) for i in range(2)]
        wpickT = at(139, TT, P)
        ye = at(140, D)
        hidp = at(144, FK, P)
        hidT = at(145, FK, P)
        sg = at(146, F)
        gsil = at(96, TT, F)
        actp = at(98, TT, FK, P)
        actT = at(100, TT, FK, P)
        rt = at(102, 6, TT, E)
        rw = at(105, KC, E)
        rb = at(148, 1, E)
        hit = at(147, NW, LIST)[0:E]
        zmask = mt[:, 1, NB:NB + 384]

        mod_dram = nc.dram_tensor("mod_rows", [2 * NADA, NB], F32, kind="Internal").ap()
        diag_dram = nc.dram_tensor("diag_blocks", [4, 32, TT * H, 32], F32, kind="Internal").ap()
        inv_dram = nc.dram_tensor("inverse_blocks", [4, TT * H, 32, 32], F32, kind="Internal").ap()

        ring_in = [sem(f"ring_in{i}") for i in range(4)]
        ring2_in = [sem(f"ring2_in{i}") for i in range(4)]
        moe_sems = [{n: sem(f"{n}{l}") for n in ("pick_ok", "gather_mm", "xg_act", "xg_dve", "gateup_mm", "sg_ok", "hidp_ok", "wpickT_mm", "wpickT_ok",
                                                 "hidpT_mm", "hidT2_ok", "y_mm", "ye_act", "ye_dve")} for l in range(2)]
        hb_ok = sem("hb_ok"); hb_half = sem("hb_half"); hr_ok = sem("hr_ok"); mask_ok = sem("mask_ok"); pos_mm = sem("pos_mm"); flag_ok = sem("flag_ok"); idx_mm = sem("idx_mm"); hit_ok = sem("hit_ok")
        list_mm = sem("list_mm"); list_ok = sem("list_ok"); moe_done = sem("moe_done")
        x_in = sem("x_in"); router_in = sem("router_in"); ccol_in = sem("ccol_in"); adab_in = sem("adab_in"); small_in = sem("small_in"); lora_in = sem("lora_in"); rows_in = sem("rows_in")
        mpre_in = sem("mpre_in"); mpost_in = sem("mpost_in"); lnx_in = sem("lnx_in")
        const_ok = sem("const_ok"); pool_step = sem("pool_step"); crep_ok = sem("crep_ok"); triA_ok = sem("triA_ok")
        ada_mm = sem("ada_mm"); ada_part = sem("ada_part"); ada_row_mm = sem("ada_row_mm"); ada_row = sem("ada_row")
        mod_stored = [sem("mod_stored0"), sem("mod_stored1")]
        ss_ready = sem("ss_ready"); ms_ready = sem("ms_ready"); rstd_ready = sem("rstd_ready")
        h_ready = sem("h_ready"); x_ready = sem("x_ready"); h_half = sem("h_half"); x_half = sem("x_half")
        tr_mm = sem("tr_mm"); tr_act = sem("tr_act"); tr_dve = sem("tr_dve")
        xs_ready = sem("xs_ready"); lora1_mm = sem("lora1_mm"); lora1_ok = sem("lora1_ok")
        lora2_mm = sem("lora2_mm"); lora2_ok = sem("lora2_ok")
        proj_mm = sem("proj_mm"); proj_ok = sem("proj_ok")
        cum_mm = sem("cum_mm"); decay_ok = sem("decay_ok"); kss_ready = sem("kss_ready"); knorm_ok = sem("knorm_ok")
        xy_free = sem("xy_free"); tok_ready = sem("tok_ready")
        sb_mm = sem("sb_mm"); sb_ok = sem("sb_ok"); sk_mm = sem("sk_mm"); sk_ok = sem("sk_ok"); xo_mm = sem("xo_mm")
        diag_out = sem("diag_out"); diag_in = sem("diag_in"); ti_init = sem("ti_init"); inv_ok = sem("inv_ok"); inv_out = sem("inv_out"); inv_in = sem("inv_in")
        xacc_mm = sem("xacc_mm"); acc_act = sem("acc_act"); acc_dve = sem("acc_dve"); ub_mm = sem("ub_mm"); u_act = sem("u_act"); u_dve = sem("u_dve")
        o_mm = sem("o_mm"); o_ok = sem("o_ok"); st_mm = sem("st_mm"); s0_ok = sem("s0_ok")
        lvar_ready = sem("lvar_ready"); lstd_ok = sem("lstd_ok")
        ccol_ok = sem("ccol_ok"); o_taken = sem("o_taken"); z_mm = sem("z_mm"); z_ok = sem("z_ok"); l_ok = sem("l_ok"); sp_ok = sem("sp_ok"); rc_mm = sem("rc_mm"); ez_ok = sem("ez_ok"); w_ok = sem("w_ok"); pv_mm = sem("pv_mm")
        log_mm = sem("log_mm"); sc_ok = sem("sc_ok")
        gu_mm = sem("gu_mm"); silu_ok = sem("silu_ok"); hid_ok = sem("hid_ok"); hidT_mm = sem("hidT_mm"); hidT_ok = sem("hidT_ok"); down_mm = sem("down_mm")
        dve_step = sem("dve_step"); act_step = sem("act_step"); x_out = sem("x_out")

        def stored(i):
            return 16 * ((i - 4) // 2 + 1)

        x_d = a["x"].rearrange("b (t p) d -> p (b t) d", p=P)
        out_d = out.rearrange("b (t p) d -> p (b t) d", p=P)

        def tile_of(w, block):
            return w.rearrange("(p k) n -> p k n", k=KC)[:, :, block * NB:(block + 1) * NB]

        def row_on_all(v, n):
            return v.rearrange("(o n) -> o n", o=1).broadcast_to([P, n])

        ring, arrivals = [], [0] * 4

        def ring_item(s, copies, free):
            arrivals[s] += 16 * len(copies)
            ring.append((s, copies, free))
            return s, arrivals[s]

        def ada_copy(s, i):
            return [(slot(s, KC, NB), tile_of(a["ada_w"][i // NADA], i % NADA))]

        def expert_copies(s, gate, up, down):
            half = KC * F
            base = slot(s, 2 * half + FK * D)
            return [(base[:, 0:half], gate.rearrange("(p k) f -> p (k f)", k=KC)),
                    (base[:, half:2 * half], up.rearrange("(p k) f -> p (k f)", k=KC)),
                    (base[:, 2 * half:], down.rearrange("(p c) d -> p (c d)", c=FK))]

        ada_at, proj_at = {}, {}
        for i, s in zip(range(4), (0, 1, 2, 0)):
            ada_at[i] = ring_item(s, ada_copy(s, i), [(ada_mm, 1)] if i == 3 else [])
        for j, s in enumerate((1, 2, 0, 1, 2, 0)):
            free = (ada_mm, (2, 3, 4)[j]) if j < 3 else (proj_mm, j - 2)
            proj_at[j] = ring_item(s, [(slot(s, KC, NB), tile_of(a["rwkv_w_rkv"][0, j // HB], j % HB))], [free])
        for i in range(4, 2 * NADA):
            s = 1 - i % 2
            free = (proj_mm, i) if i == 4 else (proj_mm, 6) if i == 5 else (ada_mm, i - 1)
            ada_at[i] = ring_item(s, ada_copy(s, i), [free])
        for j in range(HB):
            s = 1 - j
            proj_at[6 + j] = ring_item(s, [(slot(s, KC, NB), tile_of(a["rwkv_w_o"][0], j))], [(ada_mm, 23 + j)])

        UNITS = TT
        base_in = {0: list(arrivals)}
        arrivals = [0] * 4
        ring2_start = len(ring)
        qslots = (3, 0, 1, 2, 3, 0)
        for j, s in enumerate(qslots):
            free = [(moe_done, 1)] if j < 4 else [(proj_mm, 8 + j - 4 + 1)]
            proj_at[8 + j] = ring_item(s, [(slot(s, KC, NB), tile_of(a["sb_w_qkv"][0], j))], free)
        for j, s in enumerate((1, 2)):
            proj_at[14 + j] = ring_item(s, [(slot(s, KC, NB), tile_of(a["sb_w_o"][0], j))], [(proj_mm, 8 + 2 + j + 1)])
        base_in[1] = list(arrivals)

        block = ctx.enter_context(nc.Block())

        @block.sync
        def _(sp):
            def run(items, arrive):
                for s, copies, free in items:
                    for sm, v in free:
                        sp.wait_ge(sm, v)
                    for dst, src in copies:
                        sp.dma_start(dst, src).then_inc(arrive[s], 16)

            def moe(layer):
                arrive = (ring_in, ring2_in)[layer]
                y_mm = moe_sems[layer]["y_mm"]
                first = 2 if layer == 0 else 3
                if layer == 0:
                    sp.wait_ge(h_ready, 2)
                else:
                    sp.wait_ge(proj_mm, 13)
                for dst, src in expert_copies(first, a["moe_ws_gate"][layer], a["moe_ws_up"][layer], a["moe_ws_down"][layer]):
                    sp.dma_start(dst, src).then_inc(arrive[first], 16)

                def expert(e, s):
                    for dst, src in expert_copies(s, a["moe_w_gate"][layer, e], a["moe_w_up"][layer, e], a["moe_w_down"][layer, e]):
                        sp.dma_start(dst, src).then_inc(arrive[s], 16)

                def expert_at_register(e, s):
                    half = KC * F
                    base = slot(s, 2 * half + FK * D)
                    for lo, hi, w in ((0, half, "moe_w_gate"), (half, 2 * half, "moe_w_up"), (2 * half, 2 * half + FK * D, "moe_w_down")):
                        src = a[w][layer].rearrange("e (p k) f -> p e (k f)", p=P)[:, bass.ds(e, 1), :]
                        sp.dma_start(base[:, lo:hi].rearrange("p (o f) -> p o f", o=1), src).then_inc(arrive[s], 16)

                if layer == 0:
                    waits = [(proj_mm, 6), (proj_mm, 8), (proj_mm, 7)]
                else:
                    waits = [(proj_mm, 14), (proj_mm, 15), (proj_mm, 16)]
                for e in range(3):
                    sp.wait_ge(*waits[e])
                    expert(e, (first + 1 + e) % 4)
                sp.wait_ge(down_mm, UNITS * (layer + 1))
                expert(3, first)
                with sp.Fori(1, R0 - 1) as j:
                    for q in range(4):
                        sp.wait_ge(y_mm, j * 4 + (2 * (q // 2) - 2))
                        expert_at_register(sp.snap(j * 4 + q), (first + 1 + q) % 4)
                sp.wait_ge(list_ok, layer + 1)
                end = sp.value_load(rounds[0:1, 0:1], min_val=R0, max_val=R0 + LIST // 4 - 4)
                last_free = sp.value_load(rounds[0:1, 1:2], min_val=4 * R0 - 2, max_val=4 * (R0 + LIST // 4 - 4))

                def listed_expert(j, q, free):
                    e = sp.value_load(lists[0:1, 0, bass.ds(j * 4 + (q + 4 - E), 1)], min_val=0, max_val=E - 1)
                    sp.wait_ge(y_mm, free)
                    expert_at_register(e, (first + 1 + q) % 4)

                with sp.Fori(R0 - 1, end) as j:
                    for q in range(4):
                        listed_expert(j, q, j * 4 + (2 * (q // 2) - 2))
                for q in range(2):
                    listed_expert(end, q, last_free)

            sp.dma_start(x[:], x_d).then_inc(x_in, 16)
            run(ring[:ring2_start], ring_in)
            moe(0)
            run(ring[ring2_start:], ring2_in)
            moe(1)
            sp.wait_ge(x_ready, SUBLAYERS)
            sp.dma_start(out_d, x[:]).then_inc(x_out, 16)
            sp.wait_ge(x_out, 16)

        @block.gpsimd
        def _(pool):
            steps = [0]

            def link(ins):
                steps[0] += 1
                ins.then_inc(pool_step, 1)
                pool.wait_ge(pool_step, steps[0])

            g = nc.gpsimd
            link(g.memset(sel[:], 0.0))
            link(g.memset(ident[:], 0.0))
            link(g.memset(selrep, 0.0))
            for q in range(4):
                link(g.memset(sel[32 * q:32 * q + 1, :], 1.0))
                link(g.memset(selrep[32 * q:32 * q + 1], 1.0))
            link(g.affine_select(out=ident[:], in_=ident[:], compare_op=ALU.not_equal, fill=1.0, base=0, pattern=[[-1, P]], channel_multiplier=1))
            link(g.affine_select(out=sel[:], in_=sel[:], compare_op=ALU.not_equal, fill=1.0, base=-BIAS0, pattern=[[-1, 2 * NADA]], channel_multiplier=1))
            g.affine_select(out=selrep, in_=selrep, compare_op=ALU.not_equal, fill=1.0, base=-BIAS0, pattern=[[-1, 4], [0, P]], channel_multiplier=1).then_inc(const_ok, 1)

            link(g.memset(ones[:], 1.0))
            link(g.iota(place[:], pattern=[[1, MAXWIN * W]], base=1, channel_multiplier=0, allow_small_or_imprecise_dtypes=True))
            link(g.iota(ecol[:], pattern=[[0, 1]], base=0, channel_multiplier=1, allow_small_or_imprecise_dtypes=True))
            for w in range(NW):
                link(g.memset(wcol[:, w:w + 1], float(W * (w + 1) - W * (MAXWIN - 1))))
            link(g.memset(halves[:], 0.0))
            link(g.memset(hT[:, :, 0:1], 0.0))
            link(g.memset(t1[64:65, 0:2, :], 1.0))
            link(g.memset(upto[:], 1.0))
            link(g.memset(halves[64:128, 0:1], 1.0))
            link(g.memset(halves[0:64, 1:2], 1.0))
            link(g.affine_select(out=upto[:, 0, :], in_=upto[:, 0, :], compare_op=ALU.is_ge, fill=0.0, base=-1, pattern=[[1, P]], channel_multiplier=-1))
            link(g.affine_select(out=upto[:, 1, :], in_=upto[:, 1, :], compare_op=ALU.is_ge, fill=0.0, base=0, pattern=[[1, P]], channel_multiplier=-1))
            g.affine_select(out=fromj[:], in_=ones[:], compare_op=ALU.is_ge, fill=0.0, base=0, pattern=[[-1, P]], channel_multiplier=1).then_inc(const_ok, 1)

            pool.dma_start(mu[:], a["rwkv_mu"][0].rearrange("n (p k) -> p n k", k=KC)).then_inc(small_in, 16)
            pool.dma_start(mt[:, 2, :], row_on_all(a["norm_pre_mix"][0], D)).then_inc(mpre_in, 16)

            for dst, src in ((w1w, a["rwkv_w_w1"]), (w1a, a["rwkv_w_a1"]), (w1g, a["rwkv_w_g1"])):
                pool.dma_start(dst, src[0].rearrange("(p k) n -> p k n", k=KC)).then_inc(lora_in, 16)
            pool.dma_start(w2w[0:LW], a["rwkv_w_w2"][0]).then_inc(lora_in, 16)
            pool.dma_start(w2w[LW:LW + 1], a["rwkv_w0"]).then_inc(lora_in, 16)
            pool.dma_start(w2a[0:LA], a["rwkv_w_a2"][0]).then_inc(lora_in, 16)
            pool.dma_start(w2a[LA:LA + 1], a["rwkv_a0"]).then_inc(lora_in, 16)
            pool.dma_start(w2g, a["rwkv_w_g2"][0]).then_inc(lora_in, 16)
            for dst, n in ((kkrow, "rwkv_k_k"), (karow, "rwkv_k_a")):
                pool.dma_start(dst, row_on_all(a[n][0], D)).then_inc(rows_in, 16)
            pool.dma_start(rkrow, row_on_all(a["rwkv_r_k"][0].rearrange("h d -> (h d)"), D)).then_inc(rows_in, 16)

            def load_pre(s):
                l, off = s // 2, NADA // 2 * (s % 2) + NADA * (s // 2)
                gain = "norm_pre_mix" if s % 2 == 0 else "norm_pre_ffn"
                pool.wait_ge(mod_stored[1], stored(off + 3))
                pool.wait_ge(mod_stored[0], stored(off + 2))
                flat = mod_dram.rearrange("a b -> (a b)")
                pool.dma_start(mt[:, 0, :], row_on_all(flat[off * NB:(off + 2) * NB], D)).then_inc(mpre_in, 16)
                pool.dma_start(mt[:, 1, :], row_on_all(flat[(off + 2) * NB:(off + 4) * NB], D)).then_inc(mpre_in, 16)
                pool.dma_start(mt[:, 2, :], row_on_all(a[gain][l], D)).then_inc(mpre_in, 16)

            def load_post(s):
                l, off = s // 2, NADA // 2 * (s % 2) + NADA * (s // 2)
                gain = "norm_post_mix" if s % 2 == 0 else "norm_post_ffn"
                pool.wait_ge(mod_stored[1], stored(off + 5))
                pool.wait_ge(mod_stored[0], stored(off + 4))
                flat = mod_dram.rearrange("a b -> (a b)")
                pool.dma_start(mt[:, 3, :], row_on_all(flat[(off + 4) * NB:(off + 6) * NB], D)).then_inc(mpost_in, 16)
                pool.dma_start(mt[:, 4, :], row_on_all(a[gain][l], D)).then_inc(mpost_in, 16)

            pool.wait_ge(h_ready, 1)
            pool.dma_start(mt[:, 0, :], row_on_all(a["rwkv_lnx_g"][0], D)).then_inc(lnx_in, 16)
            pool.wait_ge(sb_ok, FC)
            for i in range(4):
                pool.dma_start(diag_dram[i], AAB[32 * i:32 * i + 32, :, 32 * i:32 * i + 32]).then_inc(diag_out, 16)
            pool.wait_ge(diag_out, 64)
            pool.wait_ge(tr_mm, 20)
            for i in range(4):
                pool.dma_start(DT[32 * i:32 * i + 32], diag_dram[i].rearrange("s u t -> u s t")).then_inc(diag_in, 16)
            link(g.memset(TTi, 0.0))
            g.affine_select(out=TTi, in_=TTi, compare_op=ALU.not_equal, fill=1.0, base=0, pattern=[[1, 32], [-1, 32]], channel_multiplier=0).then_inc(ti_init, 1)
            pool.wait_ge(inv_ok, 1)
            pool.dma_start(inv_dram.rearrange("i u s t -> (i u) (s t)"), h[:, 1, :]).then_inc(inv_out, 16)
            pool.wait_ge(inv_out, 16)
            for i in range(4):
                pool.dma_start(TB[32 * i:32 * i + 32], inv_dram[i].rearrange("u s t -> s u t")).then_inc(inv_in, 16)
            pool.wait_ge(xo_mm, FC)
            pool.dma_start(mt[:, 1, :], row_on_all(a["rwkv_lnx_b"][0], D)).then_inc(lnx_in, 16)
            pool.wait_ge(mod_stored[1], stored(2 * NADA - 1))
            pool.wait_ge(mod_stored[0], stored(2 * NADA - 2))
            load_post(0)
            for s in range(1, SUBLAYERS):
                pool.wait_ge(h_ready, (0, 2, 3, 5)[s])
                load_pre(s)
                pool.wait_ge(x_ready, s)
                if s % 2:
                    pool.dma_start(rw, a["moe_w_router"][s // 2].rearrange("(p k) e -> p k e", k=KC)).then_inc(router_in, 16)
                    pool.dma_start(rb[:, 0, :], row_on_all(a["moe_router_bias"][s // 2], E)).then_inc(router_in, 16)
                load_post(s)

        @block.tensor
        def _(pe):
            mm = nc.tensor.matmul

            def ada_mm_step(i):
                s, v = ada_at[i]
                pe.wait_ge(ring_in[s], v)
                if i >= 1:
                    pe.wait_ge(ada_part, i)
                w = slot(s, KC, NB)
                for j in range(2):
                    for q in range(4):
                        last = mm(PS[32 * q:32 * q + 32, 7, :], crep[:, 2 * q + j, :], w[:, 2 * q + j, :], start=(j == 0), stop=(j == 1))
                last.then_inc(ada_mm, 1)

            def ada_row_step(i):
                pe.wait_ge(ada_part, i + 1)
                if i >= 1:
                    pe.wait_ge(ada_row, i)
                if i < 4:
                    mm(PS[:, 6, :], selrep[0:APN, i, :], apart[0:APN], start=True, stop=True).then_inc(ada_row_mm, 1)
                else:
                    mm(PS[0:1, 6, :], sel[0:APN, i:i + 1], apart[0:APN], start=True, stop=True).then_inc(ada_row_mm, 1)

            def ada(i):
                if i in ada_at:
                    ada_mm_step(i)
                if i - 1 in ada_at and i != 4:
                    ada_row_step(i - 1)

            def turn(n, src, half=None, tiles=(0, 1)):
                for f in (f for t in tiles for f in (2 * t, 2 * t + 1)):
                    fill = 4 * n + f
                    if half is not None and f % 2 == 0:
                        pe.wait_ge(*((h_ready, {0: 1, 5: 2, 6: 3, 7: 4, 11: 6}[n]) if f else (h_half, half)))
                    if fill >= 2:
                        pe.wait_ge(tr_act if fill % 2 == 0 else tr_dve, fill // 2)
                    for q in range(4):
                        last = nc.tensor.transpose(PS[:, 4 + f % 2, q * P:(q + 1) * P], src(f // 2, 4 * (f % 2) + q), ident[:])
                    last.then_inc(tr_mm, 1)

            def turned(n):
                pe.wait_ge(tr_act, 2 * (n + 1))
                pe.wait_ge(tr_dve, 2 * (n + 1))

            def hsrc(t, k):
                return h[:, t, k * P:(k + 1) * P]

            def proj(n, src, banks, free):
                s, v = proj_at[n]
                pe.wait_ge((ring_in if n < 8 else ring2_in)[s], v)
                for sm, val in free:
                    pe.wait_ge(sm, val)
                w = slot(s, KC, NB)
                for t in range(TT):
                    for k in range(KC):
                        last = mm(PS[:, banks[t], :], src(k, t), w[:, k, :], start=(k == 0), stop=(k == KC - 1))
                last.then_inc(proj_mm, 1)

            def hTsrc(k, t):
                return hT[:, k, 1 + t * P:1 + (t + 1) * P]

            def head(fc, p):
                return 2 * fc + p

            pe.wait_ge(const_ok, 1)
            pe.wait_ge(crep_ok, 1)
            pe.wait_ge(adab_in, 16)
            for i in range(4):
                ada_mm_step(i)
                ada_row_step(i)

            pe.wait_ge(const_ok, 2)
            turn(0, hsrc, 1)
            pe.wait_ge(lora_in, 16 * 8)
            for m, (w1, w2, n1, n2) in enumerate(((w1w, w2w, LW, LW + 1), (w1a, w2a, LA, LA + 1), (w1g, w2g, LG, LG))):
                pe.wait_ge(xs_ready, m + 1)
                if m:
                    pe.wait_ge(lora1_ok, m)
                else:
                    turned(0)
                for k in range(KC):
                    last = mm(PS[0:n1, 5, 0:S], w1[:, k, :], xs[m % 2][:, k, :], start=(k == 0), stop=(k == KC - 1))
                last.then_inc(lora1_mm, 1)
                pe.wait_ge(lora1_ok, m + 1)
                if m:
                    pe.wait_ge(lora2_ok, m)
                for t in range(TT):
                    for b in range(HB):
                        last = mm(PS[:, 2 * t + b, :], t1[0:n2, m, t * P:(t + 1) * P], w2[0:n2, b * NB:(b + 1) * NB], start=True, stop=True)
                last.then_inc(lora2_mm, 1)
            def cum(n, bank):
                for t in range(TT):
                    for b in range(HB):
                        last = mm(PS[:, bank + 2 * t + b, :], cumx[:, n, :], sig[:, t, b * NB:(b + 1) * NB], start=True, stop=True)
                last.then_inc(cum_mm, 1)

            for n in range(6):
                m, b = n // HB, n % HB
                if b == 0:
                    pe.wait_ge(xs_ready, 4 + m)
                src = (lambda m: lambda k, t: xs[(3 + m) % 2][:, k, t * P:(t + 1) * P])(m)
                proj(n, src, (2 * b, 2 * b + 1), [(lora2_ok, 3)] if n < 2 else [(proj_ok, n - 1)])
                if n == 3:
                    for fc in range(FC):
                        for t in range(TT):
                            last = mm(PS[:, 5, fc:fc + 1], sig[:, t, fc * P:(fc + 1) * P], halves[:, t:t + 1], start=(fc == 0 and t == 0), stop=(t == TT - 1), skip_group_check=True)
                    last.then_inc(cum_mm, 1)
                if n == 4:
                    pe.wait_ge(triA_ok, 1)
                    pe.wait_ge(decay_ok, 1)
                    cum(1, 4)
            pe.wait_ge(proj_ok, 6)
            cum(0, 0)
            pe.wait_ge(decay_ok, 3)
            ada(4)
            ada(5)
            for n, buf in ((1, a_), (2, k_), (3, r_), (4, h)):
                pe.wait_ge(tok_ready, n)
                turn(n, (lambda b: lambda t, k: b[:, t, k * P:(k + 1) * P])(buf))
                ada(5 + n)
            turned(4)

            for fc in range(FC):
                if fc >= 2:
                    pe.wait_ge(sb_ok, fc - 1)
                else:
                    pe.wait_ge(decay_ok, 4)
                for t in range(TT):
                    for p in range(2):
                        last = mm(PS[:, 2 * (fc % 2) + p, t * 256:(t + 1) * 256], bT[64 * p:64 * p + 64, fc, t * P:(t + 1) * P],
                                  ART[64 * p:64 * p + 64, fc, t, :, :], start=(t == 0), stop=(t == 1), skip_group_check=True)
                last.then_inc(sb_mm, 1)
                if fc % 2:
                    ada(10 + fc // 2)

            FP = FC // 2

            def score_k(t, j):
                n = FP * t + j
                if j:
                    pe.wait_ge(sk_ok, n)
                for f in range(2):
                    fc = 2 * j + f
                    for p in range(2):
                        last = mm(PS[:, 2 + p, f * 256:(f + 1) * 256], kT[64 * p:64 * p + 64, fc, t * P:(t + 1) * P],
                                  ART[64 * p:64 * p + 64, fc, t, :, :], start=(f == 0), stop=True, skip_group_check=True)
                last.then_inc(sk_mm, 1)

            def score_v(t, j):
                n = FP * t + j
                pe.wait_ge(sk_ok, n + 1)
                for f in range(2):
                    fc = 2 * j + f
                    for p in range(2):
                        rhs = v_[:, t, head(fc, p) * HD:(head(fc, p) + 1) * HD]
                        mm(PS[:, p, fc * HD:(fc + 1) * HD], SK[j % 2][:, f, p, 0:P], rhs, start=(fc == 0), stop=False, skip_group_check=True)
                        last = mm(PS[:, 4 + p, fc * HD:(fc + 1) * HD], SK[j % 2][:, f, p, P:2 * P], rhs, start=(fc == 0), stop=False, skip_group_check=True)
                last.then_inc(xo_mm, 1)

            for t in range(TT):
                if t == 0:
                    pe.wait_ge(sb_ok, FC)
                else:
                    pe.wait_ge(o_ok, 1)
                    pe.wait_ge(s0_ok, 1)
                score_k(t, 0)
                for j in range(FP):
                    if j + 1 < FP:
                        score_k(t, j + 1)
                    score_v(t, j)
                for fc in range(FC) if t else ():
                    for p in range(2):
                        mm(PS[:, 4 + p, fc * HD:(fc + 1) * HD], ART[64 * p:64 * p + 64, fc, t, 1, :], S0T[64 * p:64 * p + 64, fc, :], start=False, stop=False, skip_group_check=True)
                        last = mm(PS[:, p, fc * HD:(fc + 1) * HD], ART[64 * p:64 * p + 64, fc, t, 0, :], S0T[64 * p:64 * p + 64, fc, :], start=False, stop=False, skip_group_check=True)
                if t == 0:
                    for i in range(14, 20):
                        ada(i)
                    pe.wait_ge(inv_in, 64)
                for i in range(4):
                    n = 4 * t + i
                    rows = slice(32 * i, 32 * i + 32)
                    if i:
                        pe.wait_ge(u_act, n)
                        pe.wait_ge(u_dve, n)
                        for fc in range(FC):
                            for p in range(2):
                                last = mm(PS[rows, p, fc * HD:(fc + 1) * HD], AAB[0:32 * i, t * H + head(fc, p), rows], U[0:32 * i, p, fc * HD:(fc + 1) * HD],
                                          start=False, stop=False, skip_group_check=True)
                        last.then_inc(xacc_mm, 1)
                    if i == 0 and t:
                        last.then_inc(xacc_mm, 1)
                    pe.wait_ge(acc_act, n + 1)
                    pe.wait_ge(acc_dve, n + 1)
                    for fc in range(FC):
                        for p in range(2):
                            last = mm(PS[rows, 2 + p, fc * HD:(fc + 1) * HD], TB[rows, t * H + head(fc, p), :], acc[rows, p, fc * HD:(fc + 1) * HD],
                                      start=(fc == 0), stop=True, skip_group_check=True)
                    last.then_inc(ub_mm, 1)
                    if t == 0:
                        ada(20 + i)
                pe.wait_ge(u_act, 4 * t + 4)
                pe.wait_ge(u_dve, 4 * t + 4)
                for fc in range(FC):
                    for p in range(2):
                        last = mm(PS[:, 4 + p, fc * HD:(fc + 1) * HD], ARB[:, t * H + head(fc, p), :], U[:, p, fc * HD:(fc + 1) * HD], start=False, stop=True, skip_group_check=True)
                last.then_inc(o_mm, 1)
                if t == 0:
                    for fc in range(FC):
                        for p in range(2):
                            cols = slice(head(fc, p) * HD, (head(fc, p) + 1) * HD)
                            mm(PS[64 * p:64 * p + 64, 2, fc * HD:(fc + 1) * HD], a_[:, 0, cols], U[:, p, fc * HD:(fc + 1) * HD], start=(fc == 0), stop=False, skip_group_check=True)
                            last = mm(PS[64 * p:64 * p + 64, 2, fc * HD:(fc + 1) * HD], k_[:, 0, cols], v_[:, 0, cols], start=False, stop=True, skip_group_check=True)
                    last.then_inc(st_mm, 1)
                    ada(24)

            def out_proj(n, t_set):
                turned(t_set)
                for j in range(HB):
                    proj(n + j, hTsrc, (j, 2 + j), [])

            def out_tile(t, j):
                sl, v = proj_at[6 + j]
                pe.wait_ge(ring_in[sl], v)
                pe.wait_ge(tr_act, 10 + t + 1)
                pe.wait_ge(tr_dve, 10 + t + 1)
                for k in range(KC):
                    last = mm(PS[:, 2 * t + j, :], hTsrc(k, t), slot(sl, KC, NB)[:, k, :], start=(k == 0), stop=(k == KC - 1))
                if t == TT - 1:
                    last.then_inc(proj_mm, 1)

            pe.wait_ge(o_ok, 2)
            turn(5, hsrc, 2, tiles=(0,))
            out_tile(0, 0)
            turn(5, hsrc, 2, tiles=(1,))
            out_tile(0, 1)
            out_tile(1, 0)
            out_tile(1, 1)

            def moe(layer, t_set):
                Q = moe_sems[layer]
                arrive = (ring_in, ring2_in)[layer]
                for t in range(TT):
                    turn(t_set, hsrc, (3, 5)[layer], tiles=(t,))
                    pe.wait_ge(router_in, 32 * (layer + 1))
                    pe.wait_ge(tr_act, 2 * t_set + t + 1)
                    pe.wait_ge(tr_dve, 2 * t_set + t + 1)
                    for k in range(KC):
                        last = mm(PS[:, 6, t * E:(t + 1) * E], hTsrc(k, t), rw[:, k, :], start=(t == 0 and k == 0), stop=(k == KC - 1), skip_group_check=True)
                last.then_inc(log_mm, 1)
                first = (2, 3)[layer]
                half = KC * F
                got = list(base_in[layer])
                got[first] += 48
                base = UNITS * layer

                pe.wait_ge(arrive[first], got[first])
                w = slot(first, 2, KC, F)
                for t in range(TT):
                    for k in range(KC):
                        last = mm(PS[:, 4 + t, :], hTsrc(k, t), w[:, :, k, :], start=(k == 0), stop=(k == KC - 1))
                    last.then_inc(gu_mm, 1)
                pe.wait_ge(sc_ok, layer + 1)
                for t in range(TT):
                    pe.wait_ge(hid_ok, base + t + 1)
                    for c in range(FK):
                        last = nc.tensor.transpose(PS[:, 6 + t, c * P:(c + 1) * P], actp[:, t, c, :], ident[:])
                    last.then_inc(hidT_mm, 1)
                w = slot(first, 2 * half + FK * D)[:, 2 * half:].rearrange("p (c d) -> p c d", c=FK)
                for t in range(TT):
                    pe.wait_ge(hidT_ok, base + t + 1)
                    for c in range(FK):
                        for b in range(HB):
                            last = mm(PS[:, 2 * t + b, :], actT[:, t, c, :], w[:, c, b * NB:(b + 1) * NB], start=(c == 0), stop=False, skip_group_check=True)
                    last.then_inc(down_mm, 1)

                pe.wait_ge(mask_ok, layer + 1)
                mask = rt[:, 3]
                mm(PS[:, 4, 0:E], upto[:, 0, :], mask[:, 0, :], start=True, stop=True, skip_group_check=True)
                mm(PS[:, 4, E:2 * E], upto[:, 0, :], mask[:, 1, :], start=False, stop=False, skip_group_check=True)
                mm(PS[:, 4, E:2 * E], ones[:], mask[:, 0, :], start=False, stop=True, skip_group_check=True)
                mm(PS[0:E, 5, 0:1], mask[:, 0, :], ones[:, 0:1], start=True, stop=False)
                mm(PS[0:E, 5, 0:1], mask[:, 1, :], ones[:, 0:1], start=False, stop=True).then_inc(pos_mm, 1)
                pe.wait_ge(flag_ok, layer + 1)
                mm(PS[0:E, 6, 0:NW], upto[0:E, 0, 0:E], efl[:, 0, :], start=True, stop=False)
                mm(PS[0:E, 6, 0:NW], ones[0:E, 0:E], efl[:, 1, :], start=False, stop=True).then_inc(idx_mm, 1)
                pe.wait_ge(hit_ok, layer + 1)
                for n, col in ((0, lambda w: ecol[:]), (1, lambda w: wcol[:, w:w + 1])):
                    for w_ in range(NW):
                        mm(PS[0:1, 7, n * LIST:(n + 1) * LIST], col(w_), hit[:, w_, :], start=(n == 0 and w_ == 0), stop=(w_ == NW - 1), skip_group_check=True)
                mm(PS[0:1, 7, 2 * LIST:2 * LIST + NW], ones[0:E, 0:1], efl[:, 0, :], start=False, stop=True, skip_group_check=True).then_inc(list_mm, 1)

                def gather(i, f, par):
                    pe.wait_ge(Q["pick_ok"], i + 1)
                    if not (isinstance(i, int) and i == 0):
                        pe.wait_ge(Q["xg_dve"] if f else Q["xg_act"], i)
                    for kk in range(4):
                        k = 4 * f + kk
                        for n in range(3):
                            for t in range(TT):
                                last = mm(PS[:, 4 + f, kk * P:(kk + 1) * P], hpart[n][:, t, k * P:(k + 1) * P], pick[par][:, t, :],
                                          start=(n == 0 and t == 0), stop=(n == 2 and t == TT - 1), skip_group_check=True)
                    last.then_inc(Q["gather_mm"], 1)

                pe.wait_ge(hb_ok, layer + 1)
                gather(0, 0, 0)
                gather(0, 1, 0)
                pe.wait_ge(list_ok, layer + 1)
                end = pe.value_load(rounds[0:1, 0:1], min_val=R0, max_val=R0 + LIST // 4 - 4)

                def pair(j, q, peeled=False, final=False):
                    i = 2 * j + q if peeled else pe.snap(j * 2 + q)
                    slots = [(first + 1 + 2 * q + m) % 4 for m in range(2)]
                    for s in slots:
                        pe.wait_ge(arrive[s], j * 48 + (got[s] + 48))
                    pe.wait_ge(Q["xg_act"], i + 1)
                    pe.wait_ge(Q["xg_dve"], i + 1)
                    if not (peeled and i == 0):
                        pe.wait_ge(Q["ye_dve"], i)
                    ws = [slot(s, 2, KC, F) for s in slots]
                    for k in range(KC):
                        for m in range(2):
                            last = mm(PS[W * m:W * m + W, 6, :], xg[q][:, k, W * m:W * m + W], ws[m][:, :, k, :], start=(k == 0), stop=(k == KC - 1))
                    last.then_inc(Q["gateup_mm"], 1)
                    if not (peeled and i == 0):
                        pe.wait_ge(Q["ye_act"], i)
                    for t in range(TT):
                        last = nc.tensor.transpose(PS[:, 7, t * P:(t + 1) * P], wpick[q][:, t, :], ident[:])
                    last.then_inc(Q["wpickT_mm"], 1)
                    if not final:
                        gather(i + 1, 0, 1 - q)
                    pe.wait_ge(Q["hidp_ok"], i + 1)
                    for c in range(FK):
                        last = nc.tensor.transpose(PS[:, 6, c * P:(c + 1) * P], hidp[:, c, :], ident[:])
                    last.then_inc(Q["hidpT_mm"], 1)
                    if not final:
                        gather(i + 1, 1, 1 - q)
                    pe.wait_ge(Q["wpickT_ok"], i + 1)
                    pe.wait_ge(Q["hidT2_ok"], i + 1)
                    wd = [slot(s, 2 * half + FK * D)[:, 2 * half:].rearrange("p (c d) -> p c d", c=FK) for s in slots]
                    for b in range(HB):
                        for c in range(FK):
                            for m in range(2):
                                last = mm(PS[W * m:W * m + W, 7 - b, :], hidT[:, c, W * m:W * m + W], wd[m][:, c, b * NB:(b + 1) * NB], start=(c == 0), stop=(c == FK - 1))
                        last.then_inc(Q["y_mm"], 1)
                    for b in range(HB):
                        pe.wait_ge(Q["ye_dve"] if b else Q["ye_act"], i + 1)
                        for t in range(TT):
                            mm(PS[:, 2 * t + b, :], wpickT[:, t, :], ye[:, b * NB:(b + 1) * NB], start=False, stop=False, skip_group_check=True)

                pair(0, 0, True)
                pair(0, 1, True)
                with pe.Fori(1, end) as j:
                    pair(j, 0)
                    pair(j, 1)
                pair(end, 0, final=True)
                nc.tensor.transpose(PS[:, 4, 0:P], ident[:], ident[:]).then_inc(moe_done, 1)

            moe(0, 6)

            turn(7, hsrc, 4)
            turned(7)
            for n in range(4):
                proj(8 + n, hTsrc, (2 * (n % 2), 2 * (n % 2) + 1), [(proj_ok, 6 + n - 1)] if n >= 2 else [(x_ready, 2)])
            for n, part in ((8, 0), (9, 1)):
                pe.wait_ge(proj_ok, 6 + 2 * (part + 1))
                turn(n, (lambda q: lambda t, k: qkv[:, t, q * D + k * P:q * D + (k + 1) * P])(part))
            turned(9)
            pe.wait_ge(proj_ok, 10)

            def z_scores(g):
                if g:
                    pe.wait_ge(z_ok, g)
                if g == 3:
                    pe.wait_ge(o_taken, 1)
                for j in range(4):
                    fc, p = 2 * g + j // 2, j % 2
                    q, k = qkT[64 * p:64 * p + 64, fc, :], qkT[64 * p:64 * p + 64, FC + fc, :]
                    mm(PS[:, j, 0:S], k[:, 0:P], q, start=True, stop=True, skip_group_check=True)
                    last = mm(PS[:, j, S:S + P], k[:, P:S], q[:, P:S], start=False, stop=True, skip_group_check=True)
                last.then_inc(z_mm, 1)

            def tail_sums(g):
                pe.wait_ge(sp_ok, g + 1)
                pe.wait_ge(*((ez_ok, g) if g else (proj_ok, 12)))
                for j in range(4):
                    mm(PS[:, 4 + j, 0:384], fromj[:], spb[g % 3][:, j, :], start=True, stop=False, skip_group_check=True)
                    last = mm(PS[:, 4 + j, P:S], ones[:], spb[g % 3][:, j, S:384], start=False, stop=True, skip_group_check=True)
                last.then_inc(rc_mm, 1)

            def weigh_v(g):
                pe.wait_ge(w_ok, g + 1)
                pe.wait_ge(z_ok, min(g + 3, 4))
                if g:
                    pe.wait_ge(o_taken, g)
                for j in range(4):
                    hd = 4 * g + j
                    w = spb[g % 3][:, j, :]
                    v0, v1 = (qkv[:, t, 2 * D + hd * HD:2 * D + (hd + 1) * HD] for t in range(TT))
                    mm(PS[:, j, 384:384 + HD], w[:, 0:P], v0, start=True, stop=True, skip_group_check=True)
                    mm(PS[:, j, 384 + HD:NB], w[:, P:2 * P], v0, start=False, stop=False, skip_group_check=True)
                    last = mm(PS[:, j, 384 + HD:NB], w[:, 2 * P:384], v1, start=False, stop=True, skip_group_check=True)
                last.then_inc(pv_mm, 1)

            z_scores(0)
            proj(12, hTsrc, (6, 7), [])
            z_scores(1)
            proj(13, hTsrc, (4, 5), [])
            z_scores(2)
            tail_sums(0)
            tail_sums(1)
            weigh_v(0)
            z_scores(3)
            tail_sums(2)
            weigh_v(1)
            tail_sums(3)
            weigh_v(2)
            weigh_v(3)
            pe.wait_ge(h_ready, 5)
            turn(10, hsrc)
            out_proj(14, 10)
            moe(1, 11)

        @block.scalar
        def _(act):
            fn = nc.scalar.activation
            steps = [0]

            def link(ins):
                steps[0] += 1
                ins.then_inc(act_step, 1)
                act.wait_ge(act_step, steps[0])

            def copy(out_, in_):
                return fn(out_, in_, ACT.Copy)

            def ada_part_step(i):
                act.wait_ge(ada_mm, i + 1)
                if i >= 1:
                    act.wait_ge(ada_row_mm, i)
                copy(apart[0:BIAS0], PS[0:BIAS0, 7, :]).then_inc(ada_part, 1)

            def ada_row_step(i):
                act.wait_ge(ada_row_mm, i + 1)
                if i < 4:
                    copy(mt[:, i // 2, (i % 2) * NB:(i % 2 + 1) * NB], PS[:, 6, :]).then_inc(ada_row, 1)
                    return
                if i >= 6:
                    act.wait_ge(mod_stored[i % 2], stored(i - 2))
                copy(arow[:, i % 2, :], PS[0:1, 6, :]).then_inc(ada_row, 1)
                act.wait_ge(ada_row, i + 1)
                act.dma_start(mod_dram[i:i + 1, :], arow[:, i % 2, :]).then_inc(mod_stored[i % 2], 16)

            def ada(i):
                if i in ada_at:
                    ada_part_step(i)
                if i - 1 in ada_at and i != 4:
                    ada_row_step(i - 1)

            def rms(n, src, second=()):
                for t in range(TT):
                    for sm, v in second if t else ():
                        act.wait_ge(sm, v)
                    fn(h[:, t, :], src(t), ACT.Square, accum_out=ss[:, n, t:t + 1]).then_inc(ss_ready, 1)
                act.wait_ge(ms_ready, n + 1)
                fn(rstd[:, n, :], ms[:, n, :], ACT.Sqrt).then_inc(rstd_ready, 1)

            def turn(n, dst, tiles=(0, 1)):
                for t in tiles:
                    act.wait_ge(tr_mm, 4 * n + 2 * t + 1)
                    copy(dst(t, 0), PS[:, 4, :].rearrange("p (k s) -> p k s", k=4)).then_inc(tr_act, 1)

            def hdst(t, b):
                return hT[:, 4 * b:4 * b + 4, 1 + t * P:1 + (t + 1) * P]

            def pre(s, t_set):
                if s:
                    act.wait_ge(x_half, s)
                    rms(2 * s, lambda t: x[:, t, :], [(x_ready, s)])
                turn(t_set, hdst)

            def post(s, y_done):
                act.wait_ge(*y_done)
                rms(2 * s + 1, lambda t: PS[:, 2 * t:2 * t + 2, :])

            act.dma_start(ccol[:], a["c"].rearrange("b (p k) -> p (b k)", k=KC)).then_inc(ccol_in, 16)
            act.dma_start(apart[BIAS0:APN], a["ada_b"].rearrange("l (n c) -> (l n) c", c=NB)).then_inc(adab_in, 16)
            act.wait_ge(ccol_in, 16)
            fn(ccol[:], ccol[:], ACT.Silu).then_inc(ccol_ok, 1)
            act.wait_ge(ccol_ok, 1)
            fn(crep[:], ccol[:].rearrange("p (k o) -> p k o", o=1).broadcast_to([P, KC, 32]), ACT.Copy).then_inc(crep_ok, 1)
            act.wait_ge(x_in, 16)
            rms(0, lambda t: x[:, t, :])
            for i in range(4):
                ada_part_step(i)
                ada_row_step(i)

            pre(0, 0)
            for m, (dst, f1, f2, n1) in enumerate(((sig, ACT.Tanh, ACT.Sigmoid, LW), (a_, ACT.Copy, ACT.Sigmoid, LA), (g_, ACT.Sigmoid, ACT.Copy, LG))):
                act.wait_ge(lora1_mm, m + 1)
                fn(t1[0:n1, m, :], PS[0:n1, 5, 0:S], f1).then_inc(lora1_ok, 1)
                act.wait_ge(lora2_mm, m + 1)
                fn(dst.rearrange("p t (b c) -> p (t b) c", b=HB), PS[:, 0:4, :], f2).then_inc(lora2_ok, 1)
            for n in range(6):
                dst = (r_, k_, v_)[n // 2]
                b = n % 2
                if n == 5:
                    act.wait_ge(kss_ready, 1)
                    fn(hs[:, 1, :], hs[:, 0, :], ACT.Sqrt).then_inc(knorm_ok, 1)
                    act.wait_ge(cum_mm, 2)
                    act.wait_ge(xy_free, 1)
                    sums = PS[:, 4:8, :]
                    fn(tmpX.rearrange("p t (b c) -> p (t b) c", b=HB), sums, ACT.Exp, scale=DECAY).then_inc(decay_ok, 1)
                    fn(tmpY.rearrange("p t (b c) -> p (t b) c", b=HB), sums, ACT.Exp, scale=-DECAY).then_inc(decay_ok, 1)
                act.wait_ge(proj_mm, n + 1)
                copy(dst[:, :, b * NB:(b + 1) * NB], PS[:, 2 * b:2 * b + 2, :]).then_inc(proj_ok, 1)
                if n == 3:
                    act.wait_ge(cum_mm, 1)
                    fn(edec[:], PS[:, 5, 0:FC], ACT.Exp, scale=-DECAY).then_inc(decay_ok, 1)
            act.wait_ge(cum_mm, 3)
            fn(sig.rearrange("p t (b c) -> p (t b) c", b=HB), PS[:, 0:4, :], ACT.Exp, scale=-DECAY).then_inc(decay_ok, 1)
            ada(4)
            ada(5)
            for n, dst in ((1, lambda t, b: bT[:, 4 * b:4 * b + 4, t * P:(t + 1) * P]),
                           (2, lambda t, b: kT[:, 4 * b:4 * b + 4, t * P:(t + 1) * P]),
                           (3, lambda t, b: ART[:, 4 * b:4 * b + 4, t, 1, :]),
                           (4, lambda t, b: ART[:, 4 * b:4 * b + 4, t, 0, :])):
                turn(n, dst)
                ada(5 + n)
            for i in range(10, 20):
                ada(i)

            def head_std(t):
                act.wait_ge(lvar_ready, t + 1)
                fn(hs[:, 3, t * H:(t + 1) * H], hs[:, 2, t * H:(t + 1) * H], ACT.Sqrt).then_inc(lstd_ok, 1)

            for t in range(TT):
                for i in range(4):
                    n = 4 * t + i
                    rows = slice(32 * i, 32 * i + 32)
                    if i == 0:
                        act.wait_ge(xo_mm, FC // 2 * (t + 1))
                    if n >= 1:
                        act.wait_ge(xacc_mm, n)
                    copy(acc[rows, 0, :], PS[rows, 0, :]).then_inc(acc_act, 1)
                    if t == 0 and i:
                        ada(20 + i - 1)
                    act.wait_ge(ub_mm, n + 1)
                    copy(U[rows, 0, :], PS[rows, 2, :]).then_inc(u_act, 1)
                    if t == 1 and i == 2:
                        head_std(0)
                act.wait_ge(o_mm, t + 1)
                copy(o_[:, t, :].rearrange("p (f q d) -> p q f d", f=FC, q=2), PS[:, 4:6, :].rearrange("p q (f d) -> p q f d", f=FC)).then_inc(o_ok, 1)
                if t == 0:
                    ada(23)
                    ada(24)
            turn(5, hdst, tiles=(0,))
            head_std(1)
            turn(5, hdst, tiles=(1,))
            post(0, (proj_mm, 8))

            def moe(layer, s, t_set):
                pre(s, t_set)
                act.wait_ge(log_mm, layer + 1)
                fn(rt[:, 0], PS[:, 6, 0:TT * E].rearrange("p (t e) -> p t e", t=TT), ACT.Sigmoid).then_inc(sc_ok, 1)
                for t in range(TT):
                    act.wait_ge(gu_mm, UNITS * layer + t + 1)
                    fn(gsil[:, t, :], PS[:, 4 + t, 0:F], ACT.Silu).then_inc(silu_ok, 1)
                copy(hpart[0], h[:]).then_inc(hb_half, 1)
                for t in range(TT):
                    act.wait_ge(hidT_mm, UNITS * layer + t + 1)
                    copy(actT[:, t], PS[:, 6 + t, 0:F].rearrange("p (c s) -> p c s", c=FK)).then_inc(hidT_ok, 1)
                act.wait_ge(hr_ok, layer + 1)
                copy(hpart[1], hrest).then_inc(hb_half, 1)
                Q = moe_sems[layer]

                def take_picked(i, par):
                    act.wait_ge(Q["gather_mm"], i * 2 + 1)
                    copy(xg[par][:, 0:4, :], PS[:, 4, :].rearrange("p (k s) -> p k s", k=4)).then_inc(Q["xg_act"], 1)

                def pair(i, par, final=False):
                    act.wait_ge(Q["gateup_mm"], i + 1)
                    if not (isinstance(i, int) and i == 0):
                        act.wait_ge(Q["hidp_ok"], i)
                    fn(sg, PS[:, 6, 0:F], ACT.Silu).then_inc(Q["sg_ok"], 1)
                    act.wait_ge(Q["wpickT_mm"], i + 1)
                    copy(wpickT, PS[:, 7, 0:TT * P].rearrange("p (t s) -> p t s", t=TT)).then_inc(Q["wpickT_ok"], 1)
                    if not final:
                        take_picked(i + 1, 1 - par)
                    act.wait_ge(Q["hidpT_mm"], i + 1)
                    copy(hidT, PS[:, 6, 0:F].rearrange("p (c s) -> p c s", c=FK)).then_inc(Q["hidT2_ok"], 1)
                    act.wait_ge(Q["y_mm"], i * 2 + 1)
                    copy(ye[:, 0:NB], PS[:, 7, :]).then_inc(Q["ye_act"], 1)

                take_picked(0, 0)
                act.wait_ge(list_ok, layer + 1)
                end = act.value_load(rounds[0:1, 0:1], min_val=R0, max_val=R0 + LIST // 4 - 4)
                pair(0, 0)
                pair(1, 1)
                with act.Fori(1, end) as j:
                    pair(act.snap(j * 2), 0)
                    pair(act.snap(j * 2 + 1), 1)
                pair(act.snap(end * 2), 0, final=True)
                post(s, (moe_done, layer + 1))

            moe(0, 1, 6)

            pre(2, 7)

            def take_proj(n, bank):
                act.wait_ge(proj_mm, 8 + n + 1)
                fn(qkv[:, :, n * NB:(n + 1) * NB], PS[:, bank:bank + 2, :], ACT.Copy, scale=HD ** -0.5 if n < 2 else 1.0).then_inc(proj_ok, 1)

            for n in range(4):
                take_proj(n, 2 * (n % 2))
            for n in (8, 9):
                turn(n, (lambda o: lambda t, b: qkT[:, o + 4 * b:o + 4 * b + 4, t * P:(t + 1) * P])((n - 8) * FC))

            def log_part(g):
                b = spb[g % 3]
                act.wait_ge(z_ok, g + 1)
                if g == 3:
                    act.wait_ge(pv_mm, 1)
                link(fn(b, zsb[g % 3], ACT.Abs))
                link(fn(b, b, ACT.Exp, scale=-1.0))
                fn(b, b, ACT.Ln, bias=1.0).then_inc(l_ok, 1)

            def weights(g):
                act.wait_ge(ez_ok, g + 1)
                fn(spb[g % 3], zsb[g % 3], ACT.Exp).then_inc(w_ok, 1)

            log_part(0)
            take_proj(4, 6)
            log_part(1)
            take_proj(5, 4)
            weights(0)
            log_part(2)
            weights(1)
            log_part(3)
            weights(2)
            weights(3)
            turn(10, hdst)
            post(2, (proj_mm, 16))
            moe(1, 3, 11)

        @block.vector
        def _(dve):
            V = nc.vector
            steps = [0]

            def link(ins):
                steps[0] += 1
                ins.then_inc(dve_step, 1)
                dve.wait_ge(dve_step, steps[0])

            def rms(n):
                dve.wait_ge(ss_ready, 2 * (n + 1))
                link(V.tensor_scalar(ms[:, n, :], ss[:, n, :], 1.0 / D, RMS_EPS, ALU.mult, ALU.add))
                V.reciprocal(ms[:, n, :], ms[:, n, :]).then_inc(ms_ready, 1)
                dve.wait_ge(rstd_ready, n + 1)

            def turn_tile(n, t, dst):
                dve.wait_ge(tr_mm, 4 * n + 2 * t + 2)
                V.tensor_copy(dst(t, 1), PS[:, 5, :].rearrange("p (k s) -> p k s", k=4)).then_inc(tr_dve, 1)

            def turn(n, dst):
                for t in range(TT):
                    turn_tile(n, t, dst)

            def hdst(t, b):
                return hT[:, 4 * b:4 * b + 4, 1 + t * P:1 + (t + 1) * P]

            def hperm(t):
                return h[:, t, :].rearrange("p (k q) -> p q k", k=KC)

            def pre(s, t_set):
                dve.wait_ge(mpre_in, 48 * s + 16)
                if s == 0:
                    dve.wait_ge(ada_row, 4)
                link(V.scalar_tensor_tensor(out=mt[:, 1, :], in0=mt[:, 1, :], scalar=1.0, in1=mt[:, 2, :], op0=ALU.add, op1=ALU.mult))
                if s:
                    rms(2 * s)
                for t in range(TT):
                    link(V.scalar_tensor_tensor(out=mt[:, 2, :], in0=x[:, t, :], scalar=rstd[:, 2 * s, t:t + 1], in1=mt[:, 1, :], op0=ALU.mult, op1=ALU.mult))
                    last = V.tensor_tensor(hperm(t), mt[:, 2, :].rearrange("p (q k) -> p q k", k=KC), mt[:, 0, :].rearrange("p (q k) -> p q k", k=KC), ALU.add)
                    if t == 0:
                        last.then_inc(h_half, 1)
                        dve.wait_ge(h_half, s + 1 + (s > 0))
                last.then_inc(h_ready, 1)
                turn(t_set, hdst)

            def post(s):
                dve.wait_ge(mpost_in, 32 * (s + 1))
                link(V.tensor_tensor(mt[:, 3, :], mt[:, 3, :], mt[:, 4, :], ALU.mult))
                rms(2 * s + 1)
                for t in range(TT):
                    link(V.scalar_tensor_tensor(out=mt[:, 4, :].rearrange("p (b c) -> p b c", b=HB), in0=PS[:, 2 * t:2 * t + 2, :], scalar=rstd[:, 2 * s + 1, t:t + 1],
                                                in1=mt[:, 3, :].rearrange("p (b c) -> p b c", b=HB), op0=ALU.mult, op1=ALU.mult))
                    last = V.tensor_tensor(x[:, t, :], x[:, t, :], mt[:, 4, :], ALU.add)
                    if t == 0:
                        last.then_inc(x_half, 1)
                        dve.wait_ge(x_half, s + 1)
                last.then_inc(x_ready, 1)

            rms(0)
            dve.wait_ge(const_ok, 2)
            V.tensor_scalar(cumx[0:64], upto[0:64], -1.0, None, ALU.add)
            V.tensor_copy(cumx[64:128], upto[64:128]).then_inc(triA_ok, 1)

            pre(0, 0)
            dve.wait_ge(tr_act, 2)
            dve.wait_ge(tr_dve, 2)
            link(V.tensor_tensor(xx, hT[:, :, 0:S], hT[:, :, 1:S + 1], ALU.subtract))
            dve.wait_ge(small_in, 16)
            for m, n in enumerate((3, 4, 5, 0, 1, 2)):
                if m >= 2:
                    if m <= 4:
                        dve.wait_ge(lora1_mm, m - 1)
                    else:
                        dve.wait_ge(proj_mm, 2)
                for k in range(KC):
                    last = V.scalar_tensor_tensor(out=xs[m % 2][:, k, :], in0=xx[:, k, :], scalar=mu[:, n, k:k + 1], in1=hT[:, k, 1:S + 1], op0=ALU.mult, op1=ALU.add)
                last.then_inc(xs_ready, 1)

            def heads(v):
                return v.rearrange("p t (h d) -> p (t h) d", d=HD)

            def both(row):
                return row.rearrange("p (o d) -> p o d", o=1).broadcast_to([P, TT, D])

            def per_head(col):
                return col.rearrange("p (n o) -> p n o", o=1).broadcast_to([P, TT * H, HD])

            dve.wait_ge(proj_ok, 4)
            dve.wait_ge(rows_in, 48)
            dve.wait_ge(lora2_ok, 3)
            dve.wait_ge(tr_mm, 4)
            link(V.tensor_tensor(h[:], k_, both(kkrow), ALU.mult))
            link(V.tensor_tensor(tmpX, h[:], h[:], ALU.mult))
            V.tensor_reduce(hs[:, 0, :], heads(tmpX), AX.X, ALU.add).then_inc(kss_ready, 1)
            link(V.scalar_tensor_tensor(out=tmpY, in0=a_, scalar=-1.0, in1=both(karow), op0=ALU.add, op1=ALU.mult))
            link(V.scalar_tensor_tensor(out=k_, in0=tmpY, scalar=1.0, in1=k_, op0=ALU.add, op1=ALU.mult))
            link(V.tensor_tensor(tmpX, r_, k_, ALU.mult))
            link(V.tensor_tensor(tmpX, tmpX, both(rkrow), ALU.mult))
            V.tensor_reduce(bonus[:], heads(tmpX), AX.X, ALU.add).then_inc(xy_free, 1)
            dve.wait_ge(knorm_ok, 1)
            link(V.tensor_scalar(hs[:, 1, :], hs[:, 1, :], 1e-12, None, ALU.max))
            link(V.reciprocal(hs[:, 1, :], hs[:, 1, :]))
            link(V.tensor_tensor(heads(h[:]), heads(h[:]), per_head(hs[:, 1, :]), ALU.mult))
            link(V.tensor_tensor(a_, a_, h[:], ALU.mult))
            dve.wait_ge(decay_ok, 2)
            V.tensor_tensor(a_, a_, tmpX, ALU.mult).then_inc(tok_ready, 1)
            V.tensor_tensor(k_, k_, tmpX, ALU.mult).then_inc(tok_ready, 1)
            dve.wait_ge(decay_ok, 3)
            V.tensor_tensor(r_, r_, tmpY, ALU.mult).then_inc(tok_ready, 1)
            dve.wait_ge(decay_ok, 4)
            V.scalar_tensor_tensor(out=h[:], in0=h[:], scalar=-1.0, in1=sig, op0=ALU.mult, op1=ALU.mult).then_inc(tok_ready, 1)
            turn(1, lambda t, b: bT[:, 4 * b:4 * b + 4, t * P:(t + 1) * P])
            turn(2, lambda t, b: kT[:, 4 * b:4 * b + 4, t * P:(t + 1) * P])
            turn(3, lambda t, b: ART[:, 4 * b:4 * b + 4, t, 1, :])
            turn(4, lambda t, b: ART[:, 4 * b:4 * b + 4, t, 0, :])
            for fc in range(FC):
                dve.wait_ge(sb_mm, fc + 1)
                b = 2 * (fc % 2)
                if fc == 0:
                    dve.wait_ge(tok_ready, 4)
                for q, dst in ((0, AAB), (1, ARB)):
                    for t in range(TT):
                        u = t * H + 2 * fc
                        last = V.tensor_tensor(dst[:, u:u + 2, :], PS[:, b:b + 2, t * 256 + q * P:t * 256 + (q + 1) * P],
                                               upto[:, q:q + 1, :].broadcast_to([P, 2, P]), ALU.mult)
                last.then_inc(sb_ok, 1)

            def mask_k(t, j):
                n = FC // 2 * t + j
                dve.wait_ge(sk_mm, n + 1)
                if n >= 2:
                    dve.wait_ge(xo_mm, n - 1)
                for f in range(2):
                    last = V.tensor_tensor(SK[j % 2][:, f], PS[:, 2:4, f * 256:(f + 1) * 256],
                                           upto[:].rearrange("p (o a) b -> p o (a b)", o=1).broadcast_to([P, 2, 2 * P]), ALU.mult)
                last.then_inc(sk_ok, 1)

            def head_norm(t, step):
                o_t, v_t, sq = o_[:, t:t + 1, :], v_[:, t:t + 1, :], (mt[:, 2:3, :], lnsq[:, 0:1, :])[t]
                mean, var, std = (hs[:, i, t * H:(t + 1) * H] for i in (0, 2, 3))
                col = lambda v: v.rearrange("p (n o) -> p n o", o=1).broadcast_to([P, H, HD])
                row = lambda i: mt[:, i:i + 1, :]
                if step == 0:
                    link(V.tensor_reduce(mean, heads(o_t), AX.X, ALU.add))
                    link(V.tensor_scalar(mean, mean, -1.0 / HD, None, ALU.mult))
                elif step == 1:
                    link(V.tensor_tensor(heads(o_t), heads(o_t), col(mean), ALU.add))
                elif step == 2:
                    link(V.tensor_tensor(sq, o_t, o_t, ALU.mult))
                elif step == 3:
                    link(V.tensor_reduce(var, heads(sq), AX.X, ALU.add))
                    link(V.tensor_scalar(var, var, 1.0 / HD, LNX_EPS, ALU.mult, ALU.add))
                elif step == 4:
                    V.reciprocal(var, var).then_inc(lvar_ready, 1)
                    if t == 0:
                        link(V.tensor_tensor(heads(v_t), heads(v_t), col(bonus[:, 0:H]), ALU.mult))
                elif step == 5:
                    link(V.tensor_tensor(heads(v_[:, 1:2, :]), heads(v_[:, 1:2, :]), col(bonus[:, H:2 * H]), ALU.mult))
                elif step == 6:
                    if t == 0:
                        dve.wait_ge(lnx_in, 32)
                        link(V.tensor_tensor(v_, v_, both(mt[:, 1, :]), ALU.add))
                elif step == 7:
                    dve.wait_ge(lstd_ok, t + 1)
                    link(V.tensor_tensor(heads(o_t), heads(o_t), col(std), ALU.mult))
                elif step == 8:
                    link(V.tensor_tensor(o_t, o_t, row(0), ALU.mult))
                    link(V.tensor_tensor(o_t, o_t, v_t, ALU.add))
                else:
                    V.tensor_tensor(hperm(t), o_[:, t, :].rearrange("p (q k) -> p q k", k=KC), g_[:, t, :].rearrange("p (q k) -> p q k", k=KC),
                                    ALU.mult).then_inc((h_half, h_ready)[t], 1)

            for t in range(TT):
                for j in range(FC // 2):
                    mask_k(t, j)
                if t == 0:
                    dve.wait_ge(diag_in, 64)
                    dve.wait_ge(ti_init, 1)
                    for s in range(31):
                        w = 31 - s
                        prod = at(22, 1 + s, w)
                        link(V.tensor_tensor(prod, TTi[:, 0:s + 1, s:s + 1].broadcast_to([P, s + 1, w]), DT[:, s:s + 1, s + 1:32].broadcast_to([P, s + 1, w]), ALU.mult))
                        last = V.tensor_tensor(TTi[:, 0:s + 1, s + 1:32], TTi[:, 0:s + 1, s + 1:32], prod, ALU.add)
                        if s < 30:
                            link(last)
                    last.then_inc(inv_ok, 1)
                for i in range(4):
                    n = 4 * t + i
                    rows = slice(32 * i, 32 * i + 32)
                    if i == 0:
                        dve.wait_ge(xo_mm, FC // 2 * (t + 1))
                    if n >= 1:
                        dve.wait_ge(xacc_mm, n)
                    V.tensor_copy(acc[rows, 1, :], PS[rows, 1, :]).then_inc(acc_dve, 1)
                    if t:
                        head_norm(0, 2 * i)
                    dve.wait_ge(ub_mm, n + 1)
                    V.tensor_copy(U[rows, 1, :], PS[rows, 3, :]).then_inc(u_dve, 1)
                    if t and i < 3:
                        head_norm(0, 2 * i + 1)
                if t == 0:
                    dve.wait_ge(st_mm, 1)
                    V.tensor_tensor(S0T, PS[:, 2, :].rearrange("p (f d) -> p f d", f=FC), edec[:].rearrange("p (f o) -> p f o", o=1).broadcast_to([P, FC, HD]), ALU.mult).then_inc(s0_ok, 1)

            for step in (7, 8, 9):
                head_norm(0, step)
            dve.wait_ge(o_ok, 2)
            for step in (0, 1):
                head_norm(1, step)
            turn_tile(5, 0, hdst)
            for step in (2, 3, 4, 6, 7, 8, 9):
                head_norm(1, step)
            turn_tile(5, 1, hdst)
            post(0)

            def moe(layer, s, t_set):
                pre(s, t_set)
                sc, biased, rest, mask, chosen, gates = (rt[:, i] for i in range(6))
                dve.wait_ge(sc_ok, layer + 1)
                dve.wait_ge(router_in, 32 * (layer + 1))
                link(V.tensor_tensor(biased, sc, rb.broadcast_to([P, TT, E]), ALU.add))
                for t in range(TT):
                    link(V.max(top8[:, t, :], biased[:, t, :]))
                    link(V.match_replace(rest[:, t, :], top8[:, t, :], biased[:, t, :], -1e30))
                V.tensor_tensor(mask, biased, rest, ALU.not_equal).then_inc(mask_ok, 1)
                dve.wait_ge(mask_ok, layer + 1)
                link(V.tensor_tensor(chosen, sc, mask, ALU.mult))
                link(V.tensor_reduce(rsum[:, 0, :], chosen, AX.X, ALU.add))
                link(V.reciprocal(rsum[:, 1, :], rsum[:, 0, :]))
                for t in range(TT):
                    last = V.tensor_scalar(gates[:, t, :], chosen[:, t, :], rsum[:, 1, t:t + 1], ROUTED_SCALE, ALU.mult, ALU.mult)
                link(last)
                Q = moe_sems[layer]
                for t in range(TT):
                    dve.wait_ge(silu_ok, UNITS * layer + t + 1)
                    V.tensor_tensor(actp[:, t].rearrange("p c q -> p q c"), PS[:, 4 + t, F:2 * F].rearrange("p (q c) -> p q c", c=FK),
                                    gsil[:, t, :].rearrange("p (q c) -> p q c", c=FK), ALU.mult).then_inc(hid_ok, 1)
                dve.wait_ge(hb_half, 2 * layer + 1)
                V.tensor_tensor(hrest, h[:], hpart[0], ALU.subtract).then_inc(hr_ok, 1)
                dve.wait_ge(pos_mm, layer + 1)
                link(V.scalar_tensor_tensor(out=posm, in0=PS[:, 4, 0:TT * E].rearrange("p (t e) -> p t e", t=TT), scalar=1.0, in1=mask, op0=ALU.add, op1=ALU.mult))
                for w in range(NW):
                    last = V.tensor_scalar(efl[:, 0, w:w + 1], PS[0:E, 5, 0:1], float(W * (w + 1)), None, ALU.is_gt)
                V.memset(efl[:, 1, 0:1], 0.0)
                link(last)
                link(V.tensor_copy(efl[:, 1, 1:2], efl[:, 0, 0:1]))
                V.tensor_tensor(efl[:, 1, 2:3], efl[:, 0, 0:1], efl[:, 0, 1:2], ALU.add).then_inc(flag_ok, 1)

                def picks(i, par, where):
                    if not (isinstance(i, int) and i < 2):
                        dve.wait_ge(Q["wpickT_mm"], i - 1)
                    for m in range(2):
                        e, c0 = where(m)
                        for t in range(TT):
                            pos, gate = posm[:, t, bass.ds(e, 1)], gates[:, t, bass.ds(e, 1)]
                            V.tensor_scalar(pick[par][:, t, W * m:W * m + W], place[:, bass.ds(c0, W)], pos, None, ALU.is_equal)
                            last = V.tensor_scalar(wpick[par][:, t, W * m:W * m + W], place[:, bass.ds(c0, W)], pos, gate, ALU.is_equal, ALU.mult)
                    last.then_inc(Q["pick_ok"], 1)

                picks(0, 0, lambda m: (m, 0))
                dve.wait_ge(idx_mm, layer + 1)
                link(V.tensor_scalar(efl[:, 2, :], PS[0:E, 6, 0:NW], 1.0, None, ALU.add))
                for w in range(NW):
                    last = V.tensor_scalar(hit[:, w, :], place[0:E, 0:LIST], efl[:, 2, w:w + 1], efl[:, 0, w:w + 1], ALU.is_equal, ALU.mult)
                last.then_inc(hit_ok, 1)
                dve.wait_ge(hb_half, 2 * layer + 2)
                V.tensor_tensor(hpart[2], hrest, hpart[1], ALU.subtract).then_inc(hb_ok, 1)
                picks(1, 1, lambda m: (2 + m, 0))
                dve.wait_ge(list_mm, layer + 1)
                V.tensor_scalar(lists[0:1, 0, 0:4], place[0:1, 0:4], float(E - 5), None, ALU.add)
                V.tensor_scalar(lists[0:1, 1, 0:4], place[0:1, 0:4], 0.0, None, ALU.mult)
                V.tensor_copy(lists[0:1, 0, 4:], PS[0:1, 7, 0:LIST])
                V.tensor_scalar(lists[0:1, 1, 4:], PS[0:1, 7, LIST:2 * LIST], float(W * (MAXWIN - 1)), None, ALU.add)
                link(V.tensor_reduce(lrow[:, 0:1], PS[0:1, 7, 2 * LIST:2 * LIST + NW], AX.X, ALU.add))
                link(V.tensor_scalar(lrow[:, 0:1], lrow[:, 0:1], 2.0, None, ALU.add))
                link(V.tensor_scalar(lrow[:, 8:16], place[0:1, 0:8], 4.0, lrow[:, 0:1], ALU.mult, ALU.is_lt))
                link(V.tensor_reduce(lrow[:, 1:2], lrow[:, 8:16], AX.X, ALU.add))
                V.tensor_scalar(rounds[:, 1:2], lrow[:, 1:2], 4.0, float(4 * R0 - 2), ALU.mult, ALU.add)
                V.tensor_scalar(rounds[:, 0:1], lrow[:, 1:2], float(R0), None, ALU.add).then_inc(list_ok, 1)
                dve.wait_ge(list_ok, layer + 1)
                end = dve.value_load(rounds[0:1, 0:1], min_val=R0, max_val=R0 + LIST // 4 - 4)

                def take_picked(i, par):
                    dve.wait_ge(Q["gather_mm"], i * 2 + 2)
                    V.tensor_copy(xg[par][:, 4:8, :], PS[:, 5, :].rearrange("p (k s) -> p k s", k=4)).then_inc(Q["xg_dve"], 1)

                def pair(i, par, where, final=False):
                    dve.wait_ge(Q["sg_ok"], i + 1)
                    if not (isinstance(i, int) and i == 0):
                        dve.wait_ge(Q["hidpT_mm"], i)
                    V.tensor_tensor(hidp.rearrange("p c q -> p q c"), PS[:, 6, F:2 * F].rearrange("p (q c) -> p q c", c=FK),
                                    sg.rearrange("p (q c) -> p q c", c=FK), ALU.mult).then_inc(Q["hidp_ok"], 1)
                    if not final:
                        take_picked(i + 1, 1 - par)
                    dve.wait_ge(Q["y_mm"], i * 2 + 2)
                    V.tensor_copy(ye[:, NB:D], PS[:, 6, :]).then_inc(Q["ye_dve"], 1)
                    if not final:
                        picks(i + 2, par, where)

                take_picked(0, 0)
                pair(0, 0, lambda m: (4 + m, 0))
                pair(1, 1, lambda m: (6 + m, 0))
                with dve.Fori(1, R0 - 1) as j:
                    for q in range(2):
                        pair(dve.snap(j * 2 + q), q, lambda m: (dve.snap(j * 4 + (4 + 2 * q + m)), 0))
                with dve.Fori(R0 - 1, end) as j:
                    for q in range(2):
                        def listed(m):
                            n = dve.snap(j * 4 + (8 + 2 * q + m - E))
                            return (dve.value_load(lists[0:1, 0, bass.ds(n, 1)], min_val=0, max_val=E - 1),
                                    dve.value_load(lists[0:1, 1, bass.ds(n, 1)], min_val=0, max_val=W * (MAXWIN - 1)))
                        pair(dve.snap(j * 2 + q), q, listed)
                pair(dve.snap(end * 2), 0, None, final=True)
                post(s)

            moe(0, 1, 6)

            pre(2, 7)
            V.memset(zmask[:, P:2 * P], 0.0)
            V.tensor_scalar(zmask[:, 0:P], upto[:, 0, :], -1.0, 1e30, ALU.add, ALU.mult)
            link(V.tensor_scalar(zmask[:, 2 * P:384], upto[:, 0, :], -1.0, 1e30, ALU.add, ALU.mult))
            for n in (8, 9):
                turn(n, (lambda o: lambda t, b: qkT[:, o + 4 * b:o + 4 * b + 4, t * P:(t + 1) * P])((n - 8) * FC))

            def take_z(g):
                dve.wait_ge(z_mm, g + 1)
                if g == 3:
                    dve.wait_ge(w_ok, 1)
                V.tensor_tensor(zsb[g % 3], PS[:, 0:4, 0:384], zmask.rearrange("p (o c) -> p o c", o=1).broadcast_to([P, 4, 384]), ALU.add).then_inc(z_ok, 1)

            def softplus(g):
                dve.wait_ge(l_ok, g + 1)
                V.scalar_tensor_tensor(out=spb[g % 3], in0=zsb[g % 3], scalar=0.0, in1=spb[g % 3], op0=ALU.max, op1=ALU.add).then_inc(sp_ok, 1)

            def log_weights(g):
                dve.wait_ge(rc_mm, g + 1)
                V.tensor_tensor(zsb[g % 3], zsb[g % 3], PS[:, 4:8, 0:384], ALU.subtract).then_inc(ez_ok, 1)

            def take_o(g):
                dve.wait_ge(pv_mm, g + 1)
                for t in range(TT):
                    dst = h[:, t, :].rearrange("p (k j q) -> p j q k", k=KC, j=H)[:, 4 * g:4 * g + 4]
                    last = V.tensor_copy(dst, PS[:, 0:4, 384 + t * HD:384 + (t + 1) * HD].rearrange("p j (q k) -> p j q k", k=KC))
                last.then_inc(o_taken if g < 3 else h_ready, 1)

            for g in range(2):
                take_z(g)
                softplus(g)
            take_z(2)
            log_weights(0)
            log_weights(1)
            softplus(2)
            take_o(0)
            take_z(3)
            log_weights(2)
            softplus(3)
            take_o(1)
            log_weights(3)
            take_o(2)
            take_o(3)
            turn(10, hdst)
            post(2)
            moe(1, 3, 11)


_IN = ['x', 'c', 'ada_w', 'ada_b', 'norm_pre_mix', 'norm_post_mix', 'norm_pre_ffn', 'norm_post_ffn', 'rwkv_mu', 'rwkv_w_rkv',
       'rwkv_w_w1', 'rwkv_w_w2', 'rwkv_w0', 'rwkv_w_a1', 'rwkv_w_a2', 'rwkv_a0', 'rwkv_w_g1', 'rwkv_w_g2', 'rwkv_k_k',
       'rwkv_k_a', 'rwkv_r_k', 'rwkv_lnx_g', 'rwkv_lnx_b', 'rwkv_w_o', 'sb_w_qkv', 'sb_w_o', 'moe_w_router',
       'moe_router_bias', 'moe_w_gate', 'moe_w_up', 'moe_w_down', 'moe_ws_gate', 'moe_ws_up', 'moe_ws_down']


def kernel(**inputs):
    import numpy as np
    import concourse.bacc as bacc
    from concourse.bass_utils import run_bass_kernel_spmd

    nc = bacc.Bacc("TRN2", target_bir_lowering=False, num_devices=1)
    arrays, aps = {}, {}
    for name in _IN:
        v = np.ascontiguousarray(inputs[name])
        arrays[f"in_{name}"] = v
        aps[name] = nc.dram_tensor(f"in_{name}", v.shape, mybir.dt.from_np(v.dtype), kind="ExternalInput").ap()
    out = nc.dram_tensor("out", inputs["x"].shape, F32, kind="ExternalOutput").ap()
    hybrid_trunk(nc, aps, out)
    r = run_bass_kernel_spmd(nc, [arrays], core_ids=[0])
    return r.results[0]["out"]
```
